# Optimizing a Trainium2 kernel written in Bass

```python
import jax, jax.numpy as jnp
from jax import lax
import numpy as np
import math
import jax
import jax.numpy as jnp

D_MODEL = 1024
BATCH = 1
SEQ = 256
DEPTH = 2

A_HEADS = 4
A_DK = 128
A_DV = 128
CONV_K = 4
B_HEADS = 4
B_DK = 128
B_DV = 128
CHUNK = 64
C_HEADS = 16
C_KV_HEADS = 4
C_GROUP = C_HEADS // C_KV_HEADS
C_HD = 64
WINDOW = 128
ROPE_THETA = 10000.0
D_FF = 4 * D_MODEL
PLE_DIM = 256
EPS = 1e-6
N_EVEN = (DEPTH + 1) // 2
N_ODD = DEPTH // 2

A_QK = A_HEADS * A_DK
A_V = A_HEADS * A_DV
B_QK = B_HEADS * B_DK
B_V = B_HEADS * B_DV
A_CONV_CH = 2 * A_QK + A_V
A_COLS = 2 * A_QK + A_V + 2 * A_HEADS + A_V
B_COLS = 2 * B_QK + B_V + 2 * B_HEADS + B_V
IN_COLS = A_COLS + B_COLS
MIX_AB = A_V + B_V
C_Q = C_HEADS * C_HD
C_KV = C_KV_HEADS * C_HD
C_COLS = C_Q + 2 * C_KV


F32 = jnp.float32

def rmsnorm(x, g):
    xf = x.astype(F32)
    y = xf * lax.rsqrt(jnp.mean(xf * xf, -1, keepdims=True) + EPS)
    return (y * g.astype(F32)).astype(x.dtype)

def l2norm(x):
    return x * lax.rsqrt(jnp.sum(x * x, -1, keepdims=True) + EPS)

def causal_conv(x, w):
    k_taps = w.shape[0]
    s = x.shape[1]
    xp = jnp.pad(x, ((0, 0), (k_taps - 1, 0), (0, 0)))
    return sum(xp[:, k:k + s] * w[k] for k in range(k_taps))

def to_chunks(x):
    b, s, h = x.shape[:3]
    x = x.reshape((b, s // CHUNK, CHUNK, h) + x.shape[3:])
    return jnp.moveaxis(x, (1, 3), (0, 2))

def from_chunks(x):
    x = jnp.moveaxis(x, (0, 2), (1, 3))
    b, n, c, h, d = x.shape
    return x.reshape(b, n * c, h, d)

def gated_delta_rule(q, k, v, g, beta):
    b, s, h, dk = q.shape
    dv = v.shape[-1]
    qc, kc, vc = to_chunks(q), to_chunks(k), to_chunks(v)
    gcum = jnp.cumsum(to_chunks(g), -1)
    bc = to_chunks(beta)
    causal = jnp.tril(jnp.ones((CHUNK, CHUNK), bool))
    strict = jnp.tril(jnp.ones((CHUNK, CHUNK), bool), -1)
    diff = gcum[..., :, None] - gcum[..., None, :]
    decay = jnp.where(causal, jnp.exp(jnp.where(causal, diff, 0.0)), 0.0)
    kb = kc * bc[..., None]
    vb = vc * bc[..., None]
    lmat = jnp.where(strict, jnp.einsum('nbhcd,nbhed->nbhce', kb, kc) * decay, 0.0)
    eye = jnp.eye(CHUNK, dtype=lmat.dtype)
    rhs = jnp.concatenate([vb, kb * jnp.exp(gcum)[..., None]], -1)
    uw = lax.linalg.triangular_solve(lmat + eye, rhs, left_side=True, lower=True,
                                     unit_diagonal=True)
    u, w = uw[..., :dv], uw[..., dv:]
    attn_intra = jnp.einsum('nbhcd,nbhed->nbhce', qc, kc) * decay
    q_dec = qc * jnp.exp(gcum)[..., None]
    g_last = gcum[..., -1]
    k_dec = kc * jnp.exp(g_last[..., None] - gcum)[..., None]

    def step(state, xs):
        u_, w_, a_, qd, kd, gl = xs
        v_new = u_ - jnp.einsum('bhcd,bhde->bhce', w_, state)
        o = (jnp.einsum('bhcd,bhde->bhce', qd, state)
             + jnp.einsum('bhcs,bhse->bhce', a_, v_new))
        state = (state * jnp.exp(gl)[..., None, None]
                 + jnp.einsum('bhcd,bhce->bhde', kd, v_new))
        return state, o

    s0 = jnp.zeros((b, h, dk, dv), F32)
    _, o = lax.scan(step, s0, (u, w, attn_intra, q_dec, k_dec, g_last))
    return from_chunks(o)

def mlstm_chunkwise(q, k, v, i_log, f_log):
    b, s, h, dk = q.shape
    dv = v.shape[-1]
    qc, kc, vc = to_chunks(q), to_chunks(k), to_chunks(v)
    ic = to_chunks(i_log)
    bcum = jnp.cumsum(to_chunks(f_log), -1)
    causal = jnp.tril(jnp.ones((CHUNK, CHUNK), bool))
    dmat = bcum[..., :, None] - bcum[..., None, :] + ic[..., None, :]
    dmat = jnp.where(causal, dmat, -jnp.inf)
    m_intra = jnp.max(dmat, -1)
    b_last = bcum[..., -1]
    w_state = b_last[..., None] - bcum + ic
    qk = jnp.einsum('nbhtd,nbhsd->nbhts', qc, kc)

    def step(carry, xs):
        c_st, n_st, m = carry
        q_, k_, v_, qk_, d_, mi, bc_, ws, bl = xs
        a = bc_ + m[..., None]
        mt = jnp.maximum(a, mi)
        inter = jnp.exp(a - mt)
        pmat = qk_ * jnp.exp(d_ - mt[..., None])
        num = (inter[..., None] * jnp.einsum('bhcd,bhde->bhce', q_, c_st)
               + jnp.einsum('bhts,bhse->bhte', pmat, v_))
        den = inter * jnp.einsum('bhcd,bhd->bhc', q_, n_st) + jnp.sum(pmat, -1)
        hout = num / jnp.maximum(jnp.abs(den), jnp.exp(-mt))[..., None]
        m_new = jnp.maximum(bl + m, jnp.max(ws, -1))
        sc = jnp.exp(bl + m - m_new)
        kw = k_ * jnp.exp(ws - m_new[..., None])[..., None]
        c_st = sc[..., None, None] * c_st + jnp.einsum('bhcd,bhce->bhde', kw, v_)
        n_st = sc[..., None] * n_st + jnp.sum(kw, -2)
        return (c_st, n_st, m_new), hout

    carry0 = (jnp.zeros((b, h, dk, dv), F32), jnp.zeros((b, h, dk), F32), jnp.zeros((b, h), F32))
    _, o = lax.scan(step, carry0, (qc, kc, vc, qk, dmat, m_intra, bcum, w_state, b_last))
    return from_chunks(o)

def mixer_ab(hn, w_in, conv_w, a_log, dt_bias, norm_a, i_bias, f_bias, norm_b, w_out):
    b, s, _ = hn.shape
    proj = hn @ w_in
    pa, pb = proj[..., :A_COLS], proj[..., A_COLS:]
    qkv = jax.nn.silu(causal_conv(pa[..., :A_CONV_CH], conv_w)).astype(F32)
    qa = l2norm(qkv[..., :A_QK].reshape(b, s, A_HEADS, A_DK)) * (A_DK ** -0.5)
    ka = l2norm(qkv[..., A_QK:2 * A_QK].reshape(b, s, A_HEADS, A_DK))
    va = qkv[..., 2 * A_QK:].reshape(b, s, A_HEADS, A_DV)
    off = A_CONV_CH
    beta = jax.nn.sigmoid(pa[..., off:off + A_HEADS].astype(F32))
    alpha_pre = pa[..., off + A_HEADS:off + 2 * A_HEADS].astype(F32) + dt_bias.astype(F32)
    g = -jnp.exp(a_log.astype(F32)) * jax.nn.softplus(alpha_pre)
    z = pa[..., off + 2 * A_HEADS:].astype(F32).reshape(b, s, A_HEADS, A_DV)
    oa = gated_delta_rule(qa, ka, va, g, beta)
    oa = rmsnorm(oa, norm_a) * jax.nn.silu(z)
    pbf = pb.astype(F32)
    qb = pbf[..., :B_QK].reshape(b, s, B_HEADS, B_DK) * (B_DK ** -0.5)
    kb = pbf[..., B_QK:2 * B_QK].reshape(b, s, B_HEADS, B_DK)
    vb = pbf[..., 2 * B_QK:2 * B_QK + B_V].reshape(b, s, B_HEADS, B_DV)
    off = 2 * B_QK + B_V
    i_log = pbf[..., off:off + B_HEADS] + i_bias.astype(F32)
    f_log = jax.nn.log_sigmoid(pbf[..., off + B_HEADS:off + 2 * B_HEADS] + f_bias.astype(F32))
    o_gate = jax.nn.sigmoid(pbf[..., off + 2 * B_HEADS:]).reshape(b, s, B_HEADS, B_DV)
    ob = mlstm_chunkwise(qb, kb, vb, i_log, f_log)
    ob = rmsnorm(ob, norm_b) * o_gate
    mixed = jnp.concatenate([oa.reshape(b, s, A_V), ob.reshape(b, s, B_V)], -1)
    return mixed.astype(hn.dtype) @ w_out

def rope(x, pos):
    half = x.shape[-1] // 2
    inv = ROPE_THETA ** (-jnp.arange(half, dtype=F32) / half)
    ang = pos.astype(F32)[..., None] * inv
    cos = jnp.cos(ang)[:, :, None, :]
    sin = jnp.sin(ang)[:, :, None, :]
    x1, x2 = x[..., :half], x[..., half:]
    return jnp.concatenate([x1 * cos - x2 * sin, x2 * cos + x1 * sin], -1)

def mixer_c(hn, pos, w_qkv, b_qkv, sinks, w_o, b_o):
    b, s, _ = hn.shape
    nb = s // WINDOW
    proj = (hn @ w_qkv + b_qkv).astype(F32)
    q = rope(proj[..., :C_Q].reshape(b, s, C_HEADS, C_HD), pos)
    q = q.reshape(b, nb, WINDOW, C_KV_HEADS, C_GROUP, C_HD)
    q = jnp.moveaxis(q, 1, 0)
    k = rope(proj[..., C_Q:C_Q + C_KV].reshape(b, s, C_KV_HEADS, C_HD), pos)
    v = proj[..., C_Q + C_KV:].reshape(b, s, C_KV_HEADS, C_HD)
    kp = jnp.pad(k, ((0, 0), (WINDOW, 0), (0, 0), (0, 0)))
    vp = jnp.pad(v, ((0, 0), (WINDOW, 0), (0, 0), (0, 0)))
    t_idx = jnp.arange(WINDOW)[:, None]
    s_idx = jnp.arange(2 * WINDOW)[None, :]
    band = (s_idx > t_idx) & (s_idx <= t_idx + WINDOW)
    sink = sinks.astype(F32).reshape(C_KV_HEADS, C_GROUP)[None, :, :, None]
    scale = C_HD ** -0.5

    def block(args):
        j, qj = args
        kj = lax.dynamic_slice_in_dim(kp, j * WINDOW, 2 * WINDOW, axis=1)
        vj = lax.dynamic_slice_in_dim(vp, j * WINDOW, 2 * WINDOW, axis=1)
        valid = band & (j * WINDOW - WINDOW + s_idx >= 0)
        sc = jnp.einsum('btkgd,bskd->bkgts', qj, kj) * scale
        sc = jnp.where(valid, sc, -jnp.inf)
        m = jnp.maximum(jnp.max(sc, -1), sink)
        pr = jnp.exp(sc - m[..., None])
        den = jnp.sum(pr, -1) + jnp.exp(sink - m)
        pr = pr / den[..., None]
        return jnp.einsum('bkgts,bskd->btkgd', pr, vj)

    o = lax.map(block, (jnp.arange(nb), q))
    o = jnp.moveaxis(o, 0, 1).reshape(b, s, C_Q)
    return o.astype(hn.dtype) @ w_o + b_o

def first_inputs(seed: int = 0) -> dict:
    key = jax.random.key(seed)
    ks = jax.random.split(key, 24)
    nrm = jax.random.normal
    x = nrm(ks[0], (BATCH, SEQ, D_MODEL), F32)
    p = nrm(ks[1], (DEPTH, BATCH, SEQ, PLE_DIM), F32)
    positions = jnp.broadcast_to(jnp.arange(SEQ, dtype=jnp.int32), (BATCH, SEQ))
    norm_gains = 1.0 + 0.05 * nrm(ks[2], (DEPTH, 4, D_MODEL), F32)
    w_in_ab = nrm(ks[3], (N_EVEN, D_MODEL, IN_COLS), F32) * D_MODEL ** -0.5
    conv_a = nrm(ks[4], (N_EVEN, CONV_K, A_CONV_CH), F32) * CONV_K ** -0.5
    a_log = jnp.log(jax.random.uniform(ks[5], (N_EVEN, A_HEADS), F32, 1.0, 16.0))
    dt = jnp.exp(jax.random.uniform(ks[6], (N_EVEN, A_HEADS), F32, np.log(1e-3), np.log(1e-1)))
    dt_bias = dt + jnp.log(-jnp.expm1(-dt))
    norm_a = 1.0 + 0.05 * nrm(ks[7], (N_EVEN, A_DV), F32)
    i_bias_b = 0.1 * nrm(ks[8], (N_EVEN, B_HEADS), F32)
    f_bias_b = 3.0 + 0.5 * nrm(ks[9], (N_EVEN, B_HEADS), F32)
    norm_b = 1.0 + 0.05 * nrm(ks[10], (N_EVEN, B_HEADS, B_DV), F32)
    w_out_ab = nrm(ks[11], (N_EVEN, MIX_AB, D_MODEL), F32) * MIX_AB ** -0.5
    w_qkv_c = nrm(ks[12], (N_ODD, D_MODEL, C_COLS), F32) * D_MODEL ** -0.5
    b_qkv_c = 0.02 * nrm(ks[13], (N_ODD, C_COLS), F32)
    sinks_c = nrm(ks[14], (N_ODD, C_HEADS), F32)
    w_o_c = nrm(ks[15], (N_ODD, C_Q, D_MODEL), F32) * C_Q ** -0.5
    b_o_c = 0.02 * nrm(ks[16], (N_ODD, D_MODEL), F32)
    w_up = nrm(ks[17], (DEPTH, D_MODEL, D_FF), F32) * D_MODEL ** -0.5
    w_down = nrm(ks[18], (DEPTH, D_FF, D_MODEL), F32) * D_FF ** -0.5
    w_ple = nrm(ks[19], (DEPTH, PLE_DIM, D_MODEL), F32) * PLE_DIM ** -0.5
    w_ple_gate = nrm(ks[20], (DEPTH, D_MODEL, D_MODEL), F32) * D_MODEL ** -0.5
    return {"x": x, "p": p, "positions": positions, "norm_gains": norm_gains,
            "w_in_ab": w_in_ab, "conv_a": conv_a, "a_log": a_log, "dt_bias": dt_bias,
            "norm_a": norm_a, "i_bias_b": i_bias_b, "f_bias_b": f_bias_b, "norm_b": norm_b,
            "w_out_ab": w_out_ab, "w_qkv_c": w_qkv_c, "b_qkv_c": b_qkv_c, "sinks_c": sinks_c,
            "w_o_c": w_o_c, "b_o_c": b_o_c, "w_up": w_up, "w_down": w_down,
            "w_ple": w_ple, "w_ple_gate": w_ple_gate}

def first_block(x, p, positions, norm_gains, w_in_ab, conv_a, a_log, dt_bias, norm_a,
              i_bias_b, f_bias_b, norm_b, w_out_ab, w_qkv_c, b_qkv_c, sinks_c, w_o_c, b_o_c,
              w_up, w_down, w_ple, w_ple_gate):
    h = x
    for layer in range(DEPTH):
        gains = norm_gains[layer]
        hn = rmsnorm(h, gains[0])
        if layer % 2 == 0:
            e = layer // 2
            mix = mixer_ab(hn, w_in_ab[e], conv_a[e], a_log[e], dt_bias[e], norm_a[e],
                           i_bias_b[e], f_bias_b[e], norm_b[e], w_out_ab[e])
        else:
            o = layer // 2
            mix = mixer_c(hn, positions, w_qkv_c[o], b_qkv_c[o], sinks_c[o], w_o_c[o], b_o_c[o])
        h = h + rmsnorm(mix, gains[1])
        hn = rmsnorm(h, gains[2])
        ff = jnp.square(jax.nn.relu(hn @ w_up[layer])) @ w_down[layer]
        h = h + rmsnorm(ff, gains[3])
        gate = jax.nn.sigmoid(h @ w_ple_gate[layer])
        h = h + gate * (p[layer] @ w_ple[layer])
    return h


MEM_LEN = 256
N_HEADS_GROUP = 4
HEAD_DIM = 64
GROUP_WIDTH = N_HEADS_GROUP * HEAD_DIM
N_GROUPS = 5
MIX_WIDTH = N_GROUPS * GROUP_WIDTH
MLA_Q_RANK = 192
MLA_KV_RANK = 128
MLA_NOPE_DIM = 64
MLA_ROPE_DIM = 32
MLA_QK_DIM = MLA_NOPE_DIM + MLA_ROPE_DIM
DIFF_QK_DIM = HEAD_DIM // 2
ROPE_THETA_2 = 500000.0
ROT_MOBA = HEAD_DIM // 4
ROT_DIFF = DIFF_QK_DIM // 4
POS_OFFSET_MAX = 8192
MOBA_BLOCK = 256
MOBA_TOPK = 3
MOBA_Q_CHUNK = 64
Q_BLOCK = 128
D_FF_2 = ((8 * D_MODEL // 3 + 127) // 128) * 128
CONV_WIDTH = 3
NEG_INF = -1e30
IN_SIZES = (MLA_Q_RANK, MLA_KV_RANK, MLA_ROPE_DIM,
            3 * GROUP_WIDTH, N_HEADS_GROUP,
            3 * GROUP_WIDTH,
            3 * GROUP_WIDTH,
            GROUP_WIDTH)
D_IN = sum(IN_SIZES)


def _rms_norm(x, g):
    xf = x.astype(jnp.float32)
    y = xf * lax.rsqrt(jnp.mean(xf * xf, axis=-1, keepdims=True) + EPS)
    return (y * g.astype(jnp.float32)).astype(x.dtype)

def _heads(t, n):
    b, s, w = t.shape
    return t.reshape(b, s, n, w // n).transpose(0, 2, 1, 3)

def _merge(t):
    b, h, s, d = t.shape
    return t.transpose(0, 2, 1, 3).reshape(b, s, h * d)

def _split_pairs(t):
    b, s, _ = t.shape
    return t.reshape(b, s, N_HEADS_GROUP, 2, DIFF_QK_DIM).transpose(3, 0, 2, 1, 4)

def _rope_tables(positions, rot):
    inv = ROPE_THETA_2 ** (-jnp.arange(0, rot, 2, dtype=jnp.float32) / rot)
    ang = positions.astype(jnp.float32)[:, None, :, None] * inv
    return jnp.cos(ang), jnp.sin(ang)

def _rope(x, cos, sin):
    rot = 2 * cos.shape[-1]
    xr = x[..., :rot].astype(jnp.float32)
    x1, x2 = xr[..., :rot // 2], xr[..., rot // 2:]
    r = jnp.concatenate([x1 * cos - x2 * sin, x1 * sin + x2 * cos], axis=-1).astype(x.dtype)
    return jnp.concatenate([r, x[..., rot:]], axis=-1)

def _causal_mask(start, n_q, n_k):
    return jnp.arange(n_k)[None, :] <= (start + jnp.arange(n_q))[:, None]

def _sweep(block_fn, seq, block):
    out = lax.map(block_fn, jnp.arange(seq // block))
    nb, b, h, q, d = out.shape
    return out.transpose(1, 2, 0, 3, 4).reshape(b, h, nb * q, d)

def _dense_causal_attention(q, k, v, scale, log_decay=None):
    seq = q.shape[2]

    def block(i):
        start = i * Q_BLOCK
        qb = lax.dynamic_slice_in_dim(q, start, Q_BLOCK, axis=2)
        s = jnp.einsum('bhqd,bhkd->bhqk', qb, k).astype(jnp.float32) * scale
        if log_decay is not None:
            cq = lax.dynamic_slice_in_dim(log_decay, start, Q_BLOCK, axis=2)
            s = s + (cq[..., :, None] - log_decay[..., None, :])
        s = jnp.where(_causal_mask(start, Q_BLOCK, seq), s, NEG_INF)
        p = jax.nn.softmax(s, axis=-1).astype(v.dtype)
        return jnp.einsum('bhqk,bhkd->bhqd', p, v)

    return _sweep(block, seq, Q_BLOCK)

def _diff_causal_attention(q1, q2, k1, k2, v, lam, scale):
    seq = q1.shape[2]

    def block(i):
        start = i * Q_BLOCK
        mask = _causal_mask(start, Q_BLOCK, seq)

        def probs(q, k):
            qb = lax.dynamic_slice_in_dim(q, start, Q_BLOCK, axis=2)
            s = jnp.einsum('bhqd,bhkd->bhqk', qb, k).astype(jnp.float32) * scale
            return jax.nn.softmax(jnp.where(mask, s, NEG_INF), axis=-1)

        p = (probs(q1, k1) - lam * probs(q2, k2)).astype(v.dtype)
        return jnp.einsum('bhqk,bhkd->bhqd', p, v)

    return _sweep(block, seq, Q_BLOCK)

def _moba_attention(q, k, v, scale):
    b, h, seq, d = q.shape
    nb = -(-seq // MOBA_BLOCK)
    pad = nb * MOBA_BLOCK - seq
    kp = jnp.pad(k, ((0, 0), (0, 0), (0, pad), (0, 0)))
    vp = jnp.pad(v, ((0, 0), (0, 0), (0, pad), (0, 0)))
    kb = kp.reshape(b, h, nb, MOBA_BLOCK, d)
    vb = vp.reshape(b, h, nb, MOBA_BLOCK, d)
    k_mean = jnp.mean(kb, axis=3)
    gate = jnp.einsum('bhsd,bhnd->bhsn', q, k_mean).astype(jnp.float32)
    q_blk = jnp.arange(seq) // MOBA_BLOCK
    past = jnp.arange(nb)[None, :] < q_blk[:, None]
    gate = jnp.where(past, gate, NEG_INF)
    topk = min(MOBA_TOPK, nb)
    _, sel = lax.top_k(gate, topk)
    sel_ok = sel < q_blk[:, None]
    bi = jnp.arange(b)[:, None, None, None]
    hi = jnp.arange(h)[None, :, None, None]
    n_sel = topk * MOBA_BLOCK

    def chunk(i):
        start = i * MOBA_Q_CHUNK
        qc = lax.dynamic_slice_in_dim(q, start, MOBA_Q_CHUNK, axis=2)
        idx = lax.dynamic_slice_in_dim(sel, start, MOBA_Q_CHUNK, axis=2)
        ok = lax.dynamic_slice_in_dim(sel_ok, start, MOBA_Q_CHUNK, axis=2)
        kg = kb[bi, hi, idx]
        vg = vb[bi, hi, idx]
        s_past = jnp.einsum('bhqd,bhqnkd->bhqnk', qc, kg).astype(jnp.float32) * scale
        s_past = jnp.where(ok[..., None], s_past, NEG_INF).reshape(b, h, MOBA_Q_CHUNK, n_sel)
        own = (start // MOBA_BLOCK) * MOBA_BLOCK
        k_own = lax.dynamic_slice_in_dim(kp, own, MOBA_BLOCK, axis=2)
        v_own = lax.dynamic_slice_in_dim(vp, own, MOBA_BLOCK, axis=2)
        s_own = jnp.einsum('bhqd,bhkd->bhqk', qc, k_own).astype(jnp.float32) * scale
        causal = (own + jnp.arange(MOBA_BLOCK))[None, :] <= (start + jnp.arange(MOBA_Q_CHUNK))[:, None]
        s_own = jnp.where(causal, s_own, NEG_INF)
        p = jax.nn.softmax(jnp.concatenate([s_past, s_own], axis=-1), axis=-1).astype(v.dtype)
        p_past = p[..., :n_sel].reshape(b, h, MOBA_Q_CHUNK, topk, MOBA_BLOCK)
        return (jnp.einsum('bhqnk,bhqnkd->bhqd', p_past, vg)
                + jnp.einsum('bhqk,bhkd->bhqd', p[..., n_sel:], v_own))

    return _sweep(chunk, seq, MOBA_Q_CHUNK)

def _memory_attention(q, k, v, scale):
    s = jnp.einsum('bhqd,bhmd->bhqm', q, k).astype(jnp.float32) * scale
    p = jax.nn.softmax(s, axis=-1).astype(v.dtype)
    return jnp.einsum('bhqm,bhmd->bhqd', p, v)

def _causal_dwconv(h, w, bias):
    seq = h.shape[1]
    hp = jnp.pad(h, ((0, 0), (CONV_WIDTH - 1, 0), (0, 0)))
    y = bias
    for j in range(CONV_WIDTH):
        y = y + w[j] * hp[:, j:j + seq]
    return y

def second_inputs(seed: int = 0) -> dict:
    key = jax.random.key(seed)
    ks = iter(jax.random.split(key, 40))
    L = DEPTH

    def nrm(shape, scale):
        return scale * jax.random.normal(next(ks), shape, jnp.float32)

    def gain(shape):
        return 1.0 + 0.05 * jax.random.normal(next(ks), shape, jnp.float32)

    x = nrm((BATCH, SEQ, D_MODEL), 1.0)
    mem = nrm((BATCH, MEM_LEN, D_MODEL), 1.0)
    offset = jax.random.randint(next(ks), (BATCH, 1), 0, POS_OFFSET_MAX, dtype=jnp.int32)
    positions = offset + jnp.arange(SEQ, dtype=jnp.int32)[None, :]
    return {
        "x": x,
        "mem": mem,
        "positions": positions,
        "attn_norm": gain((L, D_MODEL)),
        "ffn_norm": gain((L, D_MODEL)),
        "mem_norm": gain((L, D_MODEL)),
        "w_in": nrm((L, D_MODEL, D_IN), D_MODEL ** -0.5),
        "mla_cq_norm": gain((L, MLA_Q_RANK)),
        "mla_ckv_norm": gain((L, MLA_KV_RANK)),
        "mla_w_uq": nrm((L, MLA_Q_RANK, N_HEADS_GROUP * MLA_QK_DIM), MLA_Q_RANK ** -0.5),
        "mla_w_ukv": nrm((L, MLA_KV_RANK, N_HEADS_GROUP * (MLA_NOPE_DIM + HEAD_DIM)), MLA_KV_RANK ** -0.5),
        "mla_q_norm": gain((L, MLA_QK_DIM)),
        "mla_k_norm": gain((L, MLA_QK_DIM)),
        "fox_b_f": 3.0 + 0.5 * jax.random.normal(next(ks), (L, N_HEADS_GROUP), jnp.float32),
        "fox_q_norm": gain((L, HEAD_DIM)),
        "fox_k_norm": gain((L, HEAD_DIM)),
        "moba_q_norm": gain((L, HEAD_DIM)),
        "moba_k_norm": gain((L, HEAD_DIM)),
        "diff_lambda": nrm((L, 4, DIFF_QK_DIM), 0.1),
        "diff_q_norm": gain((L, DIFF_QK_DIM)),
        "diff_k_norm": gain((L, DIFF_QK_DIM)),
        "diff_sub_norm": gain((L, HEAD_DIM)),
        "mem_w_kv": nrm((L, D_MODEL, 2 * GROUP_WIDTH), D_MODEL ** -0.5),
        "mem_q_norm": gain((L, HEAD_DIM)),
        "mem_k_norm": gain((L, HEAD_DIM)),
        "w_o": nrm((L, MIX_WIDTH, D_MODEL), MIX_WIDTH ** -0.5),
        "ffn_w_gate": nrm((L, D_MODEL, D_FF_2), D_MODEL ** -0.5),
        "ffn_w_up": nrm((L, D_MODEL, D_FF_2), D_MODEL ** -0.5),
        "ffn_conv_w": nrm((L, CONV_WIDTH, D_FF_2), CONV_WIDTH ** -0.5),
        "ffn_conv_b": nrm((L, D_FF_2), 0.02),
        "ffn_w_down": nrm((L, D_FF_2, D_MODEL), D_FF_2 ** -0.5),
    }

def second_block(x, mem, positions, attn_norm, ffn_norm, mem_norm, w_in,
              mla_cq_norm, mla_ckv_norm, mla_w_uq, mla_w_ukv, mla_q_norm, mla_k_norm,
              fox_b_f, fox_q_norm, fox_k_norm,
              moba_q_norm, moba_k_norm,
              diff_lambda, diff_q_norm, diff_k_norm, diff_sub_norm,
              mem_w_kv, mem_q_norm, mem_k_norm,
              w_o, ffn_w_gate, ffn_w_up, ffn_conv_w, ffn_conv_b, ffn_w_down):
    bsz, seq, _ = x.shape
    R = MLA_ROPE_DIM
    cos_a, sin_a = _rope_tables(positions, MLA_ROPE_DIM)
    cos_c, sin_c = _rope_tables(positions, ROT_MOBA)
    cos_d, sin_d = _rope_tables(positions, ROT_DIFF)
    split_at = np.cumsum(IN_SIZES)[:-1].tolist()

    for l in range(DEPTH):
        xn = _rms_norm(x, attn_norm[l])
        h = xn @ w_in[l]
        cq, ckv, kr, fox_qkv, fox_f, moba_qkv, diff_qkv, mem_q = jnp.split(h, split_at, axis=-1)

        q_a = _heads(_rms_norm(cq, mla_cq_norm[l]) @ mla_w_uq[l], N_HEADS_GROUP)
        kv_a = _heads(_rms_norm(ckv, mla_ckv_norm[l]) @ mla_w_ukv[l], N_HEADS_GROUP)
        gq, gk = mla_q_norm[l], mla_k_norm[l]
        q_a = jnp.concatenate([_rope(_rms_norm(q_a[..., :R], gq[:R]), cos_a, sin_a),
                               _rms_norm(q_a[..., R:], gq[R:])], axis=-1)
        k_nope = _rms_norm(kv_a[..., :MLA_NOPE_DIM], gk[R:])
        k_rope = _rope(_rms_norm(kr[:, None], gk[:R]), cos_a, sin_a)
        k_a = jnp.concatenate([jnp.broadcast_to(k_rope, k_nope.shape[:-1] + (R,)), k_nope], axis=-1)
        o_a = _dense_causal_attention(q_a, k_a, kv_a[..., MLA_NOPE_DIM:], MLA_QK_DIM ** -0.5)

        q_b, k_b, v_b = [_heads(t, N_HEADS_GROUP) for t in jnp.split(fox_qkv, 3, axis=-1)]
        log_f = jax.nn.log_sigmoid(fox_f.astype(jnp.float32) + fox_b_f[l].astype(jnp.float32))
        decay = jnp.cumsum(log_f, axis=1).transpose(0, 2, 1)
        o_b = _dense_causal_attention(_rms_norm(q_b, fox_q_norm[l]), _rms_norm(k_b, fox_k_norm[l]),
                                      v_b, HEAD_DIM ** -0.5, decay)

        q_c, k_c, v_c = [_heads(t, N_HEADS_GROUP) for t in jnp.split(moba_qkv, 3, axis=-1)]
        q_c = _rope(_rms_norm(q_c, moba_q_norm[l]), cos_c, sin_c)
        k_c = _rope(_rms_norm(k_c, moba_k_norm[l]), cos_c, sin_c)
        o_c = _moba_attention(q_c, k_c, v_c, HEAD_DIM ** -0.5)

        dq, dk, dv = jnp.split(diff_qkv, 3, axis=-1)
        q_d = _rope(_rms_norm(_split_pairs(dq), diff_q_norm[l]), cos_d, sin_d)
        k_d = _rope(_rms_norm(_split_pairs(dk), diff_k_norm[l]), cos_d, sin_d)
        lam_vec = diff_lambda[l].astype(jnp.float32)
        lam_init = 0.8 - 0.6 * math.exp(-0.3 * l)
        lam = (jnp.exp(jnp.sum(lam_vec[0] * lam_vec[1]))
               - jnp.exp(jnp.sum(lam_vec[2] * lam_vec[3])) + lam_init)
        o_d = _diff_causal_attention(q_d[0], q_d[1], k_d[0], k_d[1], _heads(dv, N_HEADS_GROUP),
                                     lam, DIFF_QK_DIM ** -0.5)
        o_d = _rms_norm(o_d, diff_sub_norm[l]) * (1.0 - lam_init)

        q_e = _rms_norm(_heads(mem_q, N_HEADS_GROUP), mem_q_norm[l])
        mem_kv = _rms_norm(mem, mem_norm[l]) @ mem_w_kv[l]
        k_e, v_e = [_heads(t, N_HEADS_GROUP) for t in jnp.split(mem_kv, 2, axis=-1)]
        o_e = _memory_attention(q_e, _rms_norm(k_e, mem_k_norm[l]), v_e, HEAD_DIM ** -0.5)

        mixed = jnp.concatenate([_merge(o_a), _merge(o_b), _merge(o_c), _merge(o_d), _merge(o_e)], axis=-1)
        x = x + mixed @ w_o[l]

        xn = _rms_norm(x, ffn_norm[l])
        gate = _causal_dwconv(xn @ ffn_w_gate[l], ffn_conv_w[l], ffn_conv_b[l])
        x = x + (jax.nn.silu(gate) * (xn @ ffn_w_up[l])) @ ffn_w_down[l]
    return x


def setup_inputs(seed=0):
    out = dict(first_inputs(seed))
    for name, value in second_inputs(seed + 1).items():
        if name != "x":
            out[name + "_2"] = value
    return out


def reference(
    x, p, positions, norm_gains, w_in_ab, conv_a, a_log, dt_bias, norm_a, i_bias_b, f_bias_b,
    norm_b, w_out_ab, w_qkv_c, b_qkv_c, sinks_c, w_o_c, b_o_c, w_up, w_down, w_ple, w_ple_gate,
    mem_2, positions_2, attn_norm_2, ffn_norm_2, mem_norm_2, w_in_2, mla_cq_norm_2,
    mla_ckv_norm_2, mla_w_uq_2, mla_w_ukv_2, mla_q_norm_2, mla_k_norm_2, fox_b_f_2,
    fox_q_norm_2, fox_k_norm_2, moba_q_norm_2, moba_k_norm_2, diff_lambda_2, diff_q_norm_2,
    diff_k_norm_2, diff_sub_norm_2, mem_w_kv_2, mem_q_norm_2, mem_k_norm_2, w_o_2, ffn_w_gate_2,
    ffn_w_up_2, ffn_conv_w_2, ffn_conv_b_2, ffn_w_down_2,
):
    x = first_block(
        x, p, positions, norm_gains, w_in_ab, conv_a, a_log, dt_bias, norm_a, i_bias_b,
        f_bias_b, norm_b, w_out_ab, w_qkv_c, b_qkv_c, sinks_c, w_o_c, b_o_c, w_up, w_down,
        w_ple, w_ple_gate,
    )
    return second_block(
        x, mem_2, positions_2, attn_norm_2, ffn_norm_2, mem_norm_2, w_in_2, mla_cq_norm_2,
        mla_ckv_norm_2, mla_w_uq_2, mla_w_ukv_2, mla_q_norm_2, mla_k_norm_2, fox_b_f_2,
        fox_q_norm_2, fox_k_norm_2, moba_q_norm_2, moba_k_norm_2, diff_lambda_2, diff_q_norm_2,
        diff_k_norm_2, diff_sub_norm_2, mem_w_kv_2, mem_q_norm_2, mem_k_norm_2, w_o_2,
        ffn_w_gate_2, ffn_w_up_2, ffn_conv_w_2, ffn_conv_b_2, ffn_w_down_2,
    )


_drawn_inputs = setup_inputs


def setup_inputs(seed=0):
    import zlib

    import numpy as np

    out = dict(_drawn_inputs(seed))
    spreads = {}
    factors = {'i_bias_b': 64.0,
     'attn_norm_2': 3.189,
     'mem_norm_2': 8.0,
     'mla_cq_norm_2': 8.0,
     'mla_ckv_norm_2': 8.0,
     'mla_q_norm_2': 8.0,
     'mla_k_norm_2': 8.0,
     'fox_q_norm_2': 8.0,
     'fox_k_norm_2': 8.0,
     'moba_q_norm_2': 8.0,
     'moba_k_norm_2': 8.0,
     'diff_lambda_2': 5.048,
     'diff_q_norm_2': 8.0,
     'diff_k_norm_2': 8.0,
     'diff_sub_norm_2': 6.961,
     'mem_q_norm_2': 8.0,
     'mem_k_norm_2': 8.0,
     'ffn_conv_b_2': 8.0}
    for name, (base, spread) in spreads.items():
        noise = np.random.default_rng([zlib.crc32(name.encode()), seed]).standard_normal(out[name].shape)
        drawn = base * np.exp(spread * noise) if base else spread * noise
        out[name] = jnp.asarray(drawn.astype(out[name].dtype))
    for name, factor in factors.items():
        out[name] = (out[name] * factor).astype(out[name].dtype)
    return out
```

```python
from contextlib import ExitStack

import numpy as np

import concourse.bass as bass
import concourse.mybir as mybir

F32 = mybir.dt.float32
I32 = mybir.dt.int32
ACT = mybir.ActivationFunctionType
ALU = mybir.AluOpType
AXX = mybir.AxisListType.X

P = 128
SEQ = 256
NT = SEQ // P
D = 1024
DC = D // P
EPS = 1e-6
BIG = 1e30
TWO_PI = 2 * np.pi

HA = 4
QKV_A = 1536
W_IN = 4112
COL_BETA = QKV_A
COL_Z = QKV_A + 8
COL_QB = COL_Z + 512
COL_VB = COL_QB + 1024
COL_IF = COL_VB + 512
COL_O = COL_IF + 8
CH, CKV, CHD = 16, 4, 64
DFF1 = 4096
DFF2 = 2816
MIX2 = 1280
ROT_C, ROT_A, ROT_M, ROT_D = 32, 16, 8, 4
D_IN2 = 2916
C_CQ, C_CKV, C_KR, C_FOX, C_FF, C_MOBA, C_DIFF, C_MEM = 0, 192, 320, 352, 1120, 1124, 1892, 2660

COLS = {}
_at = 0
for _name, _n in (("pre1", 2 * 2 * DC), ("attn2", 2 * DC), ("ffn2", 2 * DC), ("mem2", 2 * DC),
                  ("conv_a", 12 * 4), ("fconv_w", 2 * 3 * 22), ("fconv_b", 2 * 22)):
    COLS[_name] = _at
    _at += _n
N_COLS = _at

ROWS = [dict(), dict(), dict(), dict()]
_parts = [
    (("post", D), ("post_ff", D), ("norm_a", 512), ("norm_b", 512), ("gate_bias", 16), ("a_log", 4)),
    (("post", D), ("post_ff", D), ("b_qkv", 1536), ("b_o", D), ("sinks", CH)),
    (("cq", 192), ("ckv", 128), ("kr", 32), ("fox", 512), ("moba", 512), ("diff", 512), ("memq", 256),
     ("memk", 256), ("mla_q", 384), ("mla_k", 256), ("sub", 256), ("fox_b", 4), ("lambda", 128)),
]
_parts.append(_parts[2])
ROW_LEN = []
for _l, _p in enumerate(_parts):
    _at = 0
    for _name, _n in _p:
        ROWS[_l][_name] = (_at, _n)
        _at += _n
    ROW_LEN.append(_at)
ROW_MAX = max(ROW_LEN)

CONST = {}
_at = 0
for _name, _n in (("ident", P), ("causal3", 384), ("causal_neg", 384), ("window_neg", 384),
                  ("level", 7 * P), ("select", 8 * P), ("freq", 60), ("sign8", 8),
                  ("inv_d", 48)):
    CONST[_name] = (_at, _n)
    _at += _n
N_CONST = _at
SLOT_D = [192, 128, 32] + [64] * 8 + [64] * 8 + [32] * 16 + [64] * 4
N_SLOT = len(SLOT_D)


def constants():
    c = np.zeros((P, N_CONST), np.float32)

    def put(name, value):
        a, n = CONST[name]
        c[:, a:a + n] = np.asarray(value, np.float32).reshape(value.shape[0], -1)

    i = np.arange(P)
    upper = (i[:, None] <= i[None, :]).astype(np.float32)
    one, zero = np.ones((P, P), np.float32), np.zeros((P, P), np.float32)
    put("ident", np.eye(P, dtype=np.float32))
    put("causal3", np.concatenate([upper, one, upper], 1))
    lower_neg = np.where(i[None, :] <= i[:, None], 0.0, -BIG)
    prev_neg = np.where(i[None, :] > i[:, None], 0.0, -BIG)
    put("causal_neg", np.concatenate([lower_neg, zero, lower_neg], 1))
    put("window_neg", np.concatenate([lower_neg, prev_neg, lower_neg], 1))
    levels = []
    for n in range(7):
        s = 1 << n
        e, k = i[:, None], i[None, :]
        levels.append(((e // (2 * s) == k // (2 * s)) & (e % (2 * s) < s) & (k % (2 * s) >= s)))
    put("level", np.concatenate(levels, 1))
    sel = np.zeros((P, 8, P))
    for h in range(8):
        sel[h, h] = 1
    put("select", sel)
    f32 = np.float32
    freq = [f32(theta) ** (-np.arange(0, r, dtype=f32) / f32(r)) for theta, r in
            ((10000.0, ROT_C), (500000.0, ROT_A), (500000.0, ROT_M), (500000.0, ROT_D))]
    put("freq", np.tile(np.concatenate(freq)[None], (P, 1)))
    put("sign8", np.tile(np.array([1.0] * 4 + [-1.0] * 4)[None], (P, 1)))
    inv = np.zeros(48)
    inv[:N_SLOT] = 1.0 / np.array(SLOT_D)
    put("inv_d", np.tile(inv[None], (P, 1)))
    return c


class Line:

    def __init__(self, engine, sem):
        self.engine, self.sem, self.count, self.waited = engine, sem, 0, {}

    def need(self, *marks):
        for m in marks:
            if m is None:
                continue
            if isinstance(m, list):
                self.need(*m)
                continue
            sem, value = m
            if self.waited.get(id(sem), 0) < value:
                self.engine.wait_ge(sem, value)
                self.waited[id(sem)] = value
        return self.engine

    def did(self, instruction):
        instruction.then_inc(self.sem, 1)
        self.count += 1
        return self.sem, self.count

    def last(self):
        return (self.sem, self.count) if self.count else None


class Banks:

    def __init__(self, banks):
        self.banks, self.free_at, self.turn, self.held = banks, [None] * len(banks), 0, [False] * len(banks)

    def take(self, pe):
        b = self.turn
        self.turn = (b + 1) % len(self.banks)
        assert not self.held[b]
        self.held[b] = True
        pe.need(self.free_at[b])
        return b

    def free(self, b, *marks):
        assert self.held[b]
        self.held[b], self.free_at[b] = False, list(marks)


class Slots:

    def __init__(self, line, tensor, n, width, sems):
        self.line, self.tensor, self.n, self.width, self.sems = line, tensor, n, width, sems
        self.turn, self.loads, self.free_at = 0, [0] * n, [None] * n

    def load(self, pieces):
        s = self.turn
        self.turn = (s + 1) % self.n
        self.line.need(self.free_at[s])
        for parts, at, shape, src in pieces:
            n = int(np.prod(shape))
            dst = self.tensor[0:parts, s * self.width + at:s * self.width + at + n]
            if len(shape) == 2:
                dst = dst.rearrange("p (k n) -> p k n", k=shape[0])
            self.line.engine.dma_start(dst, src).then_inc(self.sems[s], 16)
            self.loads[s] += 16
        return s, (self.sems[s], self.loads[s])

    def view(self, s, k, n, at=0):
        a = s * self.width + at
        return self.tensor[:, a:a + k * n].rearrange("p (k n) -> p k n", k=k)

    def free(self, s, mark):
        self.free_at[s] = mark


def spread(ap, axis, n):
    shape = list(ap.shape)
    shape.insert(axis, n)
    return ap.unsqueeze(axis).to_broadcast(shape)


def skewed(stages, n):
    for step in range(n + len(stages) - 1):
        for k, stage in reversed(list(enumerate(stages))):
            if 0 <= step - k < n:
                stage(step - k)


def program(nc, T, out):
    ctx = ExitStack()
    with ctx:
        def sbuf(name, shape, dt=F32):
            return ctx.enter_context(nc.sbuf_tensor(name, shape, dt))

        def sem(name):
            return ctx.enter_context(nc.semaphore(name))

        pe = Line(nc.tensor, sem("pe_done"))
        dve = Line(nc.vector, sem("dve_done"))
        act = Line(nc.scalar, sem("act_done"))
        pool = Line(nc.gpsimd, sem("pool_done"))
        sp = Line(nc.sync, sem("sp_done"))
        V, A, G, E = nc.vector, nc.scalar, nc.gpsimd, nc.tensor

        consts = sbuf("consts", [P, N_CONST])
        cols = sbuf("cols", [P, N_COLS])
        rows = sbuf("rows", [P, ROW_MAX])
        h = sbuf("h", [P, NT, D])
        trig = sbuf("trig", [P, 2, NT, 60])
        stat = sbuf("stat", [P, 256])
        SLOT = 8 * 512
        N_SLOTS = 3
        ring = sbuf("ring", [P, N_SLOTS * SLOT])
        WORK = 29000
        work = sbuf("work", [P, WORK])
        psum = [ctx.enter_context(nc.psum_tensor(f"bank{b}", [P, 512], F32)) for b in range(8)]
        banks = Banks(psum, )
        slots = Slots(sp, ring, N_SLOTS, SLOT, [sem(f"slot{s}_landed") for s in range(N_SLOTS)])
        s_in, s_rows, s_out = sem("inputs_landed"), sem("rows_landed"), sem("output_landed")

        def const(name, n=None):
            a, w = CONST[name]
            return consts[:, a:a + (n or w)]

        ident = const("ident")
        ones = const("causal3")[:, P:2 * P]

        cursor = [0]

        def shaped(v, *shape):
            if len(shape) == 2:
                return v.rearrange("p (a b) -> p a b", a=shape[0])
            if len(shape) == 3:
                return v.rearrange("p (a b c) -> p a b c", a=shape[0], b=shape[1])
            if len(shape) == 4:
                return v.rearrange("p (a b c d) -> p a b c d", a=shape[0], b=shape[1], c=shape[2])
            return v

        def cut(*shape):
            n = int(np.prod(shape))
            a = cursor[0]
            cursor[0] = a + n
            assert cursor[0] <= WORK, (cursor[0], WORK)
            return shaped(work[:, a:a + n], *shape)

        def join():
            ends = [x.last() for x in (pe, dve, act, pool)]
            for x in (pe, dve, act, pool, ):
                x.need(ends)
            cursor[0] = 0

        def copy_on(line, dst, src, *after):
            line.need(*after)
            if line is act:
                return act.did(A.copy(dst, src))
            return line.did(line.engine.tensor_copy(dst, src))

        def inv_root(ms, root, inv, after):
            act.need(after)
            m = act.did(A.activation(root, ms, ACT.Sqrt))
            dve.need(m)
            return dve.did(V.reciprocal(inv, root))

        def transposes(blocks, after):
            b = banks.take(pe)
            pe.need(after)
            for k, src in enumerate(blocks):
                w = src.shape[-1]
                mm = E.transpose(psum[b][0:w, k * P:(k + 1) * P], src, ident)
            return b, pe.did(mm)

        evac_turn = [0]

        def evacuate(b, dst, src, *after):
            evac_turn[0] += 1
            m = copy_on(act if evac_turn[0] % 2 else dve, dst, src, *after)
            banks.free(b, m)
            return m

        def feature_major(src, n_chunks, dst, after, gain=None):
            marks = []
            for k in range(0, n_chunks, 2):
                b, m = transposes([src[:, t, (k + i) * P:(k + i + 1) * P] for i in range(2) for t in range(NT)], after)
                bank = psum[b][:, :].rearrange("p (k n) -> p k n", k=2)
                if gain is None:
                    marks.append(evacuate(b, dst[:, k:k + 2, :], bank, m))
                else:
                    dve.need(m)
                    m = dve.did(V.tensor_tensor(dst[:, k:k + 2, :], bank, spread(gain[:, k:k + 2], 2, SEQ), ALU.mult))
                    banks.free(b, m)
                    marks.append(m)
            return marks

        def heads_transposed(src, n, d, dst, after):
            marks = []
            for k in range(0, n, 2):
                m_ = min(2, n - k)
                b, m = transposes([src(k + i, t) for i in range(m_) for t in range(NT)], after)
                bank = psum[b][0:d, 0:m_ * SEQ].rearrange("p (k n) -> p k n", k=m_)
                marks.append(evacuate(b, dst[0:d, k:k + m_, :], bank, m))
            return marks

        def normed(src, dst, after, s=0):
            marks = []
            for t in range(NT):
                act.need(after)
                m = act.did(A.activation(dst[:, t, :], src[:, t, :], ACT.Square, accum_out=stat[:, s + t:s + t + 1]))
                marks.append(m)
            dve.need(marks)
            m = dve.did(V.tensor_scalar(stat[:, s + 2:s + 4], stat[:, s:s + 2], 1.0 / D, EPS, ALU.mult, ALU.add))
            m = inv_root(stat[:, s + 2:s + 4], stat[:, s + 4:s + 6], stat[:, s + 6:s + 8], m)
            marks = []
            for t in range(NT):
                line = dve if t else pool
                line.need(m, after)
                marks.append(line.did(line.engine.tensor_scalar(dst[:, t, :], src[:, t, :], stat[:, s + 6 + t:s + 7 + t],
                                                                None, ALU.mult)))
            return marks

        def panel(w, k0, kc, n0, nn):
            s, m = slots.load([(P, 0, (kc, nn), w[k0 * P:(k0 + kc) * P, n0:n0 + nn].rearrange("(k p) n -> p k n", p=P))])
            return s, slots.view(s, kc, nn), m

        def token_linear(xT, kc, w, n0, nn, evac, after):
            s, wv, m = panel(w, 0, kc, n0, nn)
            for t in range(NT):
                b = banks.take(pe)
                pe.need(m, after)
                for k in range(kc):
                    mm = E.matmul(psum[b][:, 0:nn], xT[:, k, t * P:(t + 1) * P], wv[:, k, :],
                                  start=(k == 0), stop=(k == kc - 1))
                done = pe.did(mm)
                evac(t, b, done)
            slots.free(s, done)

        def deep_linear(xT, kc, w, after, per=4):
            held = [banks.take(pe) for _ in range(4)]
            for k0 in range(0, kc, per):
                n = min(per, kc - k0)
                s, wv, m = panel(w, k0, n, 0, D)
                pe.need(m, after)
                for t in range(NT):
                    for half in range(2):
                        for k in range(n):
                            mm = E.matmul(psum[held[2 * t + half]][:, :], xT[:, k0 + k, t * P:(t + 1) * P],
                                          wv[:, k, half * 512:(half + 1) * 512],
                                          start=(k0 + k == 0), stop=(k0 + k == kc - 1))
                done = pe.did(mm)
                slots.free(s, done)
            return held, done

        def feature_chunks(xT, wv, m, n, evac, after, m_cols=P):
            for c in range(0, n, 2):
                w_ = min(2, n - c)
                b = banks.take(pe)
                pe.need(m, after)
                for i in range(w_):
                    for k in range(DC):
                        mm = E.matmul(psum[b][0:m_cols, i * SEQ:(i + 1) * SEQ],
                                      wv[:, k, (c + i) * P:(c + i) * P + m_cols], xT[:, k, :],
                                      start=(k == 0), stop=(k == DC - 1))
                done = pe.did(mm)
                evac(c, w_, b, done)
            return done

        def add_normed(held, done, gain, mix, tmp, bias=None, gain_after=None):
            ready = []
            for t in range(NT):
                for half in range(2):
                    b = held[2 * t + half]
                    cut_ = slice(half * 512, (half + 1) * 512)
                    if bias is None:
                        ready.append(evacuate(b, mix[:, t, cut_], psum[b][:, :], done))
                    else:
                        dve.need(done, gain_after)
                        m = dve.did(V.tensor_tensor(mix[:, t, cut_], psum[b][:, :], bias[:, cut_], ALU.add))
                        banks.free(b, m)
                        ready.append(m)
            marks = normed(mix, tmp, ready)
            out_ = []
            for t in range(NT):
                dve.need(marks, gain_after)
                m = dve.did(V.tensor_tensor(tmp[:, t, :], tmp[:, t, :], gain, ALU.mult))
                dve.need(m)
                out_.append(dve.did(V.tensor_tensor(h[:, t, :], h[:, t, :], tmp[:, t, :], ALU.add)))
            return out_

        sp.engine.dma_start(consts[:, :], T["consts"]).then_inc(s_in, 16)
        sp.engine.dma_start(h[:, :, :], T["x"][0].rearrange("(t p) d -> p t d", p=P)).then_inc(s_in, 16)
        sp.engine.dma_start(cols[:, :], T["cols"]).then_inc(s_in, 16)
        pos_i = sbuf("pos_i", [P, 4], I32)
        sp.engine.dma_start(pos_i[:, :], T["positions"]).then_inc(s_in, 16)
        loaded = (s_in, 64)

        rows_count = [0]

        def load_rows(layer):
            sp.need(dve.last(), act.last(), pool.last())
            n = ROW_LEN[layer]
            sp.engine.dma_start(rows[:, 0:n], T["rows"][layer:layer + 1, 0:n].partition_broadcast(P).rearrange("q a n -> q (a n)")
                                ).then_inc(s_rows, 16)
            rows_count[0] += 16
            return (s_rows, rows_count[0])

        def row(layer, name):
            a, n = ROWS[layer][name]
            return rows[:, a:a + n]

        pos_f = sbuf("pos_f", [P, 4])
        ang = cut(NT, 60)
        turns = cut(NT, 60)
        for x in (pe, dve, act, pool):
            x.need(loaded)
        m = dve.did(V.tensor_copy(pos_f[:, :], pos_i[:, :]))
        dve.need(m)
        for t in range(NT):
            m = dve.did(V.tensor_scalar(ang[:, t, 0:ROT_C], const("freq")[:, 0:ROT_C], pos_f[:, t:t + 1], None, ALU.mult))
            m = dve.did(V.tensor_scalar(ang[:, t, ROT_C:60], const("freq")[:, ROT_C:60], pos_f[:, 2 + t:3 + t], None, ALU.mult))
        PI_A = 6.28125
        PI_B = float(np.float32(np.floor((TWO_PI - PI_A) * 2 ** 21) / 2 ** 21))
        PI_C = float(TWO_PI - PI_A - PI_B)
        MAGIC = float(3 * 2 ** 22)
        for which, shift in ((0, 0.25), (1, 0.0)):
            dst = trig[:, which, :, :]
            dve.need(m)
            m = dve.did(V.tensor_scalar(turns[:, :, :], ang[:, :, :], 1.0 / TWO_PI, shift, ALU.mult, ALU.add))
            dve.need(m)
            m = dve.did(V.tensor_scalar(turns[:, :, :], turns[:, :, :], MAGIC, None, ALU.add))
            dve.need(m)
            m = dve.did(V.tensor_scalar(turns[:, :, :], turns[:, :, :], MAGIC, None, ALU.subtract))
            src = ang
            for part in (PI_A, PI_B, PI_C):
                dve.need(m)
                m = dve.did(V.scalar_tensor_tensor(dst, turns[:, :, :], -part, src if src is dst else src[:, :, :], ALU.mult, ALU.add))
                src = dst
            if shift:
                dve.need(m)
                m = dve.did(V.tensor_scalar(dst, dst, float(np.pi / 2), None, ALU.add))
            dve.need(m)
            m = dve.did(V.tensor_scalar(dst, dst, float(np.float32(3.1415925)), -float(np.float32(3.1415925)), ALU.min, ALU.max))
            act.need(m)
            trig_ready = act.did(A.activation(dst, dst, ACT.Sin))
        join()

        def rope(x, dst, n, r, f0, t, tmp1, tmp2, after):
            c = spread(spread(trig[:, 0, t, f0:f0 + r], 1, 2), 1, n)
            s = spread(trig[:, 1, t, f0:f0 + r], 1, n)
            x4 = x.rearrange("p n (two r) -> p n two r", two=2)
            d4 = dst.rearrange("p n (two r) -> p n two r", two=2)
            a = tmp1[:, 0:n * 2 * r].rearrange("p (n two r) -> p n two r", two=2, r=r)
            b = tmp2[:, 0:n * 2 * r].rearrange("p (n two r) -> p n two r", two=2, r=r)
            dve.need(after, trig_ready, dve.last())
            dve.did(V.tensor_tensor(b[:, :, 0, :], x4[:, :, 1, :], s, ALU.mult))
            dve.did(V.tensor_tensor(b[:, :, 1, :], x4[:, :, 0, :], s, ALU.mult))
            m = dve.did(V.tensor_tensor(a, x4, c, ALU.mult))
            dve.need(m)
            dve.did(V.tensor_tensor(d4[:, :, 0, :], a[:, :, 0, :], b[:, :, 0, :], ALU.subtract))
            return dve.did(V.tensor_tensor(d4[:, :, 1, :], a[:, :, 1, :], b[:, :, 1, :], ALU.add))

        def feed_forward_1(layer, rows_ready):
            y = cut(NT, D)
            hT = cut(DC, SEQ)
            aT = cut(DFF1 // P, SEQ)
            r = cut(4, 512)
            m = normed(h, y, [dve.last()])
            g0 = COLS["pre1"] + (layer * 2 + 1) * DC
            m = feature_major(y, DC, hT, m, cols[:, g0:g0 + DC])
            used = [None] * 4
            n_done = [0]
            up = T["w_up"][layer]
            ready = []
            for n0 in range(0, DFF1, 512):
                s, wv, wm = panel(up, 0, DC, n0, 512)

                def evac(c, w_, b, done, n0=n0):
                    i = n_done[0] % 4
                    n_done[0] += 1
                    act.need(done, used[i])
                    m1 = act.did(A.activation(r[:, i, :], psum[b][:, :], ACT.Relu))
                    banks.free(b, m1)
                    line = dve if n_done[0] % 3 else pool
                    line.need(m1)
                    dst = aT[:, n0 // P + c:n0 // P + c + 2, :].rearrange("p k n -> p (k n)")
                    used[i] = line.did(line.engine.tensor_tensor(dst, r[:, i, :], r[:, i, :], ALU.mult))
                    ready.append(used[i])
                done = feature_chunks(hT, wv, wm, 4, evac, m)
                slots.free(s, done)
            held, done = deep_linear(aT, DFF1 // P, T["w_down"][layer], ready)
            return add_normed(held, done, row(layer, "post_ff"), y, cut(NT, D), gain_after=rows_ready)

        def gated_add(layer):
            hT = cut(DC, SEQ)
            gate = cut(4, 512)
            pt = cut(NT, 256)
            pT = cut(2, SEQ)
            sp.need(dve.last(), act.last(), pe.last(), pool.last())
            sp.engine.dma_start(pt, T["p"][layer, 0].rearrange("(t p) d -> p t d", p=P)).then_inc(s_in, 16)
            p_ready = (s_in, 64 + 16 * (layer + 1))
            m = feature_major(h, DC, hT, [dve.last()])
            pm = feature_major(pt, 2, pT, [p_ready])
            held, done = deep_linear(hT, DC, T["w_ple_gate"][layer], m)
            gm = []
            for i, b in enumerate(held):
                act.need(done)
                g = act.did(A.activation(gate[:, i, :], psum[b][:, :], ACT.Sigmoid))
                banks.free(b, g)
                gm.append(g)
            held, done = deep_linear(pT, 2, T["w_ple"][layer], pm)
            for i, b in enumerate(held):
                t, half = i // 2, i % 2
                dve.need(done, gm[i])
                m = dve.did(V.tensor_tensor(gate[:, i, :], gate[:, i, :], psum[b][:, :], ALU.mult))
                banks.free(b, m)
                dve.need(m)
                v = h[:, t, half * 512:(half + 1) * 512]
                m = dve.did(V.tensor_tensor(v, v, gate[:, i, :], ALU.add))
            return m

        def mixer_ab(rows_ready):
            w = T["w_in_ab"][0]
            top = cut(DC, SEQ)
            y = cut(NT, D)
            m = normed(h, y, loaded_all)
            xm = feature_major(y, DC, top, m, cols[:, COLS["pre1"]:COLS["pre1"] + DC])
            gates = cut(NT, 16)
            s, wm = slots.load([(P, 0, (DC, 8), w[:, COL_BETA:COL_BETA + 8].rearrange("(k p) n -> p k n", p=P)),
                                (P, DC * 8, (DC, 8), w[:, COL_IF:COL_IF + 8].rearrange("(k p) n -> p k n", p=P))])
            b = banks.take(pe)
            pe.need(wm, xm)
            for t in range(NT):
                for part in range(2):
                    wv = slots.view(s, DC, 8, part * DC * 8)
                    for k in range(DC):
                        mm = E.matmul(psum[b][:, t * 16 + part * 8:t * 16 + part * 8 + 8], top[:, k, t * P:(t + 1) * P],
                                      wv[:, k, :], start=(k == 0), stop=(k == DC - 1))
            done = pe.did(mm)
            slots.free(s, done)
            dve.need(done, rows_ready)
            m = dve.did(V.tensor_tensor(gates, psum[b][:, 0:32].rearrange("p (t n) -> p t n", t=NT),
                                        spread(row(0, "gate_bias"), 1, NT), ALU.add))
            banks.free(b, m)
            v8 = cut(NT, 8)
            l8 = cut(NT, 8)
            g8 = cut(NT, 8)
            beta = cut(NT, 4)
            ea = cut(8)
            gview = gates.rearrange("p t (a b) -> p t a b", a=4)
            dve.need(m)
            m = dve.did(V.tensor_tensor(v8.rearrange("p t (a b) -> p t a b", a=2), gview[:, :, 1::2, :],
                                        spread(const("sign8").rearrange("p (a b) -> p a b", a=2), 1, NT), ALU.mult))
            dve.need(m)
            m = dve.did(V.scalar_tensor_tensor(l8, v8, -1.0, v8, ALU.mult, ALU.max))
            act.need(m)
            m = act.did(A.activation(l8, l8, ACT.Exp, scale=-1.0))
            m2 = act.did(A.activation(ea[:, 0:4], row(0, "a_log"), ACT.Exp))
            act.need(m)
            m = act.did(A.activation(l8, l8, ACT.Ln, bias=1.0))
            m3 = act.did(A.activation(beta, gates[:, :, 0:4], ACT.Sigmoid))
            dve.did(V.memset(ea[:, 4:8], 1.0))
            dve.need(m, m2, dve.last())
            m = dve.did(V.scalar_tensor_tensor(g8, v8, 0.0, l8, ALU.max, ALU.add))
            dve.need(m)
            g_ready = dve.did(V.scalar_tensor_tensor(g8, g8, -1.0, spread(ea, 1, NT), ALU.mult, ALU.mult))
            gc = cut(NT, 8)
            tri = const("causal3")
            b = banks.take(pe)
            pe.need(g_ready)
            for t in range(NT):
                for s_ in range(t + 1):
                    mm = E.matmul(psum[b][:, t * 8:t * 8 + 8], tri[:, (t + s_) * P:(t + s_ + 1) * P], g8[:, s_, :],
                                  start=(s_ == 0), stop=(s_ == t))
            done = pe.did(mm)
            dve.need(done)
            gc_ready = dve.did(V.tensor_copy(gc, psum[b][:, 0:16].rearrange("p (t n) -> p t n", t=NT)))
            banks.free(b, gc_ready)
            ab = cut(NT, 8)
            dve.need(gc_ready, m3)
            dve.did(V.tensor_copy(ab[:, :, 0:4], beta))
            m = dve.did(V.tensor_tensor(ab[:, :, 4:8], gates[:, :, 8:12], gc[:, :, 4:8], ALU.subtract))
            b, done = transposes([ab[:, t, :] for t in range(NT)], [m])
            abT = cut(SEQ)
            act.need(done)
            m = act.did(A.copy(abT[0:8, :], psum[b][0:8, 0:SEQ]))
            banks.free(b, m)
            mxT = cut(SEQ)
            dve.need(m)
            mx_ready = dve.did(V.tensor_tensor_scan(mxT[0:8, :], abT[0:8, :], abT[0:8, :], 0.0, ALU.max, ALU.max))
            mcol = cut(NT, 8)
            b = banks.take(pe)
            pe.need(mx_ready)
            for t in range(NT):
                mm = E.transpose(psum[b][:, t * 8:t * 8 + 8], mxT[0:8, t * P:(t + 1) * P], ident[0:8, 0:8])
            done = pe.did(mm)
            dve.need(done)
            mcol_ready = dve.did(V.tensor_copy(mcol, psum[b][:, 0:16].rearrange("p (t n) -> p t n", t=NT)))
            banks.free(b, mcol_ready)

            qkv = cut(12, SEQ)
            pad = cut(2, 2, SEQ + 3)
            cv = cut(2, 2, SEQ)
            zeroed = pool.did(G.memset(pad[:, :, :, 0:3], 0.0))
            pad_free, cv_free = [zeroed, zeroed], [None, None]
            qkv_ready = []
            wc = COLS["conv_a"]
            turn = [0]
            for n0 in range(0, QKV_A, 512):
                s, wv, wm = panel(w, 0, DC, n0, 512)

                def evac(c, w_, b, done, n0=n0):
                    i = turn[0] % 2
                    turn[0] += 1
                    act.need(done, pad_free[i])
                    m = act.did(A.copy(pad[:, i, :, 3:], psum[b][:, :].rearrange("p (k n) -> p k n", k=2)))
                    banks.free(b, m)
                    ends = []
                    for j in range(2):
                        ch = n0 // P + c + j
                        dve.need(m, cv_free[i])
                        e = dve.did(V.tensor_scalar(cv[:, i, j, :], pad[:, i, j, 0:SEQ], cols[:, wc + ch * 4:wc + ch * 4 + 1],
                                                    None, ALU.mult))
                        ends.append(e)
                    for k in range(1, 4):
                        for j in range(2):
                            ch = n0 // P + c + j
                            dve.need(ends[j])
                            ends[j] = dve.did(V.scalar_tensor_tensor(cv[:, i, j, :], pad[:, i, j, k:k + SEQ],
                                                                     cols[:, wc + ch * 4 + k:wc + ch * 4 + k + 1],
                                                                     cv[:, i, j, :], ALU.mult, ALU.add))
                    pad_free[i] = ends[1]
                    act.need(ends)
                    cv_free[i] = act.did(A.activation(qkv[:, n0 // P + c:n0 // P + c + 2, :], cv[:, i, :, :], ACT.Silu))
                    qkv_ready.append(cv_free[i])
                slots.free(s, feature_chunks(top, wv, wm, 4, evac, xm))

            qkb = cut(8, SEQ)
            qkb_ready = []
            for part in range(2):
                s, wv, wm = panel(w, 0, DC, COL_QB + part * 512, 512)

                def evac(c, w_, b, done, part=part):
                    act.need(done)
                    m = act.did(A.mul(qkb[:, part * 4 + c:part * 4 + c + 2, :], psum[b][:, :].rearrange("p (k n) -> p k n", k=2),
                                      1.0 if part else float(P) ** -0.5))
                    banks.free(b, m)
                    qkb_ready.append(m)
                slots.free(s, feature_chunks(top, wv, wm, 4, evac, xm))
            zs, vb, og = cut(NT, 512), cut(NT, 512), cut(NT, 512)
            lin_ready = []
            for n0, dst, fn in ((COL_Z, zs, ACT.Silu), (COL_VB, vb, ACT.Copy), (COL_O, og, ACT.Sigmoid)):
                def evac(t, b, done, dst=dst, fn=fn):
                    act.need(done)
                    m = act.did(A.activation(dst[:, t, :], psum[b][:, :], fn))
                    banks.free(b, m)
                    lin_ready.append(m)
                token_linear(top, DC, w, n0, 512, evac, xm)

            kbT = cut(4, SEQ)
            sq = cut(2, 512)
            nr = cut(2, 512)
            flat = qkv.rearrange("p k n -> p (k n)")
            l2_ready = []
            sq_free, nr_free = [None, None], [None, None]
            for c in range(0, 8, 2):
                i = (c // 2) % 2
                src = flat[:, c * SEQ:(c + 2) * SEQ]
                pool.need(qkv_ready, sq_free[i])
                m = pool.did(G.tensor_tensor(sq[:, i, :], src, src, ALU.mult))
                b = banks.take(pe)
                pe.need(m)
                done = pe.did(E.matmul(psum[b][:, :], ones, sq[:, i, :], start=True, stop=True))
                sq_free[i] = done
                dve.need(done, nr_free[i])
                m = dve.did(V.tensor_scalar(nr[:, i, :], psum[b][:, :], EPS, None, ALU.add))
                banks.free(b, m)
                m = inv_root(nr[:, i, :], nr[:, i, :], nr[:, i, :], m)
                dve.need(m)
                m = dve.did(V.scalar_tensor_tensor(src, src, float(P) ** -0.5 if c < 4 else 1.0, nr[:, i, :], ALU.mult, ALU.mult))
                nr_free[i] = m
                l2_ready.append(m)
            vbeta = cut(NT, 512)
            v_ready = []
            for t in range(NT):
                b, done = transposes([qkv[:, 8 + c, t * P:(t + 1) * P] for c in range(4)], qkv_ready)
                dve.need(done, m3)
                m = dve.did(V.tensor_tensor(vbeta[:, t, :].rearrange("p (h d) -> p h d", h=4),
                                            psum[b][:, :].rearrange("p (h d) -> p h d", h=4),
                                            spread(beta[:, t, :], 2, P), ALU.mult))
                banks.free(b, m)
                v_ready.append(m)

            select = const("select").rearrange("p (h n) -> p h n", h=8)
            gb = cut(NT, P)
            LT = cut(4, 384)
            AT = cut(4, 384)
            PT = cut(4, 384)
            dec = cut(2, 384)
            dec_free = [None, None]
            gb_free = None
            LT_ready, AT_ready, PT_ready = [], [], []

            def key_query(dst_bank, kT, qT, after):
                pe.need(after)
                E.matmul(psum[dst_bank][:, 0:SEQ], kT[:, 0:P], qT[:, 0:SEQ], start=True, stop=True)
                return pe.did(E.matmul(psum[dst_bank][:, SEQ:384], kT[:, P:SEQ], qT[:, P:SEQ], start=True, stop=True))

            for hd in range(4):
                b = banks.take(pe)
                pe.need(mx_ready)
                done = pe.did(E.matmul(psum[b][:, 0:SEQ], select[0:8, hd, :], abT[0:8, :], start=True, stop=True))
                dve.need(done, l2_ready)
                kb_ready = dve.did(V.tensor_tensor(kbT[:, hd, :], qkv[:, 4 + hd, :], psum[b][:, 0:SEQ], ALU.mult))
                banks.free(b, kb_ready)
                dve.need(gb_free)
                m = dve.did(V.tensor_copy(gb, spread(g8[:, :, hd], 2, P)))
                b = banks.take(pe)
                pe.need(m)
                E.matmul(psum[b][:, 0:SEQ], gb[:, 0, :], tri[:, 0:SEQ], start=True, stop=False)
                gb_free = done = pe.did(E.matmul(psum[b][:, P:SEQ], gb[:, 1, :], tri[:, SEQ:384], start=False, stop=True))
                i = hd % 2
                dve.need(done, dec_free[i])
                dve.did(V.tensor_scalar(dec[:, i, 0:SEQ], psum[b][:, 0:SEQ], gc[:, 0, hd:hd + 1], 0.0, ALU.subtract, ALU.min))
                m = dve.did(V.tensor_scalar(dec[:, i, SEQ:384], psum[b][:, P:SEQ], gc[:, 1, hd:hd + 1], 0.0, ALU.subtract, ALU.min))
                banks.free(b, m)
                act.need(m)
                m = dec_ready = act.did(A.activation(dec[:, i, :], dec[:, i, :], ACT.Exp))
                pool.need(m)
                e2 = pool.did(G.tensor_tensor(AT[:, hd, :], dec[:, i, :], const("causal3"), ALU.mult))
                b = banks.take(pe)
                done = key_query(b, qkv[:, 4 + hd, :], kbT[:, hd, :], [kb_ready])
                dve.need(done, dec_ready)
                m = dve.did(V.tensor_tensor(LT[:, hd, :], dec[:, i, :], psum[b][:, 0:384], ALU.mult))
                dec_free[i] = [e2, m]
                banks.free(b, m)
                LT_ready.append(m)
                b = banks.take(pe)
                done = key_query(b, qkv[:, 4 + hd, :], qkv[:, hd, :], [l2_ready])
                dve.need(done, e2)
                m = dve.did(V.tensor_tensor(AT[:, hd, :], AT[:, hd, :], psum[b][:, 0:384], ALU.mult))
                banks.free(b, m)
                AT_ready.append(m)

            level = const("level").rearrange("p (l n) -> p l n", l=7)
            N_, M_ = [[cut(4, P) for _ in range(NT)] for _ in range(2)]
            C_ = [shaped(sq[:, j, :], 4, P) for j in range(NT)]
            Q_ = [shaped(nr[:, j, :], 4, P) for j in range(NT)]
            n_ready, m_ready, q_free, c_free = [None] * 2, [None] * 2, [None] * 2, [None] * 2
            idb = spread(ident, 1, 4)

            def diag(j):
                return LT[:, :, 0:P] if j == 0 else LT[:, :, SEQ:384]
            for j in range(NT):
                pool.need(LT_ready)
                m = pool.did(G.tensor_tensor(C_[j], diag(j), spread(level[:, 0, :], 1, 4), ALU.mult))
                dve.need(m)
                c_free[j] = n_ready[j] = dve.did(V.tensor_tensor(N_[j], idb, C_[j], ALU.subtract))
                b, done = transposes([N_[j][:, hd, :] for hd in range(4)], [n_ready[j]])
                act.need(done)
                m_ready[j] = act.did(A.copy(M_[j], psum[b][:, :].rearrange("p (h n) -> p h n", h=4)))
                banks.free(b, m_ready[j])
            for lv in range(1, 7):
                for j in range(NT):
                    pool.need(c_free[j])
                    cm = pool.did(G.tensor_tensor(C_[j], diag(j), spread(level[:, lv, :], 1, 4), ALU.mult))
                    b = banks.take(pe)
                    pe.need(cm, m_ready[j], n_ready[j])
                    for hd in range(4):
                        mm = E.matmul(psum[b][:, hd * P:(hd + 1) * P], C_[j][:, hd, :], M_[j][:, hd, :], start=True, stop=True)
                    c_free[j] = done = pe.did(mm)
                    act.need(done, q_free[j])
                    q = act.did(A.copy(Q_[j], psum[b][:, :].rearrange("p (h n) -> p h n", h=4)))
                    banks.free(b, q)
                    bn = banks.take(pe)
                    pe.need(q)
                    for hd in range(4):
                        mm = E.matmul(psum[bn][:, hd * P:(hd + 1) * P], Q_[j][:, hd, :], N_[j][:, hd, :], start=True, stop=True)
                    dn = pe.did(mm)
                    if lv < 6:
                        bm = banks.take(pe)
                        for hd in range(4):
                            mm = E.matmul(psum[bm][:, hd * P:(hd + 1) * P], N_[j][:, hd, :], Q_[j][:, hd, :], start=True, stop=True)
                        dm = pe.did(mm)
                        dve.need(dm)
                        m_ready[j] = dve.did(V.tensor_tensor(M_[j], M_[j], psum[bm][:, :].rearrange("p (h n) -> p h n", h=4), ALU.subtract))
                        banks.free(bm, m_ready[j])
                        dn = dm
                    q_free[j] = dn
                    dve.need(dn)
                    n_ready[j] = dve.did(V.tensor_tensor(N_[j], N_[j], psum[bn][:, :].rearrange("p (h n) -> p h n", h=4), ALU.subtract))
                    banks.free(bn, n_ready[j])

            for hd in range(4):
                i = hd % 2
                b = banks.take(pe)
                pe.need(mx_ready)
                done = pe.did(E.matmul(psum[b][:, 0:SEQ], select[0:8, 4 + hd, :], mxT[0:8, :], start=True, stop=True))
                dve.need(done, dec_free[i])
                dve.did(V.tensor_scalar(dec[:, i, 0:SEQ], psum[b][:, 0:SEQ], ab[:, 0, 4 + hd:5 + hd], 0.0, ALU.subtract, ALU.max))
                m = dve.did(V.tensor_scalar(dec[:, i, SEQ:384], psum[b][:, P:SEQ], ab[:, 1, 4 + hd:5 + hd], 0.0, ALU.subtract, ALU.max))
                banks.free(b, m)
                act.need(m)
                m = act.did(A.activation(dec[:, i, :], dec[:, i, :], ACT.Exp, scale=-1.0))
                pool.need(m)
                e = dec_free[i] = pool.did(G.tensor_tensor(PT[:, hd, :], dec[:, i, :], const("causal3"), ALU.mult))
                b = banks.take(pe)
                done = key_query(b, qkb[:, 4 + hd, :], qkb[:, hd, :], qkb_ready)
                dve.need(done, e)
                m = dve.did(V.tensor_tensor(PT[:, hd, :], PT[:, hd, :], psum[b][:, 0:384], ALU.mult))
                banks.free(b, m)
                PT_ready.append(m)

            U = shaped(kbT.rearrange("p h n -> p (h n)"), NT, 512)
            Z = cut(512)
            b = banks.take(pe)
            pe.need(n_ready, v_ready)
            for hd in range(4):
                mm = E.matmul(psum[b][:, hd * P:(hd + 1) * P], N_[0][:, hd, :], vbeta[:, 0, hd * P:(hd + 1) * P], start=True, stop=True)
            done = pe.did(mm)
            u1 = copy_on(act, U[:, 0, :], psum[b][:, :], done)
            banks.free(b, u1)
            b = banks.take(pe)
            pe.need(u1)
            for hd in range(4):
                mm = E.matmul(psum[b][:, hd * P:(hd + 1) * P], LT[:, hd, P:SEQ], U[:, 0, hd * P:(hd + 1) * P], start=True, stop=True)
            done = pe.did(mm)
            dve.need(done)
            m = dve.did(V.tensor_tensor(Z, vbeta[:, 1, :], psum[b][:, :], ALU.subtract))
            banks.free(b, m)
            b = banks.take(pe)
            pe.need(m)
            for hd in range(4):
                mm = E.matmul(psum[b][:, hd * P:(hd + 1) * P], N_[1][:, hd, :], Z[:, hd * P:(hd + 1) * P], start=True, stop=True)
            done = pe.did(mm)
            u2 = copy_on(act, U[:, 1, :], psum[b][:, :], done)
            banks.free(b, u2)

            def weighted(W3, val, t, after):
                b = banks.take(pe)
                pe.need(after)
                for hd in range(4):
                    for s_ in range(t + 1):
                        k = t + s_
                        mm = E.matmul(psum[b][:, hd * P:(hd + 1) * P], W3[:, hd, k * P:(k + 1) * P],
                                      val[:, s_, hd * P:(hd + 1) * P], start=(s_ == 0), stop=(s_ == t))
                return b, pe.did(mm)

            mixed = y
            o_ready = []
            for t in range(NT):
                b, done = weighted(AT, U, t, [u1, u2, AT_ready])
                o_ready.append(evacuate(b, mixed[:, t, 0:512], psum[b][:, :], done))
            db = banks.take(pe)
            pe.need(PT_ready)
            for t in range(NT):
                for hd in range(4):
                    for s_ in range(t + 1):
                        k = t + s_
                        mm = E.matmul(psum[db][:, t * 4 + hd:t * 4 + hd + 1], PT[:, hd, k * P:(k + 1) * P], ones[:, 0:1],
                                      start=(s_ == 0), stop=(s_ == t))
            done = pe.did(mm)
            den, em = cut(NT, 4), cut(NT, 4)
            act.need(done)
            den_abs = act.did(A.activation(den, psum[db][:, 0:8].rearrange("p (t n) -> p t n", t=NT), ACT.Abs))
            banks.free(db, den_abs)
            dve.need(mcol_ready)
            m = dve.did(V.tensor_tensor(em, gc[:, :, 4:8], mcol[:, :, 4:8], ALU.add))
            act.need(m)
            m = act.did(A.activation(em, em, ACT.Exp, scale=-1.0))
            dve.need(m, den_abs)
            m = dve.did(V.tensor_tensor(den, den, em, ALU.max))
            dve.need(m)
            den_ready = dve.did(V.reciprocal(den, den))
            for t in range(NT):
                b, done = weighted(PT, vb, t, [PT_ready, lin_ready])
                dve.need(done, den_ready)
                m = dve.did(V.tensor_tensor(mixed[:, t, 512:D].rearrange("p (h d) -> p h d", h=4),
                                            psum[b][:, :].rearrange("p (h d) -> p h d", h=4),
                                            spread(den[:, t, :], 2, P), ALU.mult))
                banks.free(b, m)
                o_ready.append(m)
            sq2 = shaped(flat[:, 0:NT * D], NT, D)
            ss = cut(16)
            pool.need(o_ready)
            m = pool.did(G.tensor_tensor(sq2, mixed, mixed, ALU.mult))
            dve.need(m)
            m = dve.did(V.tensor_reduce(ss, sq2.rearrange("p t (h d) -> p (t h) d", h=8), AXX, ALU.add))
            dve.need(m)
            m = dve.did(V.tensor_scalar(ss, ss, 1.0 / P, EPS, ALU.mult, ALU.add))
            m = inv_root(ss, ss, ss, m)
            pool.need(lin_ready, rows_ready)
            g1 = pool.did(G.tensor_tensor(zs, zs, spread(row(0, "norm_a"), 1, NT), ALU.mult))
            g2 = pool.did(G.tensor_tensor(og, og, spread(row(0, "norm_b"), 1, NT), ALU.mult))
            dve.need(m, o_ready)
            m = dve.did(V.tensor_tensor(mixed.rearrange("p t (h d) -> p (t h) d", h=8), mixed.rearrange("p t (h d) -> p (t h) d", h=8),
                                        spread(ss, 2, P), ALU.mult))
            dve.need(m, g1, g2)
            e1 = dve.did(V.tensor_tensor(mixed[:, :, 0:512], mixed[:, :, 0:512], zs, ALU.mult))
            e2 = dve.did(V.tensor_tensor(mixed[:, :, 512:D], mixed[:, :, 512:D], og, ALU.mult))
            mm_ = feature_major(mixed, DC, top, [e1, e2])
            held, done = deep_linear(top, DC, T["w_out_ab"][0], mm_)
            return held, done, sq2, mixed

        def attention(groups, S, PTb, mx, den):
            state = [None] * len(groups)
            freeS, freeP, freeSt, freeQK, ready = [None, None], [None], [None, None], [None, None], {}

            def prepare(n):
                ready[n] = groups[n]["prepare"](n % 2, freeQK[n % 2])

            def tiles(g):
                return ((0, 0, P), (1, P, SEQ)) if g["causal"] else ((0, 0, SEQ), (1, SEQ, SEQ))

            def scores(n):
                g = groups[n]
                i = n % 2
                mk = g.get("mask")
                exps = []
                for t, c0, nk in tiles(g):
                    per = 512 // nk
                    for h0 in range(0, 4, per):
                        b = banks.take(pe)
                        pe.need(ready[n])
                        for j in range(per):
                            mm = E.matmul(psum[b][:, j * nk:(j + 1) * nk], g["q"](i, h0 + j)[:, t * P:(t + 1) * P],
                                          g["k"](i, h0 + j)[:, 0:nk], start=True, stop=True)
                        done = freeQK[i] = pe.did(mm)
                        bank = psum[b][:, :].rearrange("p (h n) -> p h n", h=per)
                        dve.need(done, freeS[i], freeSt[i])
                        s_ = S[:, i, h0:h0 + per, c0:c0 + nk]
                        if g.get("bias") is not None:
                            dve.need(g["bias_ready"])
                            m = dve.did(V.scalar_tensor_tensor(s_, bank, g["scale"], g["bias"][:, h0:h0 + per, c0:c0 + nk],
                                                               ALU.mult, ALU.subtract))
                        elif mk is None:
                            m = dve.did(V.tensor_scalar(s_, bank, g["scale"], None, ALU.mult))
                        else:
                            m = dve.did(V.scalar_tensor_tensor(s_, bank, g["scale"], spread(mk[:, c0:c0 + nk], 1, per),
                                                               ALU.mult, ALU.add))
                        banks.free(b, m)
                        dve.need(m)
                        mm_ = mx[:, i, t, h0:h0 + per]
                        m = dve.did(V.tensor_reduce(mm_, s_, AXX, ALU.max))
                        if g.get("sink") is not None:
                            dve.need(m)
                            m = dve.did(V.tensor_tensor(mm_, mm_, g["sink"][:, h0:h0 + per], ALU.max))
                        dve.need(m)
                        m = negated = dve.did(V.tensor_scalar(mm_, mm_, -1.0, None, ALU.mult))
                        act.need(m)
                        for j in range(per):
                            hh = h0 + j
                            exps.append(act.did(A.activation(S[:, i, hh, c0:c0 + nk], S[:, i, hh, c0:c0 + nk], ACT.Exp,
                                                             bias=mx[:, i, t, hh:hh + 1], accum_out=den[:, i, t, hh:hh + 1])))
                m = exps[-1]
                if g.get("sink") is not None:
                    sk = den[:, i, 2:4, :]
                    dve.need(negated)
                    m2 = dve.did(V.tensor_tensor(sk, mx[:, i, :, :], spread(g["sink"], 1, NT), ALU.add))
                    act.need(m2)
                    m2 = act.did(A.activation(sk, sk, ACT.Exp))
                    dve.need(m2, m)
                    m2 = dve.did(V.tensor_tensor(den[:, i, 0:2, :], den[:, i, 0:2, :], sk, ALU.add))
                    dve.need(m2)
                else:
                    dve.need(m)
                rd = dve.did(V.reciprocal(den[:, i, 0:2, :], den[:, i, 0:2, :]))
                state[n] = [m, rd]

            def turned(n):
                g = groups[n]
                i = n % 2
                marks = []
                n_blk = 3 if g["causal"] else 4
                for k in range(n_blk):
                    b, m = transposes([S[:, i, hh, k * P:(k + 1) * P] for hh in range(4)], [state[n][0]])
                    act.need(freeP[0])
                    dve.need(freeP[0])
                    marks.append(evacuate(b, PTb[:, k, :, :], psum[b][:, :].rearrange("p (h n) -> p h n", h=4), m))
                freeS[i] = m
                state[n].append(marks)

            def values(n):
                g = groups[n]
                i = n % 2
                b = banks.take(pe)
                pe.need(state[n][2], g["v_ready"])
                for t in range(NT):
                    blocks = ((0, 0),) if g["causal"] and t == 0 else ((1, 0), (2, 1)) if g["causal"] else ((2 * t, 0), (2 * t + 1, 1))
                    for hh in range(4):
                        for x, (k, s_) in enumerate(blocks):
                            mm = E.matmul(psum[b][:, (t * 4 + hh) * 64:(t * 4 + hh + 1) * 64], PTb[:, k, hh, :], g["v"](hh, s_),
                                          start=(x == 0), stop=(x == len(blocks) - 1))
                done = pe.did(mm)
                freeP[0] = done
                bank = psum[b][:, :].rearrange("p (t h d) -> p t h d", t=NT, h=4)
                dve.need(done, state[n][1])
                m = g["finish"](bank, den[:, i, 0:2, :])
                freeSt[i] = m
                banks.free(b, m)
            skewed([prepare, scores, turned, values], len(groups))

        def scaled_into(dst):
            def finish(bank, rden):
                for t in range(NT):
                    m = dve.did(V.tensor_tensor(dst[:, t, :].rearrange("p (h d) -> p h d", h=4), bank[:, t, :, :],
                                                spread(rden[:, t, :], 2, 64), ALU.mult))
                return m
            return finish

        def mixer_c(rows_ready):
            y, hT = cut(NT, D), cut(DC, SEQ)
            m = normed(h, y, [dve.last()])
            xm = feature_major(y, DC, hT, m, cols[:, COLS["pre1"] + 2 * DC:COLS["pre1"] + 3 * DC])
            proj = cut(NT, 1536)
            marks = []
            for n0 in range(0, 1536, 512):
                def evac(t, b, done, n0=n0):
                    dve.need(done, rows_ready)
                    m = dve.did(V.tensor_tensor(proj[:, t, n0:n0 + 512], psum[b][:, :], row(1, "b_qkv")[:, n0:n0 + 512], ALU.add))
                    banks.free(b, m)
                    marks.append(m)
                token_linear(hT, DC, T["w_qkv_c"][0], n0, 512, evac, xm)
            S = cut(2, 4, 512)
            PTb = cut(4, 4, P)
            tmp1, tmp2 = cut(1280), cut(1280)
            QK = cut(2, 5, SEQ)
            mx, den = cut(2, NT, 4), cut(2, 4, 4)
            for t in range(NT):
                x = proj[:, t, 0:1280].rearrange("p (n d) -> p n d", d=CHD)
                rm = rope(x, x, 20, ROT_C, 0, t, tmp1, tmp2, marks)
            mixed = y
            groups = []
            for kv in range(CKV):
                def prep(i, free, kv=kv):
                    act.need(free)
                    dve.need(free)
                    return heads_transposed(
                        lambda hh, t: proj[:, t, (kv * 4 + hh) * 64:(kv * 4 + hh + 1) * 64] if hh < 4 else
                        proj[:, t, 1024 + kv * 64:1024 + (kv + 1) * 64], 5, 64, QK[:, i, :, :], [rm])
                groups.append(dict(
                    prepare=prep, causal=True, scale=CHD ** -0.5, mask=const("window_neg"),
                    q=lambda i, hh: QK[0:64, i, hh, :], k=lambda i, hh: QK[0:64, i, 4, :],
                    v=lambda hh, s_, kv=kv: proj[:, s_, 1280 + kv * 64:1280 + (kv + 1) * 64], v_ready=marks,
                    sink=row(1, "sinks")[:, kv * 4:kv * 4 + 4], finish=scaled_into(mixed[:, :, kv * 256:(kv + 1) * 256])))
            attention(groups, S, PTb, mx, den)
            m = dve.last()
            mT = feature_major(mixed, DC, hT, [m])
            held, done = deep_linear(hT, DC, T["w_o_c"][0], mT)
            big = proj.rearrange("p t n -> p (t n)")
            return held, done, shaped(big[:, 0:NT * D], NT, D), mixed

        def head_norms(x, n, d, ss, gain, after):
            for t in range(NT):
                line = dve
                line.need(after)
                m = line.did(line.engine.tensor_tensor(x[:, t], x[:, t], spread(ss[:, t], 2, d), ALU.mult))
                line.need(m)
                g = gain.rearrange("p (n d) -> p n d", n=n)
                m = line.did(line.engine.tensor_tensor(x[:, t], x[:, t], g, ALU.mult))
            return m

        def mixer_2(l, rows_ready):
            layer = 2 + l
            R = lambda name: row(layer, name)
            both = cut(2 * MIX2 * NT)
            y = shaped(both[:, 0:NT * D], NT, D)
            hT = shaped(both[:, NT * D:2 * NT * D], DC, SEQ)
            hp = cut(NT, D_IN2)
            S = cut(2, 4, 512)
            PTb = cut(4, 4, P)
            sq = PTb.rearrange("p a b c -> p (a b c)")
            tmp1, tmp2 = S[:, 0, 0, :], S[:, 0, 1, :]
            kvm = cut(NT, 512)
            st = cut(NT, 48)
            st2 = cut(NT, 16)

            def sum_squares(x, n, d, dst, after):
                for t in range(NT):
                    pool.need(after, dve.last())
                    a = sq[:, t * 1024:t * 1024 + n * d]
                    m = pool.did(G.tensor_tensor(a, x[:, t, :], x[:, t, :], ALU.mult))
                    dve.need(m)
                    m = dve.did(V.tensor_reduce(dst[:, t, :], a.rearrange("p (n d) -> p n d", d=d), AXX, ALU.add))
                return m

            def roots(x, inv, after):
                dve.need(after)
                if isinstance(inv, float):
                    m = dve.did(V.tensor_scalar(x, x, inv, EPS, ALU.mult, ALU.add))
                else:
                    m = dve.did(V.tensor_tensor(x, x, inv, ALU.mult))
                    dve.need(m)
                    m = dve.did(V.tensor_scalar(x, x, EPS, None, ALU.add))
                return inv_root(x, x, x, m)

            sp.engine.dma_start(hT.rearrange("p k n -> p (k n)").rearrange("p (t d) -> p t d", t=NT),
                                T["mem_2"][0].rearrange("(t p) d -> p t d", p=P)).then_inc(s_in, 16)
            mem_ready = (s_in, 64 + 32 + 16 * (l + 1))
            mem = shaped(hT.rearrange("p k n -> p (k n)"), NT, D)
            m = normed(mem, y, [mem_ready])
            g0 = COLS["mem2"] + l * DC
            dve.need(m)
            xm = feature_major(y, DC, hT, m, cols[:, g0:g0 + DC])
            mk = []

            def evac_kv(t, b, done):
                mk.append(evacuate(b, kvm[:, t, :], psum[b][:, :], done))
            token_linear(hT, DC, T["mem_w_kv_2"][l], 0, 512, evac_kv, xm)
            m = sum_squares(kvm[:, :, 0:256], 4, 64, st2[:, :, 0:4], mk)
            m = roots(st2[:, :, 0:4], 1.0 / 64, m)
            kv4 = kvm[:, :, 0:256].rearrange("p t (n d) -> p t n d", n=4)
            memk_ready = head_norms(kv4, 4, 64, st2[:, :, 0:4], R("memk"), [m, rows_ready])

            pe_mem = pe.last()
            act.need(pe_mem)
            m = normed(h, y, [pe_mem, dve.last()])
            g0 = COLS["attn2"] + l * DC
            xm = feature_major(y, DC, hT, [m, pe_mem], cols[:, g0:g0 + DC])
            pj = []
            for n0 in range(0, D_IN2, 512):
                nn = min(512, D_IN2 - n0)

                def evac(t, b, done, n0=n0, nn=nn):
                    pj.append(evacuate(b, hp[:, t, n0:n0 + nn], psum[b][:, 0:nn], done))
                token_linear(hT, DC, T["w_in_2"][l], n0, nn, evac, xm)
            slot = 0
            for c0, n, d in ((C_CQ, 1, 192), (C_CKV, 1, 128), (C_KR, 1, 32), (C_FOX, 8, 64), (C_MOBA, 8, 64),
                             (C_DIFF, 16, 32), (C_MEM, 4, 64)):
                m = sum_squares(hp[:, :, c0:c0 + n * d], n, d, st[:, :, slot:slot + n], pj)
                slot += n
            m = roots(st[:, :, 0:N_SLOT], spread(const("inv_d")[:, 0:N_SLOT], 1, NT), m)
            slot = 0
            for c0, n, d, name in ((C_CQ, 1, 192, "cq"), (C_CKV, 1, 128, "ckv"), (C_KR, 1, 32, "kr"), (C_FOX, 8, 64, "fox"),
                                   (C_MOBA, 8, 64, "moba"), (C_DIFF, 16, 32, "diff"), (C_MEM, 4, 64, "memq")):
                x = hp[:, :, c0:c0 + n * d].rearrange("p t (n d) -> p t n d", n=n)
                nm = head_norms(x, n, d, st[:, :, slot:slot + n], R(name), [m, rows_ready])
                slot += n

            cT = cut(3, SEQ)
            qa, kva, ka = cut(NT, 384), cut(NT, 512), cut(NT, 384)
            marks = []
            for k, (c0, w) in enumerate(((0, P), (P, 64), (C_CKV, P))):
                b, mt = transposes([hp[:, t, c0:c0 + w] for t in range(NT)], [nm])
                marks.append(evacuate(b, cT[0:w, k, :], psum[b][0:w, 0:SEQ], mt))
            uq, ukv = T["mla_w_uq_2"][l], T["mla_w_ukv_2"][l]
            s, wm = slots.load([(P, 0, (384,), uq[0:P, :]), (64, 384, (384,), uq[P:192, :]), (P, 768, (512,), ukv)])
            w3 = slots.view(s, 1, SLOT)[:, 0, :]
            am = []
            for t in range(NT):
                b = banks.take(pe)
                pe.need(wm, marks)
                E.matmul(psum[b][:, 0:384], cT[:, 0, t * P:(t + 1) * P], w3[:, 0:384], start=True, stop=False)
                done = pe.did(E.matmul(psum[b][:, 0:384], cT[0:64, 1, t * P:(t + 1) * P], w3[0:64, 384:768], start=False, stop=True))
                am.append(evacuate(b, qa[:, t, :], psum[b][:, 0:384], done))
                b = banks.take(pe)
                done = pe.did(E.matmul(psum[b][:, :], cT[:, 2, t * P:(t + 1) * P], w3[:, 768:1280], start=True, stop=True))
                am.append(evacuate(b, kva[:, t, :], psum[b][:, :], done))
            slots.free(s, done)
            qa4 = qa.rearrange("p t (n d) -> p t n d", n=4)
            kv4a = kva.rearrange("p t (n d) -> p t n d", n=4)
            ka4 = ka.rearrange("p t (n d) -> p t n d", n=4)
            for t in range(NT):
                pool.need(am, dve.last())
                m1 = pool.did(G.tensor_tensor(sq[:, t * 1024:t * 1024 + 384], qa[:, t, :], qa[:, t, :], ALU.mult))
                m2 = pool.did(G.tensor_tensor(sq[:, t * 1024 + 384:t * 1024 + 896], kva[:, t, :], kva[:, t, :], ALU.mult))
                dve.need(m1, m2)
                q3 = sq[:, t * 1024:t * 1024 + 384].rearrange("p (n d) -> p n d", n=4)
                k3 = sq[:, t * 1024 + 384:t * 1024 + 896].rearrange("p (n d) -> p n d", n=4)
                dve.did(V.tensor_reduce(st2[:, t, 0:4], q3[:, :, 0:32], AXX, ALU.add))
                dve.did(V.tensor_reduce(st2[:, t, 4:8], q3[:, :, 32:96], AXX, ALU.add))
                m = dve.did(V.tensor_reduce(st2[:, t, 8:12], k3[:, :, 0:64], AXX, ALU.add))
            dve.need(m)
            dve.did(V.tensor_scalar(st2[:, :, 0:4], st2[:, :, 0:4], 1.0 / 32, EPS, ALU.mult, ALU.add))
            m = dve.did(V.tensor_scalar(st2[:, :, 4:12], st2[:, :, 4:12], 1.0 / 64, EPS, ALU.mult, ALU.add))
            m = inv_root(st2[:, :, 0:12], st2[:, :, 0:12], st2[:, :, 0:12], m)
            gq = R("mla_q").rearrange("p (n d) -> p n d", n=4)
            gk = R("mla_k").rearrange("p (n d) -> p n d", n=4)
            for t in range(NT):
                dve.need(m)
                dve.did(V.tensor_tensor(qa4[:, t, :, 0:32], qa4[:, t, :, 0:32], spread(st2[:, t, 0:4], 2, 32), ALU.mult))
                dve.did(V.tensor_tensor(qa4[:, t, :, 32:96], qa4[:, t, :, 32:96], spread(st2[:, t, 4:8], 2, 64), ALU.mult))
                e = dve.did(V.tensor_tensor(ka4[:, t, :, 32:96], kv4a[:, t, :, 0:64], spread(st2[:, t, 8:12], 2, 64), ALU.mult))
                dve.need(e)
                dve.did(V.tensor_tensor(qa4[:, t], qa4[:, t], gq, ALU.mult))
                e = dve.did(V.tensor_tensor(ka4[:, t, :, 32:96], ka4[:, t, :, 32:96], gk, ALU.mult))
                rope(qa4[:, t, :, 0:32], qa4[:, t, :, 0:32], 4, ROT_A, ROT_C, t, tmp1, tmp2, e)
                kr = hp[:, t, C_KR:C_KR + 32].rearrange("p (n d) -> p n d", n=1)
                e = rope(kr, kr, 1, ROT_A, ROT_C, t, tmp1, tmp2, nm)
                dve.need(e)
                e = dve.did(V.tensor_copy(ka4[:, t, :, 0:32], spread(hp[:, t, C_KR:C_KR + 32], 1, 4)))
                mo = hp[:, t, C_MOBA:C_MOBA + 512].rearrange("p (n d) -> p n d", n=8)[:, :, 0:2 * ROT_M]
                rope(mo, mo, 8, ROT_M, ROT_C + ROT_A, t, tmp1, tmp2, nm)
                di = hp[:, t, C_DIFF:C_DIFF + 512].rearrange("p (n d) -> p n d", n=16)[:, :, 0:2 * ROT_D]
                qk_ready = rope(di, di, 16, ROT_D, ROT_C + ROT_A + ROT_M, t, tmp1, tmp2, nm)

            fx = cut(NT, 4)
            lf = cut(NT, 4)
            dve.need(pj, rows_ready)
            m = dve.did(V.tensor_tensor(fx, hp[:, :, C_FF:C_FF + 4], spread(R("fox_b"), 1, NT), ALU.add))
            dve.need(m)
            m = dve.did(V.scalar_tensor_tensor(lf, fx, -1.0, fx, ALU.mult, ALU.max))
            act.need(m)
            m = act.did(A.activation(lf, lf, ACT.Exp, scale=-1.0))
            act.need(m)
            m = act.did(A.activation(lf, lf, ACT.Ln, bias=1.0))
            dve.need(m)
            m = dve.did(V.scalar_tensor_tensor(lf, fx, 0.0, lf, ALU.min, ALU.subtract))
            tri = const("causal3")
            b = banks.take(pe)
            pe.need(m)
            for t in range(NT):
                for s_ in range(t + 1):
                    mm = E.matmul(psum[b][:, t * 4:t * 4 + 4], tri[:, (t + s_) * P:(t + s_ + 1) * P], lf[:, s_, :],
                                  start=(s_ == 0), stop=(s_ == t))
            done = pe.did(mm)
            fc = cut(NT, 4)
            dve.need(done)
            fc_ready = dve.did(V.tensor_copy(fc, psum[b][:, 0:8].rearrange("p (t n) -> p t n", t=NT)))
            banks.free(b, fc_ready)
            X = cut(4, 384)
            gb = cut(4, NT, P)
            m = dve.did(V.tensor_copy(gb, spread(lf.rearrange("p t h -> p h t"), 3, P)))
            for hh in range(4):
                b = banks.take(pe)
                pe.need(m)
                E.matmul(psum[b][:, 0:SEQ], gb[:, hh, 0, :], tri[:, 0:SEQ], start=True, stop=False)
                done = pe.did(E.matmul(psum[b][:, P:SEQ], gb[:, hh, 1, :], tri[:, SEQ:384], start=False, stop=True))
                dve.need(done, fc_ready)
                cn = const("causal_neg")
                dve.did(V.scalar_tensor_tensor(X[:, hh, 0:P], psum[b][:, 0:P], fc[:, 0, hh:hh + 1], cn[:, 0:P], ALU.subtract, ALU.subtract))
                X_ready = dve.did(V.scalar_tensor_tensor(X[:, hh, P:384], psum[b][:, 0:SEQ], fc[:, 1, hh:hh + 1], cn[:, P:384],
                                                         ALU.subtract, ALU.subtract))
                banks.free(b, X_ready)
            lam_init = 0.8 - 0.6 * float(np.exp(-0.3 * l))
            lm = cut(68)
            lv = R("lambda").rearrange("p (a d) -> p a d", a=4)
            lm3 = lm[:, 0:64].rearrange("p (a d) -> p a d", a=2)
            m = dve.did(V.tensor_tensor(lm3, lv[:, 0::2, :], lv[:, 1::2, :], ALU.mult))
            dve.need(m)
            m = dve.did(V.tensor_reduce(lm[:, 64:66], lm3, AXX, ALU.add))
            act.need(m)
            m = act.did(A.activation(lm[:, 64:66], lm[:, 64:66], ACT.Exp))
            dve.need(m)
            m = dve.did(V.tensor_tensor(lm[:, 66:67], lm[:, 64:65], lm[:, 65:66], ALU.subtract))
            dve.need(m)
            lam_ready = dve.did(V.tensor_scalar(lm[:, 66:67], lm[:, 66:67], lam_init, -1.0, ALU.add, ALU.mult))

            QK = cut(2, 8, SEQ)
            mx, den = cut(2, NT, 4), cut(2, 4, 4)
            both_d = gb.rearrange("p h t n -> p (h t n)")
            d1, d2 = [shaped(both_d[:, k * 512:(k + 1) * 512], NT, 256) for k in range(2)]
            mixed = shaped(both[:, 0:NT * MIX2], NT, MIX2)
            mT = shaped(both[:, NT * MIX2:2 * NT * MIX2], MIX2 // P, SEQ)

            def group(src, d, scale, v, v_ready, finish, **more):
                def prep(i, free):
                    act.need(free)
                    dve.need(free)
                    return heads_transposed(src, 8, d, QK[:, i, :, :], [qk_ready, memk_ready])
                return dict(prepare=prep, scale=scale, v=v, v_ready=v_ready, finish=finish,
                            q=lambda i, hh: QK[0:d, i, hh, :], k=lambda i, hh: QK[0:d, i, 4 + hh, :], **more)

            def hp_v(c0):
                return lambda hh, s_: hp[:, s_, c0 + hh * 64:c0 + (hh + 1) * 64]

            def finish_diff(bank, rden):
                m = scaled_into(d2)(bank, rden)
                dve.need(m, lam_ready)
                m = dve.did(V.scalar_tensor_tensor(d1, d2, lm[:, 66:67], d1, ALU.mult, ALU.add))
                dve.need(m)
                m = dve.did(V.tensor_tensor(d2, d1, d1, ALU.mult))
                dve.need(m)
                m = dve.did(V.tensor_reduce(st2[:, :, 0:4], d2.rearrange("p t (n d) -> p t n d", n=4), AXX, ALU.add))
                m = roots(st2[:, :, 0:4], 1.0 / 64, m)
                dve.need(m)
                for t in range(NT):
                    m = dve.did(V.tensor_tensor(d1[:, t, :].rearrange("p (n d) -> p n d", n=4), d1[:, t, :].rearrange("p (n d) -> p n d", n=4),
                                                spread(st2[:, t, 0:4], 2, 64), ALU.mult))
                dve.need(m)
                return dve.did(V.scalar_tensor_tensor(mixed[:, :, 768:1024], d1, 1.0 - lam_init, spread(R("sub"), 1, NT),
                                                      ALU.mult, ALU.mult))

            cneg = const("causal_neg")
            groups = [
                group(lambda x, t: hp[:, t, C_FOX + x * 64:C_FOX + (x + 1) * 64], 64, 64 ** -0.5, hp_v(C_FOX + 512), pj,
                      scaled_into(mixed[:, :, 256:512]), causal=True, bias=X, bias_ready=X_ready),
                group(lambda x, t: hp[:, t, C_MOBA + x * 64:C_MOBA + (x + 1) * 64], 64, 64 ** -0.5, hp_v(C_MOBA + 512), pj,
                      scaled_into(mixed[:, :, 512:768]), causal=True, mask=cneg),
                group(lambda x, t: (qa4 if x < 4 else ka4)[:, t, x % 4, :], 96, 96 ** -0.5,
                      lambda hh, s_: kva[:, s_, hh * P + 64:(hh + 1) * P], am, scaled_into(mixed[:, :, 0:256]), causal=True, mask=cneg),
            ]
            for pair in range(2):
                groups.append(group(lambda x, t, pair=pair: hp[:, t, C_DIFF + (2 * x + pair) * 32:C_DIFF + (2 * x + pair + 1) * 32],
                                    32, 32 ** -0.5, hp_v(C_DIFF + 512), pj, finish_diff if pair else scaled_into(d1),
                                    causal=True, mask=cneg))
            groups.append(group(lambda x, t: hp[:, t, C_MEM + x * 64:C_MEM + (x + 1) * 64] if x < 4 else
                                kvm[:, t, (x - 4) * 64:(x - 3) * 64], 64, 64 ** -0.5,
                                lambda hh, s_: kvm[:, s_, 256 + hh * 64:256 + (hh + 1) * 64], mk,
                                scaled_into(mixed[:, :, 1024:1280]), causal=False))
            attention(groups, S, PTb, mx, den)
            m = dve.last()
            m = feature_major(mixed, MIX2 // P, mT, [m])
            held, done = deep_linear(mT, MIX2 // P, T["w_o_2"][l], m)
            for i, b in enumerate(held):
                v = h[:, i // 2, (i % 2) * 512:(i % 2 + 1) * 512]
                dve.need(done)
                m = dve.did(V.tensor_tensor(v, v, psum[b][:, :], ALU.add))
                banks.free(b, m)

        def feed_forward_2(l):
            y, hT = cut(NT, D), cut(DC, SEQ)
            aT = cut(DFF2 // P, SEQ)
            pad = cut(3, 2, SEQ + 2)
            cv = cut(3, 2, SEQ)
            m = normed(h, y, [dve.last()])
            g0 = COLS["ffn2"] + l * DC
            xm = feature_major(y, DC, hT, m, cols[:, g0:g0 + DC])
            zeroed = pool.did(G.memset(pad[:, :, :, 0:2], 0.0))
            pad_free, cv_free = [zeroed] * 3, [None] * 3
            cw, cb = COLS["fconv_w"] + l * 66, COLS["fconv_b"] + l * 22
            turn, ready = [0], []
            wg, wu = T["ffn_w_gate_2"][l], T["ffn_w_up_2"][l]
            for n0 in range(0, DFF2, 512):
                nn = min(512, DFF2 - n0)
                sg, vg, mg = panel(wg, 0, DC, n0, nn)
                su, vu, mu = panel(wu, 0, DC, n0, nn)
                for c in range(0, nn // P, 2):
                    silu = {}

                    def evac_gate(c_, w_, b, done, n0=n0, c=c):
                        i = turn[0] % 3
                        turn[0] += 1
                        act.need(done, pad_free[i])
                        m = act.did(A.copy(pad[:, i, :, 2:], psum[b][:, :].rearrange("p (k n) -> p k n", k=2)))
                        banks.free(b, m)
                        ends = [None, None]
                        for j in range(2):
                            ch = n0 // P + c + j
                            dve.need(m, cv_free[i])
                            ends[j] = dve.did(V.tensor_scalar(cv[:, i, j, :], pad[:, i, j, 0:SEQ], cols[:, cw + ch:cw + ch + 1],
                                                              cols[:, cb + ch:cb + ch + 1], ALU.mult, ALU.add))
                        for k in range(1, 3):
                            for j in range(2):
                                ch = n0 // P + c + j
                                dve.need(ends[j])
                                ends[j] = dve.did(V.scalar_tensor_tensor(cv[:, i, j, :], pad[:, i, j, k:k + SEQ],
                                                                         cols[:, cw + k * 22 + ch:cw + k * 22 + ch + 1],
                                                                         cv[:, i, j, :], ALU.mult, ALU.add))
                        pad_free[i] = ends[1]
                        act.need(ends)
                        silu["i"], silu["m"] = i, act.did(A.activation(cv[:, i, :, :], cv[:, i, :, :], ACT.Silu))

                    def evac_up(c_, w_, b, done, n0=n0, c=c):
                        i = silu["i"]
                        dve.need(done, silu["m"])
                        ch = n0 // P + c
                        m = dve.did(V.tensor_tensor(aT[:, ch:ch + 2, :], cv[:, i, :, :],
                                                    psum[b][:, :].rearrange("p (k n) -> p k n", k=2), ALU.mult))
                        banks.free(b, m)
                        cv_free[i] = m
                        ready.append(m)
                    feature_chunks(hT, vg[:, :, c * P:(c + 2) * P], mg, 2, evac_gate, xm)
                    done = feature_chunks(hT, vu[:, :, c * P:(c + 2) * P], mu, 2, evac_up, xm)
                slots.free(sg, done)
                slots.free(su, done)
            held, done = deep_linear(aT, DFF2 // P, T["ffn_w_down_2"][l], ready)
            for i, b in enumerate(held):
                v = h[:, i // 2, (i % 2) * 512:(i % 2 + 1) * 512]
                dve.need(done)
                m = dve.did(V.tensor_tensor(v, v, psum[b][:, :], ALU.add))
                banks.free(b, m)

        loaded_all = [loaded]
        for layer in range(2):
            rows_ready = load_rows(layer)
            held, done, mix, tmp = (mixer_ab if layer == 0 else mixer_c)(rows_ready)
            add_normed(held, done, row(layer, "post"), mix, tmp, row(1, "b_o") if layer else None, rows_ready)
            join()
            feed_forward_1(layer, rows_ready)
            join()
            gated_add(layer)
            join()
        for l in range(2):
            rows_ready = load_rows(2 + l)
            mixer_2(l, rows_ready)
            join()
            feed_forward_2(l)
            join()
        sp.need(dve.last())
        sp.engine.dma_start(out[0].rearrange("(t p) d -> p t d", p=P), h[:, :, :]).then_inc(s_out, 16)
        sp.engine.wait_ge(s_out, 16)


WEIGHTS = ["x", "p", "w_in_ab", "w_out_ab", "w_qkv_c", "w_o_c", "w_up", "w_down", "w_ple", "w_ple_gate", "mem_2",
           "w_in_2", "mla_w_uq_2", "mla_w_ukv_2", "mem_w_kv_2", "w_o_2", "ffn_w_gate_2", "ffn_w_up_2", "ffn_w_down_2"]


def columns(v):
    return np.ascontiguousarray(v.reshape(-1, P).T)


def kernel(**inputs):
    import concourse.bacc as bacc
    from concourse.bass_utils import run_bass_kernel_spmd

    inputs = {k: np.asarray(v) for k, v in inputs.items()}
    f = np.float32
    cols = [columns(inputs["norm_gains"][layer, which]) for layer in range(2) for which in (0, 2)]
    cols += [columns(inputs[name][l]) for name in ("attn_norm_2", "ffn_norm_2", "mem_norm_2") for l in range(2)]
    cols.append(inputs["conv_a"][0].reshape(4, 12, P).transpose(2, 1, 0).reshape(P, 48))
    cols += [inputs["ffn_conv_w_2"][l].reshape(3, 22, P).transpose(2, 0, 1).reshape(P, 66) for l in range(2)]
    cols += [columns(inputs["ffn_conv_b_2"][l]) for l in range(2)]
    zeros4 = np.zeros(4, f)
    rows = np.zeros((4, ROW_MAX), f)

    def put(layer, name, *values):
        a, n = ROWS[layer][name]
        rows[layer, a:a + n] = np.concatenate([v.reshape(-1) for v in values])

    for layer in range(2):
        put(layer, "post", inputs["norm_gains"][layer, 1])
        put(layer, "post_ff", inputs["norm_gains"][layer, 3])
    put(0, "norm_a", *[inputs["norm_a"][0]] * 4)
    put(0, "norm_b", inputs["norm_b"][0])
    put(0, "gate_bias", zeros4, inputs["dt_bias"][0], inputs["i_bias_b"][0], inputs["f_bias_b"][0])
    put(0, "a_log", inputs["a_log"][0])
    put(1, "b_qkv", inputs["b_qkv_c"][0])
    put(1, "b_o", inputs["b_o_c"][0])
    put(1, "sinks", inputs["sinks_c"][0])
    for l in range(2):
        i = {k: inputs[k + "_2"][l] for k in ("mla_cq_norm", "mla_ckv_norm", "mla_q_norm", "mla_k_norm", "fox_q_norm",
                                              "fox_k_norm", "moba_q_norm", "moba_k_norm", "diff_q_norm", "diff_k_norm",
                                              "diff_sub_norm", "mem_q_norm", "mem_k_norm", "fox_b_f", "diff_lambda")}
        put(2 + l, "cq", i["mla_cq_norm"])
        put(2 + l, "ckv", i["mla_ckv_norm"])
        put(2 + l, "kr", i["mla_k_norm"][:32])
        put(2 + l, "fox", *[i["fox_q_norm"]] * 4, *[i["fox_k_norm"]] * 4)
        put(2 + l, "moba", *[i["moba_q_norm"]] * 4, *[i["moba_k_norm"]] * 4)
        put(2 + l, "diff", *[i["diff_q_norm"]] * 8, *[i["diff_k_norm"]] * 8)
        put(2 + l, "memq", *[i["mem_q_norm"]] * 4)
        put(2 + l, "memk", *[i["mem_k_norm"]] * 4)
        put(2 + l, "mla_q", *[i["mla_q_norm"]] * 4)
        put(2 + l, "mla_k", *[i["mla_k_norm"][32:]] * 4)
        put(2 + l, "sub", *[i["diff_sub_norm"]] * 4)
        put(2 + l, "fox_b", i["fox_b_f"])
        put(2 + l, "lambda", i["diff_lambda"])
    arrays = {name: np.ascontiguousarray(inputs[name]) for name in WEIGHTS}
    arrays["cols"] = np.ascontiguousarray(np.concatenate(cols, 1))
    arrays["rows"] = rows
    arrays["consts"] = constants()
    arrays["positions"] = np.ascontiguousarray(np.concatenate(
        [inputs[n].reshape(NT, P).T for n in ("positions", "positions_2")], 1))

    nc = bacc.Bacc("TRN2", target_bir_lowering=False, num_devices=1)
    arrays = {f"in_{k}": v for k, v in arrays.items()}
    T = {k[3:]: nc.dram_tensor(k, v.shape, bass.mybir.dt.from_np(v.dtype), kind="ExternalInput").ap() for k, v in arrays.items()}
    out = nc.dram_tensor("out_0_dram", (1, SEQ, D), F32, kind="ExternalOutput").ap()
    program(nc, T, out)
    result = run_bass_kernel_spmd(nc, [arrays], core_ids=[0])
    return result.results[0]["out_0_dram"]
```

```python
from contextlib import ExitStack

import numpy as np

import concourse.bass as bass
import concourse.mybir as mybir

F32 = mybir.dt.float32
I32 = mybir.dt.int32
F32R = mybir.dt.float32r
ACT = mybir.ActivationFunctionType
ALU = mybir.AluOpType
AXX = mybir.AxisListType.X

P = 128
SEQ = 256
NT = SEQ // P
D = 1024
DC = D // P
EPS = 1e-6
BIG = 1e30
TWO_PI = 2 * np.pi

HA = 4
QKV_A = 1536
W_IN = 4112
COL_BETA = QKV_A
COL_Z = QKV_A + 8
COL_QB = COL_Z + 512
COL_VB = COL_QB + 1024
COL_IF = COL_VB + 512
COL_O = COL_IF + 8
CH, CKV, CHD = 16, 4, 64
DFF1 = 4096
DFF2 = 2816
MIX2 = 1280
ROT_C, ROT_A, ROT_M, ROT_D = 32, 16, 8, 4
D_IN2 = 2916
C_CQ, C_CKV, C_KR, C_FOX, C_FF, C_MOBA, C_DIFF, C_MEM = 0, 192, 320, 352, 1120, 1124, 1892, 2660

COLS = {}
_at = 0
for _name, _n in (("pre1", 2 * 2 * DC), ("attn2", 2 * DC), ("ffn2", 2 * DC), ("mem2", 2 * DC),
                  ("conv_a", 12 * 4), ("fconv_w", 2 * 3 * 22), ("fconv_b", 2 * 22)):
    COLS[_name] = _at
    _at += _n
N_COLS = _at

ROWS = [dict(), dict(), dict(), dict()]
_parts = [
    (("post", D), ("post_ff", D), ("norm_a", 512), ("norm_b", 512), ("gate_bias", 16), ("a_log", 4)),
    (("post", D), ("post_ff", D), ("b_qkv", 1536), ("b_o", D), ("sinks", CH)),
    (("cq", 192), ("ckv", 128), ("kr", 32), ("fox", 512), ("moba", 512), ("diff", 512), ("memq", 256),
     ("memk", 256), ("mla_q", 384), ("mla_k", 256), ("sub", 256), ("fox_b", 4), ("lambda", 128)),
]
_parts.append(_parts[2])
ROW_LEN = []
for _l, _p in enumerate(_parts):
    _at = 0
    for _name, _n in _p:
        ROWS[_l][_name] = (_at, _n)
        _at += _n
    ROW_LEN.append(_at)
ROW_MAX = max(ROW_LEN)

CONST = {}
_at = 0
for _name, _n in (("ident", P), ("causal3", 384), ("causal_neg", 384), ("window_neg", 384),
                  ("level", 7 * P), ("select", 8 * P), ("freq", 60), ("sign8", 8),
                  ("inv_d", 48)):
    CONST[_name] = (_at, _n)
    _at += _n
N_CONST = _at
SLOT_D = [192, 128, 32] + [64] * 8 + [64] * 8 + [32] * 16 + [64] * 4
N_SLOT = len(SLOT_D)


def constants():
    c = np.zeros((P, N_CONST), np.float32)

    def put(name, value):
        a, n = CONST[name]
        c[:, a:a + n] = np.asarray(value, np.float32).reshape(value.shape[0], -1)

    i = np.arange(P)
    upper = (i[:, None] <= i[None, :]).astype(np.float32)
    one, zero = np.ones((P, P), np.float32), np.zeros((P, P), np.float32)
    put("ident", np.eye(P, dtype=np.float32))
    put("causal3", np.concatenate([upper, one, upper], 1))
    lower_neg = np.where(i[None, :] <= i[:, None], 0.0, -BIG)
    prev_neg = np.where(i[None, :] > i[:, None], 0.0, -BIG)
    put("causal_neg", np.concatenate([lower_neg, zero, lower_neg], 1))
    put("window_neg", np.concatenate([lower_neg, prev_neg, lower_neg], 1))
    levels = []
    for n in range(7):
        s = 1 << n
        e, k = i[:, None], i[None, :]
        levels.append(((e // (2 * s) == k // (2 * s)) & (e % (2 * s) < s) & (k % (2 * s) >= s)))
    put("level", np.concatenate(levels, 1))
    sel = np.zeros((P, 8, P))
    for h in range(8):
        sel[h, h] = 1
    put("select", sel)
    f32 = np.float32
    freq = [f32(theta) ** (-np.arange(0, r, dtype=f32) / f32(r)) for theta, r in
            ((10000.0, ROT_C), (500000.0, ROT_A), (500000.0, ROT_M), (500000.0, ROT_D))]
    put("freq", np.tile(np.concatenate(freq)[None], (P, 1)))
    put("sign8", np.tile(np.array([1.0] * 4 + [-1.0] * 4)[None], (P, 1)))
    inv = np.zeros(48)
    inv[:N_SLOT] = 1.0 / np.array(SLOT_D)
    put("inv_d", np.tile(inv[None], (P, 1)))
    return c


class Line:

    def __init__(self, engine, sem):
        self.engine, self.sem, self.count, self.waited = engine, sem, 0, {}

    def need(self, *marks):
        for m in marks:
            if m is None:
                continue
            if isinstance(m, list):
                self.need(*m)
                continue
            sem, value = m
            if self.waited.get(id(sem), 0) < value:
                self.engine.wait_ge(sem, value)
                self.waited[id(sem)] = value
        return self.engine

    def did(self, instruction):
        instruction.then_inc(self.sem, 1)
        self.count += 1
        return self.sem, self.count

    def last(self):
        return (self.sem, self.count) if self.count else None


class Banks:

    def __init__(self, banks):
        self.banks, self.free_at, self.turn, self.held = banks, [None] * len(banks), 0, [False] * len(banks)

    def take(self, pe):
        b = self.turn
        self.turn = (b + 1) % len(self.banks)
        assert not self.held[b]
        self.held[b] = True
        pe.need(self.free_at[b])
        return b

    def free(self, b, *marks):
        assert self.held[b]
        self.held[b], self.free_at[b] = False, list(marks)


class Weights:

    def __init__(self, sp, act, dve, plan, raw, high, low, width, sems):
        self.sp, self.act, self.dve, self.plan = sp, act, dve, plan
        self.raw, self.high, self.low, self.width, self.sems = raw, high, low, width, sems
        self.n_raw, self.n_half = raw.shape[1] // width, high.shape[1] // width
        self.landed = [0] * self.n_raw
        self.raw_free, self.half_free = {}, {}
        self.arrived, self.split_mark = {}, {}
        self.number, n = [], 0
        for p in plan:
            self.number.append(n)
            n += p["split"]
        self.next_load = self.next_split = self.next_take = 0

    def slot(self, tensor, s, n):
        return tensor[:, s * self.width:s * self.width + n]

    def ahead(self):
        moved = True
        while moved:
            moved = False
            j = self.next_load
            if j < len(self.plan) and (j < self.n_raw or j - self.n_raw in self.raw_free):
                s = j % self.n_raw
                self.sp.need(self.raw_free.get(j - self.n_raw))
                p = self.plan[j]
                for dst, src in p["pieces"](self.slot(self.raw, s, p["size"])):
                    self.sp.engine.dma_start(dst, src).then_inc(self.sems[s], 16)
                    self.landed[s] += 16
                self.arrived[j] = (self.sems[s], self.landed[s])
                self.next_load += 1
                moved = True
            j = self.next_split
            if j < self.next_load:
                p, n = self.plan[j], self.number[j]
                if not p["split"]:
                    self.next_split += 1
                    moved = True
                elif n < self.n_half or n - self.n_half in self.half_free:
                    raw = self.slot(self.raw, j % self.n_raw, p["size"])
                    high, low = [self.slot(x, n % self.n_half, p["size"]) for x in (self.high, self.low)]
                    free = self.half_free.get(n - self.n_half)
                    self.act.need(self.arrived[j], free)
                    m = self.act.did(self.act.engine.copy(high, raw))
                    self.dve.need(m, self.arrived[j], free)
                    m = self.dve.did(self.dve.engine.tensor_tensor(low, raw, high.bitcast(F32), ALU.subtract))
                    self.raw_free[j] = self.split_mark[j] = m
                    self.next_split += 1
                    moved = True

    def take(self, key):
        j = self.next_take
        p = self.plan[j]
        assert p["key"] == key, (p["key"], key)
        self.next_take += 1
        self.ahead()
        shape = dict(k=p["kc"])
        if not p["split"]:
            return (self.slot(self.raw, j % self.n_raw, p["size"]),), self.arrived[j]
        s = self.number[j] % self.n_half
        return tuple(self.slot(x, s, p["size"]).rearrange("p (k n) -> p k n", **shape)
                     for x in (self.high, self.low)), self.split_mark[j]

    def done(self, mark):
        j = self.next_take - 1
        if self.plan[j]["split"]:
            self.half_free[self.number[j]] = mark
        else:
            self.raw_free[j] = mark


def panel(key, w, k0, kc, n0, nn):
    def pieces(slot):
        return [(slot.rearrange("p (k n) -> p k n", k=kc),
                 w[k0 * P:(k0 + kc) * P, n0:n0 + nn].rearrange("(k p) n -> p k n", p=P))]
    return dict(key=(key, k0, n0), pieces=pieces, kc=kc, size=kc * nn, split=True)


def by_features(key, w, n0, n1):
    return [panel(key, w, 0, DC, n, 256) for n in range(n0, n1, 256)]


def by_tokens(key, w, n0, n1):
    return [panel(key, w, k, 4, n, min(512, n1 - n)) for n in range(n0, n1, 512) for k in (0, 4)]


def deep(key, w, kc):
    return [panel(key, w, k, 2, 0, D) for k in range(0, kc, 2)]


def weight_plan(T):
    w = T["w_in_ab"][0]

    def gate_pieces(slot):
        v = slot.rearrange("p (k n) -> p k n", k=DC)
        return [(v[:, :, i * 8:i * 8 + 8], w[:, c:c + 8].rearrange("(k p) n -> p k n", p=P))
                for i, c in enumerate((COL_BETA, COL_IF))]
    plan = [dict(key="gates", pieces=gate_pieces, kc=DC, size=DC * 16, split=True)]
    plan += by_features("qkv_a", w, 0, QKV_A) + by_features("qk_b", w, COL_QB, COL_VB)
    for c in (COL_Z, COL_VB, COL_O):
        plan += by_tokens("zvo", w, c, c + 512)
    plan += deep("out_ab", T["w_out_ab"][0], DC)
    for layer in range(2):
        if layer:
            plan += by_tokens("qkv_c", T["w_qkv_c"][0], 0, 1536) + deep("o_c", T["w_o_c"][0], DC)
        plan += by_features("up", T["w_up"][layer], 0, DFF1) + deep("down", T["w_down"][layer], DFF1 // P)
        plan += deep("ple", T["w_ple"][layer], 2) + deep("ple_gate", T["w_ple_gate"][layer], DC)
    for l in range(2):
        uq, ukv = T["mla_w_uq_2"][l], T["mla_w_ukv_2"][l]

        def mla_pieces(slot, uq=uq, ukv=ukv):
            return [(slot[:, 0:384], uq[0:P, :]), (slot[0:64, 384:768], uq[P:192, :]), (slot[:, 768:1280], ukv)]
        plan += by_tokens("mem_kv", T["mem_w_kv_2"][l], 0, 512) + by_tokens("in_2", T["w_in_2"][l], 0, D_IN2)
        plan.append(dict(key="mla", pieces=mla_pieces, kc=1, size=1280, split=False))
        plan += deep("o_2", T["w_o_2"][l], MIX2 // P)
        for n in range(0, DFF2, 256):
            plan += by_features("ff_gate", T["ffn_w_gate_2"][l], n, n + 256) + by_features("ff_up", T["ffn_w_up_2"][l], n, n + 256)
        plan += deep("down_2", T["ffn_w_down_2"][l], DFF2 // P)
    return plan


def spread(ap, axis, n):
    shape = list(ap.shape)
    shape.insert(axis, n)
    return ap.unsqueeze(axis).to_broadcast(shape)


def skewed(stages, n):
    for step in range(n + len(stages) - 1):
        for k, stage in reversed(list(enumerate(stages))):
            if 0 <= step - k < n:
                stage(step - k)


def program(nc, T, out):
    ctx = ExitStack()
    with ctx:
        def sbuf(name, shape, dt=F32):
            return ctx.enter_context(nc.sbuf_tensor(name, shape, dt))

        def sem(name):
            return ctx.enter_context(nc.semaphore(name))

        pe = Line(nc.tensor, sem("pe_done"))
        dve = Line(nc.vector, sem("dve_done"))
        act = Line(nc.scalar, sem("act_done"))
        pool = Line(nc.gpsimd, sem("pool_done"))
        sp = Line(nc.sync, sem("sp_done"))
        V, A, G, E = nc.vector, nc.scalar, nc.gpsimd, nc.tensor

        consts = sbuf("consts", [P, N_CONST])
        cols = sbuf("cols", [P, N_COLS])
        rows = sbuf("rows", [P, ROW_MAX])
        h = sbuf("h", [P, NT, D])
        trig = sbuf("trig", [P, 2, NT, 60])
        stat = sbuf("stat", [P, 256])
        WIDTH = 8 * 256
        N_RAW, N_HALF = 3, 2
        raw = sbuf("weights_raw", [P, N_RAW * WIDTH])
        high, low = [sbuf("weights_" + n, [P, N_HALF * WIDTH], F32R) for n in ("high", "low")]
        psum = [ctx.enter_context(nc.psum_tensor(f"bank{b}", [P, 512], F32)) for b in range(8)]
        banks = Banks(psum)
        weights = Weights(sp, act, dve, weight_plan(T), raw, high, low, WIDTH, [sem(f"raw{s}_landed") for s in range(N_RAW)])
        s_in, s_rows, s_out = sem("inputs_landed"), sem("rows_landed"), sem("output_landed")

        def const(name, n=None):
            a, w = CONST[name]
            return consts[:, a:a + (n or w)]

        ident = const("ident")
        ones = const("causal3")[:, P:2 * P]

        scopes, n_cut = [], [0]

        def shaped(v, *shape):
            names = "abcd"[:len(shape)]
            return v if len(shape) == 1 else v.rearrange("p (%s) -> p %s" % (" ".join(names), " ".join(names)),
                                                         **{k: n for k, n in zip(names, shape)})

        def cut(*shape, dt=F32):
            n_cut[0] += 1
            n = int(np.prod(shape))
            return shaped(scopes[-1].enter_context(nc.sbuf_tensor(f"buffer{n_cut[0]}", [P, n], dt))[:, :], *shape)

        def cut_pair(*shape):
            return cut(*shape, dt=F32R), cut(*shape, dt=F32R)

        def scope():
            scopes.append(ExitStack())

        def close():
            scopes.pop().close()

        def join():
            ends = [x.last() for x in (pe, dve, act, pool)]
            for x in (pe, dve, act, pool):
                x.need(ends)

        def copy_on(line, dst, src, *after):
            line.need(*after)
            if line is act:
                return act.did(A.copy(dst, src))
            return line.did(line.engine.tensor_copy(dst, src))

        def inv_root(ms, root, inv, after):
            act.need(after)
            m = act.did(A.activation(root, ms, ACT.Sqrt))
            dve.need(m)
            return dve.did(V.reciprocal(inv, root))

        def transposes(blocks, after):
            b = banks.take(pe)
            pe.need(after)
            for k, src in enumerate(blocks):
                w = src.shape[-1]
                mm = E.transpose(psum[b][0:w, k * P:(k + 1) * P], src, ident)
            return b, pe.did(mm)

        evac_turn = [0]

        def evacuate(b, dst, src, *after):
            evac_turn[0] += 1
            m = copy_on(act if evac_turn[0] % 2 else dve, dst, src, *after)
            banks.free(b, m)
            return m

        def feature_major(src, n_chunks, dst, after, gain=None):
            marks = []
            high, low = dst
            for k in range(0, n_chunks, 2):
                b, done = transposes([src[:, t, (k + i) * P:(k + i + 1) * P] for i in range(2) for t in range(NT)], after)
                bank = psum[b][:, :].rearrange("p (k n) -> p k n", k=2)
                act.need(done)
                if gain is None:
                    m = act.did(A.copy(high[:, k:k + 2, :], bank))
                    dve.need(m)
                    m = dve.did(V.tensor_tensor(low[:, k:k + 2, :], bank, high[:, k:k + 2, :].bitcast(F32), ALU.subtract))
                else:
                    for i in range(2):
                        m = act.did(A.activation(high[:, k + i, :], bank[:, i, :], ACT.Copy, scale=gain[:, k + i:k + i + 1]))
                    dve.need(m)
                    for i in range(2):
                        m = dve.did(V.scalar_tensor_tensor(low[:, k + i, :], bank[:, i, :], gain[:, k + i:k + i + 1],
                                                           high[:, k + i, :].bitcast(F32), ALU.mult, ALU.subtract))
                banks.free(b, m)
                marks.append(m)
            return marks

        def heads_transposed(src, n, d, dst, after):
            marks = []
            for k in range(0, n, 2):
                m_ = min(2, n - k)
                b, m = transposes([src(k + i, t) for i in range(m_) for t in range(NT)], after)
                bank = psum[b][0:d, 0:m_ * SEQ].rearrange("p (k n) -> p k n", k=m_)
                marks.append(evacuate(b, dst[0:d, k:k + m_, :], bank, m))
            return marks

        def normed(src, dst, after, s=0):
            marks = []
            for t in range(NT):
                act.need(after)
                m = act.did(A.activation(dst[:, t, :], src[:, t, :], ACT.Square, accum_out=stat[:, s + t:s + t + 1]))
                marks.append(m)
            dve.need(marks)
            m = dve.did(V.tensor_scalar(stat[:, s + 2:s + 4], stat[:, s:s + 2], 1.0 / D, EPS, ALU.mult, ALU.add))
            m = inv_root(stat[:, s + 2:s + 4], stat[:, s + 4:s + 6], stat[:, s + 6:s + 8], m)
            marks = []
            for t in range(NT):
                line = dve if t else pool
                line.need(m, after)
                marks.append(line.did(line.engine.tensor_scalar(dst[:, t, :], src[:, t, :], stat[:, s + 6 + t:s + 7 + t],
                                                                None, ALU.mult)))
            return marks

        def product(out, x, w, first, last):
            (xh, xl), (wh, wl) = x, w
            E.matmul(out, xh, wh, start=first, stop=False)
            E.matmul(out, xh, wl, start=False, stop=False)
            return E.matmul(out, xl, wh, start=False, stop=last)

        def half(pair, index):
            return tuple(v[index] for v in pair)

        def token_linear(xT, key, n0, nn, evac, after):
            held = [banks.take(pe) for _ in range(NT)]
            for k0 in (0, 4):
                w, m = weights.take((key, k0, n0))
                pe.need(m, after)
                done = []
                for t in range(NT):
                    for k in range(4):
                        mm = product(psum[held[t]][:, 0:nn], half(xT, np.s_[:, k0 + k, t * P:(t + 1) * P]),
                                     half(w, np.s_[:, k, :]), k0 + k == 0, k0 + k == DC - 1)
                    done.append(pe.did(mm))
                weights.done(done[-1])
            for t in range(NT):
                evac(t, held[t], done[t])

        def deep_linear(xT, kc, key, after):
            held = [banks.take(pe) for _ in range(4)]
            for k0 in range(0, kc, 2):
                w, m = weights.take((key, k0, 0))
                pe.need(m, after)
                done = []
                for t in range(NT):
                    for side in range(2):
                        for k in range(2):
                            mm = product(psum[held[2 * t + side]][:, :], half(xT, np.s_[:, k0 + k, t * P:(t + 1) * P]),
                                         half(w, np.s_[:, k, side * 512:(side + 1) * 512]), k0 + k == 0, k0 + k == kc - 1)
                        done.append(pe.did(mm))
                weights.done(done[-1])
            return held, done

        def feature_linear(xT, key, n0, evac, after):
            w, m = weights.take((key, 0, n0))
            b = banks.take(pe)
            pe.need(m, after)
            for i in range(2):
                for k in range(DC):
                    mm = product(psum[b][:, i * SEQ:(i + 1) * SEQ], half(w, np.s_[:, k, i * P:(i + 1) * P]),
                                 half(xT, np.s_[:, k, :]), k == 0, k == DC - 1)
            done = pe.did(mm)
            weights.done(done)
            evac(n0 // P, b, done)

        def add_normed(held, done, gain, mix, tmp, bias=None, gain_after=None):
            ready = []
            for t in range(NT):
                for half in range(2):
                    b = held[2 * t + half]
                    cut_ = slice(half * 512, (half + 1) * 512)
                    if bias is None:
                        ready.append(evacuate(b, mix[:, t, cut_], psum[b][:, :], done[2 * t + half]))
                    else:
                        dve.need(done[2 * t + half], gain_after)
                        m = dve.did(V.tensor_tensor(mix[:, t, cut_], psum[b][:, :], bias[:, cut_], ALU.add))
                        banks.free(b, m)
                        ready.append(m)
            marks = normed(mix, tmp, ready)
            out_ = []
            for t in range(NT):
                dve.need(marks, gain_after)
                m = dve.did(V.tensor_tensor(tmp[:, t, :], tmp[:, t, :], gain, ALU.mult))
                dve.need(m)
                out_.append(dve.did(V.tensor_tensor(h[:, t, :], h[:, t, :], tmp[:, t, :], ALU.add)))
            return out_

        sp.engine.dma_start(consts[:, :], T["consts"]).then_inc(s_in, 16)
        sp.engine.dma_start(h[:, :, :], T["x"][0].rearrange("(t p) d -> p t d", p=P)).then_inc(s_in, 16)
        sp.engine.dma_start(cols[:, :], T["cols"]).then_inc(s_in, 16)
        pos_i = sbuf("pos_i", [P, 4], I32)
        sp.engine.dma_start(pos_i[:, :], T["positions"]).then_inc(s_in, 16)
        loaded = (s_in, 64)

        rows_count = [0]

        def load_rows(layer):
            sp.need(dve.last(), act.last(), pool.last())
            n = ROW_LEN[layer]
            sp.engine.dma_start(rows[:, 0:n], T["rows"][layer:layer + 1, 0:n].partition_broadcast(P).rearrange("q a n -> q (a n)")
                                ).then_inc(s_rows, 16)
            rows_count[0] += 16
            return (s_rows, rows_count[0])

        def row(layer, name):
            a, n = ROWS[layer][name]
            return rows[:, a:a + n]

        pos_f = sbuf("pos_f", [P, 4])
        scope()
        ang = cut(NT, 60)
        turns = cut(NT, 60)
        for x in (pe, dve, act, pool):
            x.need(loaded)
        m = dve.did(V.tensor_copy(pos_f[:, :], pos_i[:, :]))
        dve.need(m)
        for t in range(NT):
            m = dve.did(V.tensor_scalar(ang[:, t, 0:ROT_C], const("freq")[:, 0:ROT_C], pos_f[:, t:t + 1], None, ALU.mult))
            m = dve.did(V.tensor_scalar(ang[:, t, ROT_C:60], const("freq")[:, ROT_C:60], pos_f[:, 2 + t:3 + t], None, ALU.mult))
        PI_A = 6.28125
        PI_B = float(np.float32(np.floor((TWO_PI - PI_A) * 2 ** 21) / 2 ** 21))
        PI_C = float(TWO_PI - PI_A - PI_B)
        MAGIC = float(3 * 2 ** 22)
        for which, shift in ((0, 0.25), (1, 0.0)):
            dst = trig[:, which, :, :]
            dve.need(m)
            m = dve.did(V.tensor_scalar(turns[:, :, :], ang[:, :, :], 1.0 / TWO_PI, shift, ALU.mult, ALU.add))
            dve.need(m)
            m = dve.did(V.tensor_scalar(turns[:, :, :], turns[:, :, :], MAGIC, None, ALU.add))
            dve.need(m)
            m = dve.did(V.tensor_scalar(turns[:, :, :], turns[:, :, :], MAGIC, None, ALU.subtract))
            src = ang
            for part in (PI_A, PI_B, PI_C):
                dve.need(m)
                m = dve.did(V.scalar_tensor_tensor(dst, turns[:, :, :], -part, src if src is dst else src[:, :, :], ALU.mult, ALU.add))
                src = dst
            if shift:
                dve.need(m)
                m = dve.did(V.tensor_scalar(dst, dst, float(np.pi / 2), None, ALU.add))
            dve.need(m)
            m = dve.did(V.tensor_scalar(dst, dst, float(np.float32(3.1415925)), -float(np.float32(3.1415925)), ALU.min, ALU.max))
            act.need(m)
            trig_ready = act.did(A.activation(dst, dst, ACT.Sin))
        join()
        close()

        def rope(x, dst, n, r, f0, t, tmp1, tmp2, after):
            c = spread(spread(trig[:, 0, t, f0:f0 + r], 1, 2), 1, n)
            s = spread(trig[:, 1, t, f0:f0 + r], 1, n)
            x4 = x.rearrange("p n (two r) -> p n two r", two=2)
            d4 = dst.rearrange("p n (two r) -> p n two r", two=2)
            a = tmp1[:, 0:n * 2 * r].rearrange("p (n two r) -> p n two r", two=2, r=r)
            b = tmp2[:, 0:n * 2 * r].rearrange("p (n two r) -> p n two r", two=2, r=r)
            dve.need(after, trig_ready, dve.last())
            dve.did(V.tensor_tensor(b[:, :, 0, :], x4[:, :, 1, :], s, ALU.mult))
            dve.did(V.tensor_tensor(b[:, :, 1, :], x4[:, :, 0, :], s, ALU.mult))
            m = dve.did(V.tensor_tensor(a, x4, c, ALU.mult))
            dve.need(m)
            dve.did(V.tensor_tensor(d4[:, :, 0, :], a[:, :, 0, :], b[:, :, 0, :], ALU.subtract))
            return dve.did(V.tensor_tensor(d4[:, :, 1, :], a[:, :, 1, :], b[:, :, 1, :], ALU.add))

        def feed_forward_1(layer, rows_ready):
            y = cut(NT, D)
            hT = cut_pair(DC, SEQ)
            aT = cut_pair(DFF1 // P, SEQ)
            r = cut(2, 512)
            sq = cut(2, 512)
            m = normed(h, y, [dve.last()])
            g0 = COLS["pre1"] + (layer * 2 + 1) * DC
            xm = feature_major(y, DC, hT, m, cols[:, g0:g0 + DC])
            r_free, sq_free = [None] * 2, [None] * 2
            ready = []

            def evac(c, b, done):
                i = len(ready) % 2
                dst = [v[:, c:c + 2, :].rearrange("p k n -> p (k n)") for v in aT]
                act.need(done, r_free[i])
                m = act.did(A.activation(r[:, i, :], psum[b][:, :], ACT.Relu))
                banks.free(b, m)
                act.need(m)
                hi = act.did(A.activation(dst[0], r[:, i, :], ACT.Square))
                dve.need(m, sq_free[i])
                m = dve.did(V.tensor_tensor(sq[:, i, :], r[:, i, :], r[:, i, :], ALU.mult))
                r_free[i] = [m, hi]
                dve.need(m, hi)
                sq_free[i] = dve.did(V.tensor_tensor(dst[1], sq[:, i, :], dst[0].bitcast(F32), ALU.subtract))
                ready.append(sq_free[i])
            for n0 in range(0, DFF1, 256):
                feature_linear(hT, "up", n0, evac, xm)
            held, done = deep_linear(aT, DFF1 // P, "down", ready)
            return add_normed(held, done, row(layer, "post_ff"), y, cut(NT, D), gain_after=rows_ready)

        def gated_add(layer):
            hT = cut_pair(DC, SEQ)
            gate = cut(4, 512)
            emb = cut(4, 512)
            pt = cut(NT, 256)
            pT = cut_pair(2, SEQ)
            sp.need(dve.last(), act.last(), pe.last(), pool.last())
            sp.engine.dma_start(pt, T["p"][layer, 0].rearrange("(t p) d -> p t d", p=P)).then_inc(s_in, 16)
            p_ready = (s_in, 64 + 16 * (layer + 1))
            m = feature_major(h, DC, hT, [dve.last()])
            pm = feature_major(pt, 2, pT, [p_ready])
            held, done = deep_linear(pT, 2, "ple", pm)
            em = [evacuate(b, emb[:, i, :], psum[b][:, :], done[i]) for i, b in enumerate(held)]
            held, done = deep_linear(hT, DC, "ple_gate", m)
            for i, b in enumerate(held):
                t, half_ = i // 2, i % 2
                act.need(done[i])
                g = act.did(A.activation(gate[:, i, :], psum[b][:, :], ACT.Sigmoid))
                banks.free(b, g)
                dve.need(g, em[i])
                m = dve.did(V.tensor_tensor(gate[:, i, :], gate[:, i, :], emb[:, i, :], ALU.mult))
                dve.need(m)
                v = h[:, t, half_ * 512:(half_ + 1) * 512]
                m = dve.did(V.tensor_tensor(v, v, gate[:, i, :], ALU.add))
            return m

        def mixer_ab(rows_ready):
            top = cut_pair(DC, SEQ)
            y = cut(NT, D)
            m = normed(h, y, loaded_all)
            xm = feature_major(y, DC, top, m, cols[:, COLS["pre1"]:COLS["pre1"] + DC])
            gates = cut(NT, 16)
            wg, wm = weights.take("gates")
            b = banks.take(pe)
            pe.need(wm, xm)
            for t in range(NT):
                for k in range(DC):
                    mm = product(psum[b][:, t * 16:t * 16 + 16], half(top, np.s_[:, k, t * P:(t + 1) * P]),
                                 half(wg, np.s_[:, k, :]), k == 0, k == DC - 1)
            done = pe.did(mm)
            weights.done(done)
            dve.need(done, rows_ready)
            m = dve.did(V.tensor_tensor(gates, psum[b][:, 0:32].rearrange("p (t n) -> p t n", t=NT),
                                        spread(row(0, "gate_bias"), 1, NT), ALU.add))
            banks.free(b, m)
            v8 = cut(NT, 8)
            l8 = cut(NT, 8)
            g8 = cut(NT, 8)
            beta = cut(NT, 4)
            ea = cut(8)
            gview = gates.rearrange("p t (a b) -> p t a b", a=4)
            dve.need(m)
            m = dve.did(V.tensor_tensor(v8.rearrange("p t (a b) -> p t a b", a=2), gview[:, :, 1::2, :],
                                        spread(const("sign8").rearrange("p (a b) -> p a b", a=2), 1, NT), ALU.mult))
            dve.need(m)
            m = dve.did(V.scalar_tensor_tensor(l8, v8, -1.0, v8, ALU.mult, ALU.max))
            act.need(m)
            m = act.did(A.activation(l8, l8, ACT.Exp, scale=-1.0))
            m2 = act.did(A.activation(ea[:, 0:4], row(0, "a_log"), ACT.Exp))
            act.need(m)
            m = act.did(A.activation(l8, l8, ACT.Ln, bias=1.0))
            m3 = act.did(A.activation(beta, gates[:, :, 0:4], ACT.Sigmoid))
            dve.did(V.memset(ea[:, 4:8], 1.0))
            dve.need(m, m2, dve.last())
            m = dve.did(V.scalar_tensor_tensor(g8, v8, 0.0, l8, ALU.max, ALU.add))
            dve.need(m)
            g_ready = dve.did(V.scalar_tensor_tensor(g8, g8, -1.0, spread(ea, 1, NT), ALU.mult, ALU.mult))
            gc = cut(NT, 8)
            tri = const("causal3")
            b = banks.take(pe)
            pe.need(g_ready)
            for t in range(NT):
                for s_ in range(t + 1):
                    mm = E.matmul(psum[b][:, t * 8:t * 8 + 8], tri[:, (t + s_) * P:(t + s_ + 1) * P], g8[:, s_, :],
                                  start=(s_ == 0), stop=(s_ == t))
            done = pe.did(mm)
            dve.need(done)
            gc_ready = dve.did(V.tensor_copy(gc, psum[b][:, 0:16].rearrange("p (t n) -> p t n", t=NT)))
            banks.free(b, gc_ready)
            ab = cut(NT, 8)
            dve.need(gc_ready, m3)
            dve.did(V.tensor_copy(ab[:, :, 0:4], beta))
            m = dve.did(V.tensor_tensor(ab[:, :, 4:8], gates[:, :, 8:12], gc[:, :, 4:8], ALU.subtract))
            b, done = transposes([ab[:, t, :] for t in range(NT)], [m])
            abT = cut(SEQ)
            act.need(done)
            m = act.did(A.copy(abT[0:8, :], psum[b][0:8, 0:SEQ]))
            banks.free(b, m)
            mxT = cut(SEQ)
            dve.need(m)
            mx_ready = dve.did(V.tensor_tensor_scan(mxT[0:8, :], abT[0:8, :], abT[0:8, :], 0.0, ALU.max, ALU.max))
            mcol = cut(NT, 8)
            b = banks.take(pe)
            pe.need(mx_ready)
            for t in range(NT):
                mm = E.transpose(psum[b][:, t * 8:t * 8 + 8], mxT[0:8, t * P:(t + 1) * P], ident[0:8, 0:8])
            done = pe.did(mm)
            dve.need(done)
            mcol_ready = dve.did(V.tensor_copy(mcol, psum[b][:, 0:16].rearrange("p (t n) -> p t n", t=NT)))
            banks.free(b, mcol_ready)

            qkv = cut(12, SEQ)
            qkb = cut(8, SEQ)
            zs, vb, og = cut(NT, 512), cut(NT, 512), cut(NT, 512)
            scope()
            pad = cut(2, 2, SEQ + 3)
            cv = cut(2, 2, SEQ)
            zeroed = pool.did(G.memset(pad[:, :, :, 0:3], 0.0))
            pad_free, cv_free = [zeroed, zeroed], [None, None]
            qkv_ready = []
            wc = COLS["conv_a"]
            turn = [0]

            def evac(c, b, done):
                i = turn[0] % 2
                turn[0] += 1
                act.need(done, pad_free[i])
                m = act.did(A.copy(pad[:, i, :, 3:], psum[b][:, :].rearrange("p (k n) -> p k n", k=2)))
                banks.free(b, m)
                ends = []
                for j in range(2):
                    ch = c + j
                    dve.need(m, cv_free[i])
                    e = dve.did(V.tensor_scalar(cv[:, i, j, :], pad[:, i, j, 0:SEQ], cols[:, wc + ch * 4:wc + ch * 4 + 1],
                                                None, ALU.mult))
                    ends.append(e)
                for k in range(1, 4):
                    for j in range(2):
                        ch = c + j
                        dve.need(ends[j])
                        ends[j] = dve.did(V.scalar_tensor_tensor(cv[:, i, j, :], pad[:, i, j, k:k + SEQ],
                                                                 cols[:, wc + ch * 4 + k:wc + ch * 4 + k + 1],
                                                                 cv[:, i, j, :], ALU.mult, ALU.add))
                pad_free[i] = ends[1]
                act.need(ends)
                cv_free[i] = act.did(A.activation(qkv[:, c:c + 2, :], cv[:, i, :, :], ACT.Silu))
                qkv_ready.append(cv_free[i])
            for n0 in range(0, QKV_A, 256):
                feature_linear(top, "qkv_a", n0, evac, xm)

            qkb_ready = []

            def evac_qk(c, b, done):
                c -= COL_QB // P
                act.need(done)
                m = act.did(A.mul(qkb[:, c:c + 2, :], psum[b][:, :].rearrange("p (k n) -> p k n", k=2),
                                  float(P) ** -0.5 if c < 4 else 1.0))
                banks.free(b, m)
                qkb_ready.append(m)
            for n0 in range(COL_QB, COL_VB, 256):
                feature_linear(top, "qk_b", n0, evac_qk, xm)
            lin_ready = []
            for n0, dst, fn in ((COL_Z, zs, ACT.Silu), (COL_VB, vb, ACT.Copy), (COL_O, og, ACT.Sigmoid)):
                def evac(t, b, done, dst=dst, fn=fn):
                    act.need(done)
                    m = act.did(A.activation(dst[:, t, :], psum[b][:, :], fn))
                    banks.free(b, m)
                    lin_ready.append(m)
                token_linear(top, "zvo", n0, 512, evac, xm)

            close()

            kbT = cut(4, SEQ)
            sq = cut(2, 512)
            nr = cut(2, 512)
            flat = qkv.rearrange("p k n -> p (k n)")
            l2_ready = []
            sq_free, nr_free = [None, None], [None, None]
            for c in range(0, 8, 2):
                i = (c // 2) % 2
                src = flat[:, c * SEQ:(c + 2) * SEQ]
                pool.need(qkv_ready, sq_free[i])
                m = pool.did(G.tensor_tensor(sq[:, i, :], src, src, ALU.mult))
                b = banks.take(pe)
                pe.need(m)
                done = pe.did(E.matmul(psum[b][:, :], ones, sq[:, i, :], start=True, stop=True))
                sq_free[i] = done
                dve.need(done, nr_free[i])
                m = dve.did(V.tensor_scalar(nr[:, i, :], psum[b][:, :], EPS, None, ALU.add))
                banks.free(b, m)
                m = inv_root(nr[:, i, :], nr[:, i, :], nr[:, i, :], m)
                dve.need(m)
                m = dve.did(V.scalar_tensor_tensor(src, src, float(P) ** -0.5 if c < 4 else 1.0, nr[:, i, :], ALU.mult, ALU.mult))
                nr_free[i] = m
                l2_ready.append(m)
            vbeta = cut(NT, 512)
            v_ready = []
            for t in range(NT):
                b, done = transposes([qkv[:, 8 + c, t * P:(t + 1) * P] for c in range(4)], qkv_ready)
                dve.need(done, m3)
                m = dve.did(V.tensor_tensor(vbeta[:, t, :].rearrange("p (h d) -> p h d", h=4),
                                            psum[b][:, :].rearrange("p (h d) -> p h d", h=4),
                                            spread(beta[:, t, :], 2, P), ALU.mult))
                banks.free(b, m)
                v_ready.append(m)

            select = const("select").rearrange("p (h n) -> p h n", h=8)
            gb = cut(NT, P)
            LT = cut(4, 384)
            AT = cut(4, 384)
            PT = cut(4, 384)
            dec = cut(2, 384)
            dec_free = [None, None]
            gb_free = None
            LT_ready, AT_ready, PT_ready = [], [], []

            def key_query(dst_bank, kT, qT, after):
                pe.need(after)
                E.matmul(psum[dst_bank][:, 0:SEQ], kT[:, 0:P], qT[:, 0:SEQ], start=True, stop=True)
                return pe.did(E.matmul(psum[dst_bank][:, SEQ:384], kT[:, P:SEQ], qT[:, P:SEQ], start=True, stop=True))

            for hd in range(4):
                b = banks.take(pe)
                pe.need(mx_ready)
                done = pe.did(E.matmul(psum[b][:, 0:SEQ], select[0:8, hd, :], abT[0:8, :], start=True, stop=True))
                dve.need(done, l2_ready)
                kb_ready = dve.did(V.tensor_tensor(kbT[:, hd, :], qkv[:, 4 + hd, :], psum[b][:, 0:SEQ], ALU.mult))
                banks.free(b, kb_ready)
                dve.need(gb_free)
                m = dve.did(V.tensor_copy(gb, spread(g8[:, :, hd], 2, P)))
                b = banks.take(pe)
                pe.need(m)
                E.matmul(psum[b][:, 0:SEQ], gb[:, 0, :], tri[:, 0:SEQ], start=True, stop=False)
                gb_free = done = pe.did(E.matmul(psum[b][:, P:SEQ], gb[:, 1, :], tri[:, SEQ:384], start=False, stop=True))
                i = hd % 2
                dve.need(done, dec_free[i])
                dve.did(V.tensor_scalar(dec[:, i, 0:SEQ], psum[b][:, 0:SEQ], gc[:, 0, hd:hd + 1], 0.0, ALU.subtract, ALU.min))
                m = dve.did(V.tensor_scalar(dec[:, i, SEQ:384], psum[b][:, P:SEQ], gc[:, 1, hd:hd + 1], 0.0, ALU.subtract, ALU.min))
                banks.free(b, m)
                act.need(m)
                m = dec_ready = act.did(A.activation(dec[:, i, :], dec[:, i, :], ACT.Exp))
                pool.need(m)
                e2 = pool.did(G.tensor_tensor(AT[:, hd, :], dec[:, i, :], const("causal3"), ALU.mult))
                b = banks.take(pe)
                done = key_query(b, qkv[:, 4 + hd, :], kbT[:, hd, :], [kb_ready])
                dve.need(done, dec_ready)
                m = dve.did(V.tensor_tensor(LT[:, hd, :], dec[:, i, :], psum[b][:, 0:384], ALU.mult))
                dec_free[i] = [e2, m]
                banks.free(b, m)
                LT_ready.append(m)
                b = banks.take(pe)
                done = key_query(b, qkv[:, 4 + hd, :], qkv[:, hd, :], [l2_ready])
                dve.need(done, e2)
                m = dve.did(V.tensor_tensor(AT[:, hd, :], AT[:, hd, :], psum[b][:, 0:384], ALU.mult))
                banks.free(b, m)
                AT_ready.append(m)

            level = const("level").rearrange("p (l n) -> p l n", l=7)
            N_, M_ = [[cut(4, P) for _ in range(NT)] for _ in range(2)]
            C_ = [shaped(sq[:, j, :], 4, P) for j in range(NT)]
            Q_ = [shaped(nr[:, j, :], 4, P) for j in range(NT)]
            n_ready, m_ready, q_free, c_free = [None] * 2, [None] * 2, [None] * 2, [None] * 2
            idb = spread(ident, 1, 4)

            def diag(j):
                return LT[:, :, 0:P] if j == 0 else LT[:, :, SEQ:384]
            for j in range(NT):
                pool.need(LT_ready)
                m = pool.did(G.tensor_tensor(C_[j], diag(j), spread(level[:, 0, :], 1, 4), ALU.mult))
                dve.need(m)
                c_free[j] = n_ready[j] = dve.did(V.tensor_tensor(N_[j], idb, C_[j], ALU.subtract))
                b, done = transposes([N_[j][:, hd, :] for hd in range(4)], [n_ready[j]])
                act.need(done)
                m_ready[j] = act.did(A.copy(M_[j], psum[b][:, :].rearrange("p (h n) -> p h n", h=4)))
                banks.free(b, m_ready[j])
            for lv in range(1, 7):
                for j in range(NT):
                    pool.need(c_free[j])
                    cm = pool.did(G.tensor_tensor(C_[j], diag(j), spread(level[:, lv, :], 1, 4), ALU.mult))
                    b = banks.take(pe)
                    pe.need(cm, m_ready[j], n_ready[j])
                    for hd in range(4):
                        mm = E.matmul(psum[b][:, hd * P:(hd + 1) * P], C_[j][:, hd, :], M_[j][:, hd, :], start=True, stop=True)
                    c_free[j] = done = pe.did(mm)
                    act.need(done, q_free[j])
                    q = act.did(A.copy(Q_[j], psum[b][:, :].rearrange("p (h n) -> p h n", h=4)))
                    banks.free(b, q)
                    bn = banks.take(pe)
                    pe.need(q)
                    for hd in range(4):
                        mm = E.matmul(psum[bn][:, hd * P:(hd + 1) * P], Q_[j][:, hd, :], N_[j][:, hd, :], start=True, stop=True)
                    dn = pe.did(mm)
                    if lv < 6:
                        bm = banks.take(pe)
                        for hd in range(4):
                            mm = E.matmul(psum[bm][:, hd * P:(hd + 1) * P], N_[j][:, hd, :], Q_[j][:, hd, :], start=True, stop=True)
                        dm = pe.did(mm)
                        dve.need(dm)
                        m_ready[j] = dve.did(V.tensor_tensor(M_[j], M_[j], psum[bm][:, :].rearrange("p (h n) -> p h n", h=4), ALU.subtract))
                        banks.free(bm, m_ready[j])
                        dn = dm
                    q_free[j] = dn
                    dve.need(dn)
                    n_ready[j] = dve.did(V.tensor_tensor(N_[j], N_[j], psum[bn][:, :].rearrange("p (h n) -> p h n", h=4), ALU.subtract))
                    banks.free(bn, n_ready[j])

            for hd in range(4):
                i = hd % 2
                b = banks.take(pe)
                pe.need(mx_ready)
                done = pe.did(E.matmul(psum[b][:, 0:SEQ], select[0:8, 4 + hd, :], mxT[0:8, :], start=True, stop=True))
                dve.need(done, dec_free[i])
                dve.did(V.tensor_scalar(dec[:, i, 0:SEQ], psum[b][:, 0:SEQ], ab[:, 0, 4 + hd:5 + hd], 0.0, ALU.subtract, ALU.max))
                m = dve.did(V.tensor_scalar(dec[:, i, SEQ:384], psum[b][:, P:SEQ], ab[:, 1, 4 + hd:5 + hd], 0.0, ALU.subtract, ALU.max))
                banks.free(b, m)
                act.need(m)
                m = act.did(A.activation(dec[:, i, :], dec[:, i, :], ACT.Exp, scale=-1.0))
                pool.need(m)
                e = dec_free[i] = pool.did(G.tensor_tensor(PT[:, hd, :], dec[:, i, :], const("causal3"), ALU.mult))
                b = banks.take(pe)
                done = key_query(b, qkb[:, 4 + hd, :], qkb[:, hd, :], qkb_ready)
                dve.need(done, e)
                m = dve.did(V.tensor_tensor(PT[:, hd, :], PT[:, hd, :], psum[b][:, 0:384], ALU.mult))
                banks.free(b, m)
                PT_ready.append(m)

            U = shaped(kbT.rearrange("p h n -> p (h n)"), NT, 512)
            Z = cut(512)
            b = banks.take(pe)
            pe.need(n_ready, v_ready)
            for hd in range(4):
                mm = E.matmul(psum[b][:, hd * P:(hd + 1) * P], N_[0][:, hd, :], vbeta[:, 0, hd * P:(hd + 1) * P], start=True, stop=True)
            done = pe.did(mm)
            u1 = copy_on(act, U[:, 0, :], psum[b][:, :], done)
            banks.free(b, u1)
            b = banks.take(pe)
            pe.need(u1)
            for hd in range(4):
                mm = E.matmul(psum[b][:, hd * P:(hd + 1) * P], LT[:, hd, P:SEQ], U[:, 0, hd * P:(hd + 1) * P], start=True, stop=True)
            done = pe.did(mm)
            dve.need(done)
            m = dve.did(V.tensor_tensor(Z, vbeta[:, 1, :], psum[b][:, :], ALU.subtract))
            banks.free(b, m)
            b = banks.take(pe)
            pe.need(m)
            for hd in range(4):
                mm = E.matmul(psum[b][:, hd * P:(hd + 1) * P], N_[1][:, hd, :], Z[:, hd * P:(hd + 1) * P], start=True, stop=True)
            done = pe.did(mm)
            u2 = copy_on(act, U[:, 1, :], psum[b][:, :], done)
            banks.free(b, u2)

            def weighted(W3, val, t, after):
                b = banks.take(pe)
                pe.need(after)
                for hd in range(4):
                    for s_ in range(t + 1):
                        k = t + s_
                        mm = E.matmul(psum[b][:, hd * P:(hd + 1) * P], W3[:, hd, k * P:(k + 1) * P],
                                      val[:, s_, hd * P:(hd + 1) * P], start=(s_ == 0), stop=(s_ == t))
                return b, pe.did(mm)

            mixed = y
            o_ready = []
            for t in range(NT):
                b, done = weighted(AT, U, t, [u1, u2, AT_ready])
                o_ready.append(evacuate(b, mixed[:, t, 0:512], psum[b][:, :], done))
            db = banks.take(pe)
            pe.need(PT_ready)
            for t in range(NT):
                for hd in range(4):
                    for s_ in range(t + 1):
                        k = t + s_
                        mm = E.matmul(psum[db][:, t * 4 + hd:t * 4 + hd + 1], PT[:, hd, k * P:(k + 1) * P], ones[:, 0:1],
                                      start=(s_ == 0), stop=(s_ == t))
            done = pe.did(mm)
            den, em = cut(NT, 4), cut(NT, 4)
            act.need(done)
            den_abs = act.did(A.activation(den, psum[db][:, 0:8].rearrange("p (t n) -> p t n", t=NT), ACT.Abs))
            banks.free(db, den_abs)
            dve.need(mcol_ready)
            m = dve.did(V.tensor_tensor(em, gc[:, :, 4:8], mcol[:, :, 4:8], ALU.add))
            act.need(m)
            m = act.did(A.activation(em, em, ACT.Exp, scale=-1.0))
            dve.need(m, den_abs)
            m = dve.did(V.tensor_tensor(den, den, em, ALU.max))
            dve.need(m)
            den_ready = dve.did(V.reciprocal(den, den))
            for t in range(NT):
                b, done = weighted(PT, vb, t, [PT_ready, lin_ready])
                dve.need(done, den_ready)
                m = dve.did(V.tensor_tensor(mixed[:, t, 512:D].rearrange("p (h d) -> p h d", h=4),
                                            psum[b][:, :].rearrange("p (h d) -> p h d", h=4),
                                            spread(den[:, t, :], 2, P), ALU.mult))
                banks.free(b, m)
                o_ready.append(m)
            sq2 = shaped(flat[:, 0:NT * D], NT, D)
            ss = cut(16)
            pool.need(o_ready)
            m = pool.did(G.tensor_tensor(sq2, mixed, mixed, ALU.mult))
            dve.need(m)
            m = dve.did(V.tensor_reduce(ss, sq2.rearrange("p t (h d) -> p (t h) d", h=8), AXX, ALU.add))
            dve.need(m)
            m = dve.did(V.tensor_scalar(ss, ss, 1.0 / P, EPS, ALU.mult, ALU.add))
            m = inv_root(ss, ss, ss, m)
            pool.need(lin_ready, rows_ready)
            g1 = pool.did(G.tensor_tensor(zs, zs, spread(row(0, "norm_a"), 1, NT), ALU.mult))
            g2 = pool.did(G.tensor_tensor(og, og, spread(row(0, "norm_b"), 1, NT), ALU.mult))
            dve.need(m, o_ready)
            m = dve.did(V.tensor_tensor(mixed.rearrange("p t (h d) -> p (t h) d", h=8), mixed.rearrange("p t (h d) -> p (t h) d", h=8),
                                        spread(ss, 2, P), ALU.mult))
            dve.need(m, g1, g2)
            e1 = dve.did(V.tensor_tensor(mixed[:, :, 0:512], mixed[:, :, 0:512], zs, ALU.mult))
            e2 = dve.did(V.tensor_tensor(mixed[:, :, 512:D], mixed[:, :, 512:D], og, ALU.mult))
            mm_ = feature_major(mixed, DC, top, [e1, e2])
            held, done = deep_linear(top, DC, "out_ab", mm_)
            return held, done, sq2, mixed

        def attention(groups, S, PTb, mx, den):
            state = [None] * len(groups)
            freeS, freeP, freeSt, freeQK, ready = [None, None], [None], [None, None], [None, None], {}

            def prepare(n):
                ready[n] = groups[n]["prepare"](n % 2, freeQK[n % 2])

            def tiles(g):
                return ((0, 0, P), (1, P, SEQ)) if g["causal"] else ((0, 0, SEQ), (1, SEQ, SEQ))

            def scores(n):
                g = groups[n]
                i = n % 2
                mk = g.get("mask")
                exps = []
                for t, c0, nk in tiles(g):
                    per = 512 // nk
                    for h0 in range(0, 4, per):
                        b = banks.take(pe)
                        pe.need(ready[n])
                        for j in range(per):
                            mm = E.matmul(psum[b][:, j * nk:(j + 1) * nk], g["q"](i, h0 + j)[:, t * P:(t + 1) * P],
                                          g["k"](i, h0 + j)[:, 0:nk], start=True, stop=True)
                        done = freeQK[i] = pe.did(mm)
                        bank = psum[b][:, :].rearrange("p (h n) -> p h n", h=per)
                        dve.need(done, freeS[i], freeSt[i])
                        s_ = S[:, i, h0:h0 + per, c0:c0 + nk]
                        if g.get("bias") is not None:
                            dve.need(g["bias_ready"])
                            m = dve.did(V.scalar_tensor_tensor(s_, bank, g["scale"], g["bias"][:, h0:h0 + per, c0:c0 + nk],
                                                               ALU.mult, ALU.subtract))
                        elif mk is None:
                            m = dve.did(V.tensor_scalar(s_, bank, g["scale"], None, ALU.mult))
                        else:
                            m = dve.did(V.scalar_tensor_tensor(s_, bank, g["scale"], spread(mk[:, c0:c0 + nk], 1, per),
                                                               ALU.mult, ALU.add))
                        banks.free(b, m)
                        dve.need(m)
                        mm_ = mx[:, i, t, h0:h0 + per]
                        m = dve.did(V.tensor_reduce(mm_, s_, AXX, ALU.max))
                        if g.get("sink") is not None:
                            dve.need(m)
                            m = dve.did(V.tensor_tensor(mm_, mm_, g["sink"][:, h0:h0 + per], ALU.max))
                        dve.need(m)
                        m = negated = dve.did(V.tensor_scalar(mm_, mm_, -1.0, None, ALU.mult))
                        act.need(m)
                        for j in range(per):
                            hh = h0 + j
                            exps.append(act.did(A.activation(S[:, i, hh, c0:c0 + nk], S[:, i, hh, c0:c0 + nk], ACT.Exp,
                                                             bias=mx[:, i, t, hh:hh + 1], accum_out=den[:, i, t, hh:hh + 1])))
                m = exps[-1]
                if g.get("sink") is not None:
                    sk = den[:, i, 2:4, :]
                    dve.need(negated)
                    m2 = dve.did(V.tensor_tensor(sk, mx[:, i, :, :], spread(g["sink"], 1, NT), ALU.add))
                    act.need(m2)
                    m2 = act.did(A.activation(sk, sk, ACT.Exp))
                    dve.need(m2, m)
                    m2 = dve.did(V.tensor_tensor(den[:, i, 0:2, :], den[:, i, 0:2, :], sk, ALU.add))
                    dve.need(m2)
                else:
                    dve.need(m)
                rd = dve.did(V.reciprocal(den[:, i, 0:2, :], den[:, i, 0:2, :]))
                state[n] = [m, rd]

            def turned(n):
                g = groups[n]
                i = n % 2
                marks = []
                n_blk = 3 if g["causal"] else 4
                for k in range(n_blk):
                    b, m = transposes([S[:, i, hh, k * P:(k + 1) * P] for hh in range(4)], [state[n][0]])
                    act.need(freeP[0])
                    dve.need(freeP[0])
                    marks.append(evacuate(b, PTb[:, k, :, :], psum[b][:, :].rearrange("p (h n) -> p h n", h=4), m))
                freeS[i] = m
                state[n].append(marks)

            def values(n):
                g = groups[n]
                i = n % 2
                b = banks.take(pe)
                pe.need(state[n][2], g["v_ready"])
                for t in range(NT):
                    blocks = ((0, 0),) if g["causal"] and t == 0 else ((1, 0), (2, 1)) if g["causal"] else ((2 * t, 0), (2 * t + 1, 1))
                    for hh in range(4):
                        for x, (k, s_) in enumerate(blocks):
                            mm = E.matmul(psum[b][:, (t * 4 + hh) * 64:(t * 4 + hh + 1) * 64], PTb[:, k, hh, :], g["v"](hh, s_),
                                          start=(x == 0), stop=(x == len(blocks) - 1))
                done = pe.did(mm)
                freeP[0] = done
                bank = psum[b][:, :].rearrange("p (t h d) -> p t h d", t=NT, h=4)
                dve.need(done, state[n][1])
                m = g["finish"](bank, den[:, i, 0:2, :])
                freeSt[i] = m
                banks.free(b, m)
            skewed([prepare, scores, turned, values], len(groups))

        def scaled_into(dst):
            def finish(bank, rden):
                for t in range(NT):
                    m = dve.did(V.tensor_tensor(dst[:, t, :].rearrange("p (h d) -> p h d", h=4), bank[:, t, :, :],
                                                spread(rden[:, t, :], 2, 64), ALU.mult))
                return m
            return finish

        def mixer_c(rows_ready):
            y, hT = cut(NT, D), cut_pair(DC, SEQ)
            m = normed(h, y, [dve.last()])
            xm = feature_major(y, DC, hT, m, cols[:, COLS["pre1"] + 2 * DC:COLS["pre1"] + 3 * DC])
            proj = cut(NT, 1536)
            marks = []
            for n0 in range(0, 1536, 512):
                def evac(t, b, done, n0=n0):
                    dve.need(done, rows_ready)
                    m = dve.did(V.tensor_tensor(proj[:, t, n0:n0 + 512], psum[b][:, :], row(1, "b_qkv")[:, n0:n0 + 512], ALU.add))
                    banks.free(b, m)
                    marks.append(m)
                token_linear(hT, "qkv_c", n0, 512, evac, xm)
            S = cut(2, 4, 512)
            PTb = cut(4, 4, P)
            tmp1, tmp2 = cut(1280), cut(1280)
            QK = cut(2, 5, SEQ)
            mx, den = cut(2, NT, 4), cut(2, 4, 4)
            for t in range(NT):
                x = proj[:, t, 0:1280].rearrange("p (n d) -> p n d", d=CHD)
                rm = rope(x, x, 20, ROT_C, 0, t, tmp1, tmp2, marks)
            mixed = y
            groups = []
            for kv in range(CKV):
                def prep(i, free, kv=kv):
                    act.need(free)
                    dve.need(free)
                    return heads_transposed(
                        lambda hh, t: proj[:, t, (kv * 4 + hh) * 64:(kv * 4 + hh + 1) * 64] if hh < 4 else
                        proj[:, t, 1024 + kv * 64:1024 + (kv + 1) * 64], 5, 64, QK[:, i, :, :], [rm])
                groups.append(dict(
                    prepare=prep, causal=True, scale=CHD ** -0.5, mask=const("window_neg"),
                    q=lambda i, hh: QK[0:64, i, hh, :], k=lambda i, hh: QK[0:64, i, 4, :],
                    v=lambda hh, s_, kv=kv: proj[:, s_, 1280 + kv * 64:1280 + (kv + 1) * 64], v_ready=marks,
                    sink=row(1, "sinks")[:, kv * 4:kv * 4 + 4], finish=scaled_into(mixed[:, :, kv * 256:(kv + 1) * 256])))
            attention(groups, S, PTb, mx, den)
            m = dve.last()
            mT = feature_major(mixed, DC, hT, [m])
            held, done = deep_linear(hT, DC, "o_c", mT)
            big = proj.rearrange("p t n -> p (t n)")
            return held, done, shaped(big[:, 0:NT * D], NT, D), mixed

        def head_norms(x, n, d, ss, gain, after):
            for t in range(NT):
                line = dve
                line.need(after)
                m = line.did(line.engine.tensor_tensor(x[:, t], x[:, t], spread(ss[:, t], 2, d), ALU.mult))
                line.need(m)
                g = gain.rearrange("p (n d) -> p n d", n=n)
                m = line.did(line.engine.tensor_tensor(x[:, t], x[:, t], g, ALU.mult))
            return m

        def mixer_2(l, rows_ready):
            layer = 2 + l
            R = lambda name: row(layer, name)
            mixed = cut(NT, MIX2)
            hp = cut(NT, D_IN2)
            kvm = cut(NT, 512)
            PTb = cut(4, 4, P)
            sq = PTb.rearrange("p a b c -> p (a b c)")
            st = cut(NT, 48)
            st2 = cut(NT, 16)

            def sum_squares(x, n, d, dst, after):
                for t in range(NT):
                    pool.need(after, dve.last())
                    a = sq[:, t * 1024:t * 1024 + n * d]
                    m = pool.did(G.tensor_tensor(a, x[:, t, :], x[:, t, :], ALU.mult))
                    dve.need(m)
                    m = dve.did(V.tensor_reduce(dst[:, t, :], a.rearrange("p (n d) -> p n d", d=d), AXX, ALU.add))
                return m

            def roots(x, inv, after):
                dve.need(after)
                if isinstance(inv, float):
                    m = dve.did(V.tensor_scalar(x, x, inv, EPS, ALU.mult, ALU.add))
                else:
                    m = dve.did(V.tensor_tensor(x, x, inv, ALU.mult))
                    dve.need(m)
                    m = dve.did(V.tensor_scalar(x, x, EPS, None, ALU.add))
                return inv_root(x, x, x, m)

            scope()
            y, hT = cut(NT, D), cut_pair(DC, SEQ)
            mem = shaped(mixed.rearrange("p t d -> p (t d)")[:, 0:NT * D], NT, D)
            sp.engine.dma_start(mem, T["mem_2"][0].rearrange("(t p) d -> p t d", p=P)).then_inc(s_in, 16)
            mem_ready = (s_in, 64 + 32 + 16 * (l + 1))
            m = normed(mem, y, [mem_ready])
            g0 = COLS["mem2"] + l * DC
            dve.need(m)
            xm = feature_major(y, DC, hT, m, cols[:, g0:g0 + DC])
            mk = []

            def evac_kv(t, b, done):
                mk.append(evacuate(b, kvm[:, t, :], psum[b][:, :], done))
            token_linear(hT, "mem_kv", 0, 512, evac_kv, xm)
            m = sum_squares(kvm[:, :, 0:256], 4, 64, st2[:, :, 0:4], mk)
            m = roots(st2[:, :, 0:4], 1.0 / 64, m)
            kv4 = kvm[:, :, 0:256].rearrange("p t (n d) -> p t n d", n=4)
            memk_ready = head_norms(kv4, 4, 64, st2[:, :, 0:4], R("memk"), [m, rows_ready])

            pe_mem = pe.last()
            act.need(pe_mem)
            m = normed(h, y, [pe_mem, dve.last()])
            g0 = COLS["attn2"] + l * DC
            xm = feature_major(y, DC, hT, [m, pe_mem], cols[:, g0:g0 + DC])
            pj = []
            for n0 in range(0, D_IN2, 512):
                nn = min(512, D_IN2 - n0)

                def evac(t, b, done, n0=n0, nn=nn):
                    pj.append(evacuate(b, hp[:, t, n0:n0 + nn], psum[b][:, 0:nn], done))
                token_linear(hT, "in_2", n0, nn, evac, xm)
            close()
            join()
            scope()
            S = cut(2, 4, 512)
            tmp1, tmp2 = S[:, 0, 0, :], S[:, 0, 1, :]
            slot = 0
            for c0, n, d in ((C_CQ, 1, 192), (C_CKV, 1, 128), (C_KR, 1, 32), (C_FOX, 8, 64), (C_MOBA, 8, 64),
                             (C_DIFF, 16, 32), (C_MEM, 4, 64)):
                m = sum_squares(hp[:, :, c0:c0 + n * d], n, d, st[:, :, slot:slot + n], pj)
                slot += n
            m = roots(st[:, :, 0:N_SLOT], spread(const("inv_d")[:, 0:N_SLOT], 1, NT), m)
            slot = 0
            for c0, n, d, name in ((C_CQ, 1, 192, "cq"), (C_CKV, 1, 128, "ckv"), (C_KR, 1, 32, "kr"), (C_FOX, 8, 64, "fox"),
                                   (C_MOBA, 8, 64, "moba"), (C_DIFF, 16, 32, "diff"), (C_MEM, 4, 64, "memq")):
                x = hp[:, :, c0:c0 + n * d].rearrange("p t (n d) -> p t n d", n=n)
                nm = head_norms(x, n, d, st[:, :, slot:slot + n], R(name), [m, rows_ready])
                slot += n

            cT = cut(3, SEQ)
            qa, kva, ka = cut(NT, 384), cut(NT, 512), cut(NT, 384)
            marks = []
            for k, (c0, w) in enumerate(((0, P), (P, 64), (C_CKV, P))):
                b, mt = transposes([hp[:, t, c0:c0 + w] for t in range(NT)], [nm])
                marks.append(evacuate(b, cT[0:w, k, :], psum[b][0:w, 0:SEQ], mt))
            (w3,), wm = weights.take("mla")
            am = []
            for t in range(NT):
                b = banks.take(pe)
                pe.need(wm, marks)
                E.matmul(psum[b][:, 0:384], cT[:, 0, t * P:(t + 1) * P], w3[:, 0:384], start=True, stop=False)
                done = pe.did(E.matmul(psum[b][:, 0:384], cT[0:64, 1, t * P:(t + 1) * P], w3[0:64, 384:768], start=False, stop=True))
                am.append(evacuate(b, qa[:, t, :], psum[b][:, 0:384], done))
                b = banks.take(pe)
                done = pe.did(E.matmul(psum[b][:, :], cT[:, 2, t * P:(t + 1) * P], w3[:, 768:1280], start=True, stop=True))
                am.append(evacuate(b, kva[:, t, :], psum[b][:, :], done))
            weights.done(done)
            qa4 = qa.rearrange("p t (n d) -> p t n d", n=4)
            kv4a = kva.rearrange("p t (n d) -> p t n d", n=4)
            ka4 = ka.rearrange("p t (n d) -> p t n d", n=4)
            for t in range(NT):
                pool.need(am, dve.last())
                m1 = pool.did(G.tensor_tensor(sq[:, t * 1024:t * 1024 + 384], qa[:, t, :], qa[:, t, :], ALU.mult))
                m2 = pool.did(G.tensor_tensor(sq[:, t * 1024 + 384:t * 1024 + 896], kva[:, t, :], kva[:, t, :], ALU.mult))
                dve.need(m1, m2)
                q3 = sq[:, t * 1024:t * 1024 + 384].rearrange("p (n d) -> p n d", n=4)
                k3 = sq[:, t * 1024 + 384:t * 1024 + 896].rearrange("p (n d) -> p n d", n=4)
                dve.did(V.tensor_reduce(st2[:, t, 0:4], q3[:, :, 0:32], AXX, ALU.add))
                dve.did(V.tensor_reduce(st2[:, t, 4:8], q3[:, :, 32:96], AXX, ALU.add))
                m = dve.did(V.tensor_reduce(st2[:, t, 8:12], k3[:, :, 0:64], AXX, ALU.add))
            dve.need(m)
            dve.did(V.tensor_scalar(st2[:, :, 0:4], st2[:, :, 0:4], 1.0 / 32, EPS, ALU.mult, ALU.add))
            m = dve.did(V.tensor_scalar(st2[:, :, 4:12], st2[:, :, 4:12], 1.0 / 64, EPS, ALU.mult, ALU.add))
            m = inv_root(st2[:, :, 0:12], st2[:, :, 0:12], st2[:, :, 0:12], m)
            gq = R("mla_q").rearrange("p (n d) -> p n d", n=4)
            gk = R("mla_k").rearrange("p (n d) -> p n d", n=4)
            for t in range(NT):
                dve.need(m)
                dve.did(V.tensor_tensor(qa4[:, t, :, 0:32], qa4[:, t, :, 0:32], spread(st2[:, t, 0:4], 2, 32), ALU.mult))
                dve.did(V.tensor_tensor(qa4[:, t, :, 32:96], qa4[:, t, :, 32:96], spread(st2[:, t, 4:8], 2, 64), ALU.mult))
                e = dve.did(V.tensor_tensor(ka4[:, t, :, 32:96], kv4a[:, t, :, 0:64], spread(st2[:, t, 8:12], 2, 64), ALU.mult))
                dve.need(e)
                dve.did(V.tensor_tensor(qa4[:, t], qa4[:, t], gq, ALU.mult))
                e = dve.did(V.tensor_tensor(ka4[:, t, :, 32:96], ka4[:, t, :, 32:96], gk, ALU.mult))
                rope(qa4[:, t, :, 0:32], qa4[:, t, :, 0:32], 4, ROT_A, ROT_C, t, tmp1, tmp2, e)
                kr = hp[:, t, C_KR:C_KR + 32].rearrange("p (n d) -> p n d", n=1)
                e = rope(kr, kr, 1, ROT_A, ROT_C, t, tmp1, tmp2, nm)
                dve.need(e)
                e = dve.did(V.tensor_copy(ka4[:, t, :, 0:32], spread(hp[:, t, C_KR:C_KR + 32], 1, 4)))
                mo = hp[:, t, C_MOBA:C_MOBA + 512].rearrange("p (n d) -> p n d", n=8)[:, :, 0:2 * ROT_M]
                rope(mo, mo, 8, ROT_M, ROT_C + ROT_A, t, tmp1, tmp2, nm)
                di = hp[:, t, C_DIFF:C_DIFF + 512].rearrange("p (n d) -> p n d", n=16)[:, :, 0:2 * ROT_D]
                qk_ready = rope(di, di, 16, ROT_D, ROT_C + ROT_A + ROT_M, t, tmp1, tmp2, nm)

            fx = cut(NT, 4)
            lf = cut(NT, 4)
            dve.need(pj, rows_ready)
            m = dve.did(V.tensor_tensor(fx, hp[:, :, C_FF:C_FF + 4], spread(R("fox_b"), 1, NT), ALU.add))
            dve.need(m)
            m = dve.did(V.scalar_tensor_tensor(lf, fx, -1.0, fx, ALU.mult, ALU.max))
            act.need(m)
            m = act.did(A.activation(lf, lf, ACT.Exp, scale=-1.0))
            act.need(m)
            m = act.did(A.activation(lf, lf, ACT.Ln, bias=1.0))
            dve.need(m)
            m = dve.did(V.scalar_tensor_tensor(lf, fx, 0.0, lf, ALU.min, ALU.subtract))
            tri = const("causal3")
            b = banks.take(pe)
            pe.need(m)
            for t in range(NT):
                for s_ in range(t + 1):
                    mm = E.matmul(psum[b][:, t * 4:t * 4 + 4], tri[:, (t + s_) * P:(t + s_ + 1) * P], lf[:, s_, :],
                                  start=(s_ == 0), stop=(s_ == t))
            done = pe.did(mm)
            fc = cut(NT, 4)
            dve.need(done)
            fc_ready = dve.did(V.tensor_copy(fc, psum[b][:, 0:8].rearrange("p (t n) -> p t n", t=NT)))
            banks.free(b, fc_ready)
            X = cut(4, 384)
            gb = cut(4, NT, P)
            m = dve.did(V.tensor_copy(gb, spread(lf.rearrange("p t h -> p h t"), 3, P)))
            for hh in range(4):
                b = banks.take(pe)
                pe.need(m)
                E.matmul(psum[b][:, 0:SEQ], gb[:, hh, 0, :], tri[:, 0:SEQ], start=True, stop=False)
                done = pe.did(E.matmul(psum[b][:, P:SEQ], gb[:, hh, 1, :], tri[:, SEQ:384], start=False, stop=True))
                dve.need(done, fc_ready)
                cn = const("causal_neg")
                dve.did(V.scalar_tensor_tensor(X[:, hh, 0:P], psum[b][:, 0:P], fc[:, 0, hh:hh + 1], cn[:, 0:P], ALU.subtract, ALU.subtract))
                X_ready = dve.did(V.scalar_tensor_tensor(X[:, hh, P:384], psum[b][:, 0:SEQ], fc[:, 1, hh:hh + 1], cn[:, P:384],
                                                         ALU.subtract, ALU.subtract))
                banks.free(b, X_ready)
            lam_init = 0.8 - 0.6 * float(np.exp(-0.3 * l))
            lm = cut(68)
            lv = R("lambda").rearrange("p (a d) -> p a d", a=4)
            lm3 = lm[:, 0:64].rearrange("p (a d) -> p a d", a=2)
            m = dve.did(V.tensor_tensor(lm3, lv[:, 0::2, :], lv[:, 1::2, :], ALU.mult))
            dve.need(m)
            m = dve.did(V.tensor_reduce(lm[:, 64:66], lm3, AXX, ALU.add))
            act.need(m)
            m = act.did(A.activation(lm[:, 64:66], lm[:, 64:66], ACT.Exp))
            dve.need(m)
            m = dve.did(V.tensor_tensor(lm[:, 66:67], lm[:, 64:65], lm[:, 65:66], ALU.subtract))
            dve.need(m)
            lam_ready = dve.did(V.tensor_scalar(lm[:, 66:67], lm[:, 66:67], lam_init, -1.0, ALU.add, ALU.mult))

            QK = cut(2, 8, SEQ)
            mx, den = cut(2, NT, 4), cut(2, 4, 4)
            both_d = gb.rearrange("p h t n -> p (h t n)")
            d1, d2 = [shaped(both_d[:, k * 512:(k + 1) * 512], NT, 256) for k in range(2)]

            def group(src, d, scale, v, v_ready, finish, **more):
                def prep(i, free):
                    act.need(free)
                    dve.need(free)
                    return heads_transposed(src, 8, d, QK[:, i, :, :], [qk_ready, memk_ready])
                return dict(prepare=prep, scale=scale, v=v, v_ready=v_ready, finish=finish,
                            q=lambda i, hh: QK[0:d, i, hh, :], k=lambda i, hh: QK[0:d, i, 4 + hh, :], **more)

            def hp_v(c0):
                return lambda hh, s_: hp[:, s_, c0 + hh * 64:c0 + (hh + 1) * 64]

            def finish_diff(bank, rden):
                m = scaled_into(d2)(bank, rden)
                dve.need(m, lam_ready)
                m = dve.did(V.scalar_tensor_tensor(d1, d2, lm[:, 66:67], d1, ALU.mult, ALU.add))
                dve.need(m)
                m = dve.did(V.tensor_tensor(d2, d1, d1, ALU.mult))
                dve.need(m)
                m = dve.did(V.tensor_reduce(st2[:, :, 0:4], d2.rearrange("p t (n d) -> p t n d", n=4), AXX, ALU.add))
                m = roots(st2[:, :, 0:4], 1.0 / 64, m)
                dve.need(m)
                for t in range(NT):
                    m = dve.did(V.tensor_tensor(d1[:, t, :].rearrange("p (n d) -> p n d", n=4), d1[:, t, :].rearrange("p (n d) -> p n d", n=4),
                                                spread(st2[:, t, 0:4], 2, 64), ALU.mult))
                dve.need(m)
                return dve.did(V.scalar_tensor_tensor(mixed[:, :, 768:1024], d1, 1.0 - lam_init, spread(R("sub"), 1, NT),
                                                      ALU.mult, ALU.mult))

            cneg = const("causal_neg")
            groups = [
                group(lambda x, t: hp[:, t, C_FOX + x * 64:C_FOX + (x + 1) * 64], 64, 64 ** -0.5, hp_v(C_FOX + 512), pj,
                      scaled_into(mixed[:, :, 256:512]), causal=True, bias=X, bias_ready=X_ready),
                group(lambda x, t: hp[:, t, C_MOBA + x * 64:C_MOBA + (x + 1) * 64], 64, 64 ** -0.5, hp_v(C_MOBA + 512), pj,
                      scaled_into(mixed[:, :, 512:768]), causal=True, mask=cneg),
                group(lambda x, t: (qa4 if x < 4 else ka4)[:, t, x % 4, :], 96, 96 ** -0.5,
                      lambda hh, s_: kva[:, s_, hh * P + 64:(hh + 1) * P], am, scaled_into(mixed[:, :, 0:256]), causal=True, mask=cneg),
            ]
            for pair in range(2):
                groups.append(group(lambda x, t, pair=pair: hp[:, t, C_DIFF + (2 * x + pair) * 32:C_DIFF + (2 * x + pair + 1) * 32],
                                    32, 32 ** -0.5, hp_v(C_DIFF + 512), pj, finish_diff if pair else scaled_into(d1),
                                    causal=True, mask=cneg))
            groups.append(group(lambda x, t: hp[:, t, C_MEM + x * 64:C_MEM + (x + 1) * 64] if x < 4 else
                                kvm[:, t, (x - 4) * 64:(x - 3) * 64], 64, 64 ** -0.5,
                                lambda hh, s_: kvm[:, s_, 256 + hh * 64:256 + (hh + 1) * 64], mk,
                                scaled_into(mixed[:, :, 1024:1280]), causal=False))
            attention(groups, S, PTb, mx, den)
            m = dve.last()
            close()
            join()
            scope()
            mT = cut_pair(MIX2 // P, SEQ)
            m = feature_major(mixed, MIX2 // P, mT, [m])
            held, done = deep_linear(mT, MIX2 // P, "o_2", m)
            close()
            for i, b in enumerate(held):
                v = h[:, i // 2, (i % 2) * 512:(i % 2 + 1) * 512]
                dve.need(done[i])
                m = dve.did(V.tensor_tensor(v, v, psum[b][:, :], ALU.add))
                banks.free(b, m)

        def feed_forward_2(l):
            y, hT = cut(NT, D), cut_pair(DC, SEQ)
            aT = cut_pair(DFF2 // P, SEQ)
            pad = cut(2, 2, SEQ + 2)
            cv = cut(3, 2, SEQ)
            m = normed(h, y, [dve.last()])
            g0 = COLS["ffn2"] + l * DC
            xm = feature_major(y, DC, hT, m, cols[:, g0:g0 + DC])
            zeroed = pool.did(G.memset(pad[:, :, :, 0:2], 0.0))
            pad_free, cv_free = [zeroed] * 2, [None] * 3
            cw, cb = COLS["fconv_w"] + l * 66, COLS["fconv_b"] + l * 22
            ready, gated = [], {}

            def evac_gate(c, b, done):
                i, q = (c // 2) % 3, (c // 2) % 2
                act.need(done, pad_free[q])
                m = act.did(A.copy(pad[:, q, :, 2:], psum[b][:, :].rearrange("p (k n) -> p k n", k=2)))
                banks.free(b, m)
                ends = [None, None]
                for k in range(3):
                    for j in range(2):
                        tap = cols[:, cw + k * 22 + c + j:cw + k * 22 + c + j + 1]
                        dve.need(m, cv_free[i], ends[j])
                        src = pad[:, q, j, k:k + SEQ]
                        if k == 0:
                            ends[j] = dve.did(V.tensor_scalar(cv[:, i, j, :], src, tap, cols[:, cb + c + j:cb + c + j + 1],
                                                              ALU.mult, ALU.add))
                        else:
                            ends[j] = dve.did(V.scalar_tensor_tensor(cv[:, i, j, :], src, tap, cv[:, i, j, :], ALU.mult, ALU.add))
                pad_free[q] = ends[1]
                act.need(ends)
                gated[c] = i, act.did(A.activation(cv[:, i, :, :], cv[:, i, :, :], ACT.Silu))

            def evac_up(c, b, done):
                i, m = gated[c]
                dve.need(done, m)
                m = dve.did(V.tensor_tensor(cv[:, i, :, :], cv[:, i, :, :], psum[b][:, :].rearrange("p (k n) -> p k n", k=2), ALU.mult))
                banks.free(b, m)
                act.need(m)
                hi = act.did(A.copy(aT[0][:, c:c + 2, :], cv[:, i, :, :]))
                dve.need(m, hi)
                cv_free[i] = dve.did(V.tensor_tensor(aT[1][:, c:c + 2, :], cv[:, i, :, :], aT[0][:, c:c + 2, :].bitcast(F32), ALU.subtract))
                ready.append(cv_free[i])
            for n0 in range(0, DFF2, 256):
                feature_linear(hT, "ff_gate", n0, evac_gate, xm)
                feature_linear(hT, "ff_up", n0, evac_up, xm)
            held, done = deep_linear(aT, DFF2 // P, "down_2", ready)
            for i, b in enumerate(held):
                v = h[:, i // 2, (i % 2) * 512:(i % 2 + 1) * 512]
                dve.need(done[i])
                m = dve.did(V.tensor_tensor(v, v, psum[b][:, :], ALU.add))
                banks.free(b, m)

        loaded_all = [loaded]
        for layer in range(2):
            rows_ready = load_rows(layer)
            scope()
            held, done, mix, tmp = (mixer_ab if layer == 0 else mixer_c)(rows_ready)
            add_normed(held, done, row(layer, "post"), mix, tmp, row(1, "b_o") if layer else None, rows_ready)
            join()
            close()
            scope()
            feed_forward_1(layer, rows_ready)
            join()
            close()
            scope()
            gated_add(layer)
            join()
            close()
        for l in range(2):
            rows_ready = load_rows(2 + l)
            scope()
            mixer_2(l, rows_ready)
            join()
            close()
            scope()
            feed_forward_2(l)
            join()
            close()
        sp.need(dve.last())
        sp.engine.dma_start(out[0].rearrange("(t p) d -> p t d", p=P), h[:, :, :]).then_inc(s_out, 16)
        sp.engine.wait_ge(s_out, 16)


WEIGHTS = ["x", "p", "w_in_ab", "w_out_ab", "w_qkv_c", "w_o_c", "w_up", "w_down", "w_ple", "w_ple_gate", "mem_2",
           "w_in_2", "mla_w_uq_2", "mla_w_ukv_2", "mem_w_kv_2", "w_o_2", "ffn_w_gate_2", "ffn_w_up_2", "ffn_w_down_2"]


def columns(v):
    return np.ascontiguousarray(v.reshape(-1, P).T)


def kernel(**inputs):
    import concourse.bacc as bacc
    from concourse.bass_utils import run_bass_kernel_spmd

    inputs = {k: np.asarray(v) for k, v in inputs.items()}
    f = np.float32
    cols = [columns(inputs["norm_gains"][layer, which]) for layer in range(2) for which in (0, 2)]
    cols += [columns(inputs[name][l]) for name in ("attn_norm_2", "ffn_norm_2", "mem_norm_2") for l in range(2)]
    cols.append(inputs["conv_a"][0].reshape(4, 12, P).transpose(2, 1, 0).reshape(P, 48))
    cols += [inputs["ffn_conv_w_2"][l].reshape(3, 22, P).transpose(2, 0, 1).reshape(P, 66) for l in range(2)]
    cols += [columns(inputs["ffn_conv_b_2"][l]) for l in range(2)]
    zeros4 = np.zeros(4, f)
    rows = np.zeros((4, ROW_MAX), f)

    def put(layer, name, *values):
        a, n = ROWS[layer][name]
        rows[layer, a:a + n] = np.concatenate([v.reshape(-1) for v in values])

    for layer in range(2):
        put(layer, "post", inputs["norm_gains"][layer, 1])
        put(layer, "post_ff", inputs["norm_gains"][layer, 3])
    put(0, "norm_a", *[inputs["norm_a"][0]] * 4)
    put(0, "norm_b", inputs["norm_b"][0])
    put(0, "gate_bias", zeros4, inputs["dt_bias"][0], inputs["i_bias_b"][0], inputs["f_bias_b"][0])
    put(0, "a_log", inputs["a_log"][0])
    put(1, "b_qkv", inputs["b_qkv_c"][0])
    put(1, "b_o", inputs["b_o_c"][0])
    put(1, "sinks", inputs["sinks_c"][0])
    for l in range(2):
        i = {k: inputs[k + "_2"][l] for k in ("mla_cq_norm", "mla_ckv_norm", "mla_q_norm", "mla_k_norm", "fox_q_norm",
                                              "fox_k_norm", "moba_q_norm", "moba_k_norm", "diff_q_norm", "diff_k_norm",
                                              "diff_sub_norm", "mem_q_norm", "mem_k_norm", "fox_b_f", "diff_lambda")}
        put(2 + l, "cq", i["mla_cq_norm"])
        put(2 + l, "ckv", i["mla_ckv_norm"])
        put(2 + l, "kr", i["mla_k_norm"][:32])
        put(2 + l, "fox", *[i["fox_q_norm"]] * 4, *[i["fox_k_norm"]] * 4)
        put(2 + l, "moba", *[i["moba_q_norm"]] * 4, *[i["moba_k_norm"]] * 4)
        put(2 + l, "diff", *[i["diff_q_norm"]] * 8, *[i["diff_k_norm"]] * 8)
        put(2 + l, "memq", *[i["mem_q_norm"]] * 4)
        put(2 + l, "memk", *[i["mem_k_norm"]] * 4)
        put(2 + l, "mla_q", *[i["mla_q_norm"]] * 4)
        put(2 + l, "mla_k", *[i["mla_k_norm"][32:]] * 4)
        put(2 + l, "sub", *[i["diff_sub_norm"]] * 4)
        put(2 + l, "fox_b", i["fox_b_f"])
        put(2 + l, "lambda", i["diff_lambda"])
    arrays = {name: np.ascontiguousarray(inputs[name]) for name in WEIGHTS}
    arrays["cols"] = np.ascontiguousarray(np.concatenate(cols, 1))
    arrays["rows"] = rows
    arrays["consts"] = constants()
    arrays["positions"] = np.ascontiguousarray(np.concatenate(
        [inputs[n].reshape(NT, P).T for n in ("positions", "positions_2")], 1))

    nc = bacc.Bacc("TRN2", target_bir_lowering=False, num_devices=1)
    arrays = {f"in_{k}": v for k, v in arrays.items()}
    T = {k[3:]: nc.dram_tensor(k, v.shape, bass.mybir.dt.from_np(v.dtype), kind="ExternalInput").ap() for k, v in arrays.items()}
    out = nc.dram_tensor("out_0_dram", (1, SEQ, D), F32, kind="ExternalOutput").ap()
    program(nc, T, out)
    result = run_bass_kernel_spmd(nc, [arrays], core_ids=[0])
    return result.results[0]["out_0_dram"]
```

```python
from contextlib import ExitStack

import numpy as np

import concourse.bass as bass
import concourse.mybir as mybir

F32 = mybir.dt.float32
I32 = mybir.dt.int32
F32R = mybir.dt.float32r
ACT = mybir.ActivationFunctionType
ALU = mybir.AluOpType
AXX = mybir.AxisListType.X

P = 128
SEQ = 256
NT = SEQ // P
D = 1024
DC = D // P
EPS = 1e-6
BIG = 1e30
TWO_PI = 2 * np.pi

QKV_A = 1536
COL_BETA = QKV_A
COL_Z = QKV_A + 8
COL_QB = COL_Z + 512
COL_VB = COL_QB + 1024
COL_IF = COL_VB + 512
COL_O = COL_IF + 8
CH, CKV, CHD = 16, 4, 64
DFF1 = 4096
DFF2 = 2816
MIX2 = 1280
ROT_C, ROT_A, ROT_M, ROT_D = 32, 16, 8, 4
D_IN2 = 2916
C_CQ, C_CKV, C_KR, C_FOX, C_FF, C_MOBA, C_DIFF, C_MEM = 0, 192, 320, 352, 1120, 1124, 1892, 2660
OUT_2 = [2, 0, 4, 6, 8]

FEATURES_AB = [("qkv_a", 0), ("qkv_a", 256), ("qk_b", COL_QB), ("qkv_a", 512), ("qk_b", COL_QB + 256), ("qkv_a", 768),
               ("qk_b", COL_QB + 512), ("qkv_a", 1024), ("qk_b", COL_QB + 768), ("qkv_a", 1280)]

OUT_AB = [4, 6, 0, 2]

COLS = {}
_at = 0
for _name, _n in (("pre1", 2 * 2 * DC), ("attn2", 2 * DC), ("ffn2", 2 * DC), ("mem2", 2 * DC),
                  ("conv_a", 12 * 4), ("fconv_w", 2 * 3 * 22), ("fconv_b", 2 * 22)):
    COLS[_name] = _at
    _at += _n
N_COLS = _at

ROWS = [dict(), dict(), dict(), dict()]
_parts = [
    (("post", D), ("post_ff", D), ("norm_a", 512), ("norm_b", 512), ("gate_bias", 16), ("a_log", 4)),
    (("post", D), ("post_ff", D), ("b_qkv", 1536), ("b_o", D), ("sinks", CH)),
    (("cq", 192), ("ckv", 128), ("kr", 32), ("fox", 512), ("moba", 512), ("diff", 512), ("memq", 256),
     ("memk", 256), ("mla_q", 384), ("mla_k", 256), ("sub", 256), ("fox_b", 4), ("lambda", 128)),
]
_parts.append(_parts[2])
ROW_LEN = []
for _l, _p in enumerate(_parts):
    _at = 0
    for _name, _n in _p:
        ROWS[_l][_name] = (_at, _n)
        _at += _n
    ROW_LEN.append(_at)
ROW_MAX = max(ROW_LEN)

CONST = {}
_at = 0
for _name, _n in (("ident", P), ("causal3", 384), ("causal_neg", 384), ("window_neg", 384),
                  ("freq", 60), ("inv_d", 48), ("sign8", 8), ("level", 7 * P), ("select", 8 * P)):
    CONST[_name] = (_at, _n)
    _at += _n
N_CONST = _at
N_KEPT = CONST["sign8"][0]
SLOT_D = [192, 128, 32] + [64] * 8 + [64] * 8 + [32] * 16 + [64] * 4
N_SLOT = len(SLOT_D)


def constants():
    c = np.zeros((P, N_CONST), np.float32)

    def put(name, value):
        a, n = CONST[name]
        c[:, a:a + n] = np.asarray(value, np.float32).reshape(value.shape[0], -1)

    i = np.arange(P)
    upper = (i[:, None] <= i[None, :]).astype(np.float32)
    one, zero = np.ones((P, P), np.float32), np.zeros((P, P), np.float32)
    put("ident", np.eye(P, dtype=np.float32))
    put("causal3", np.concatenate([upper, one, upper], 1))
    lower_neg = np.where(i[None, :] <= i[:, None], 0.0, -BIG)
    prev_neg = np.where(i[None, :] > i[:, None], 0.0, -BIG)
    put("causal_neg", np.concatenate([lower_neg, zero, lower_neg], 1))
    put("window_neg", np.concatenate([lower_neg, prev_neg, lower_neg], 1))
    levels = []
    for n in range(7):
        s = 1 << n
        e, k = i[:, None], i[None, :]
        levels.append(((e // (2 * s) == k // (2 * s)) & (e % (2 * s) < s) & (k % (2 * s) >= s)))
    put("level", np.concatenate(levels, 1))
    sel = np.zeros((P, 8, P))
    for h in range(8):
        sel[h, h] = 1
    put("select", sel)
    f32 = np.float32
    freq = [f32(theta) ** (-np.arange(0, r, dtype=f32) / f32(r)) for theta, r in
            ((10000.0, ROT_C), (500000.0, ROT_A), (500000.0, ROT_M), (500000.0, ROT_D))]
    put("freq", np.tile(np.concatenate(freq)[None], (P, 1)))
    put("sign8", np.tile(np.array([1.0] * 4 + [-1.0] * 4)[None], (P, 1)))
    inv = np.zeros(48)
    inv[:N_SLOT] = 1.0 / np.array(SLOT_D)
    put("inv_d", np.tile(inv[None], (P, 1)))
    return c


class Line:

    def __init__(self, engine, sem):
        self.engine, self.sem, self.count, self.waited = engine, sem, 0, {}

    def need(self, *marks):
        for m in marks:
            if m is None:
                continue
            if isinstance(m, list):
                self.need(*m)
                continue
            sem, value = m
            if self.waited.get(id(sem), 0) < value:
                self.engine.wait_ge(sem, value)
                self.waited[id(sem)] = value
        return self.engine

    def did(self, instruction):
        instruction.then_inc(self.sem, 1)
        self.count += 1
        return self.sem, self.count

    def last(self):
        return (self.sem, self.count) if self.count else None


class Banks:

    def __init__(self, banks):
        self.banks, self.free_at, self.turn, self.held = banks, [None] * len(banks), 0, [False] * len(banks)

    def take(self, pe):
        while self.held[self.turn]:
            self.turn = (self.turn + 1) % len(self.banks)
        b = self.turn
        self.turn = (b + 1) % len(self.banks)
        self.held[b] = True
        pe.need(self.free_at[b])
        return b

    def free(self, b, *marks):
        assert self.held[b]
        self.held[b], self.free_at[b] = False, list(marks)


class Weights:

    def __init__(self, sp, act, dve, plan, raw, high, low, width, sems):
        self.sp, self.act, self.dve, self.plan = sp, act, dve, plan
        self.raw, self.high, self.low, self.width, self.sems = raw, high, low, width, sems
        self.n_raw, self.n_half = raw.shape[1] // width, high.shape[1] // (width // 2)
        self.landed = [0] * self.n_raw
        self.raw_free, self.half_free = {}, {}
        self.arrived, self.split_mark = {}, {}
        self.parts = [(j, part) for j, p in enumerate(plan) for part in p["parts"]]
        self.first_part, n = [], 0
        for p in plan:
            self.first_part.append(n)
            n += len(p["parts"])
        self.next_load = self.next_split = self.next_take = 0

    def raw_slot(self, j):
        a = (j % self.n_raw) * self.width
        return self.raw[:, a:a + self.plan[j]["size"]]

    def half_slots(self, n):
        k, w = self.parts[n][1](self.raw_slot(self.parts[n][0])).shape[1:]
        a = (n % self.n_half) * (self.width // 2)
        return [x[:, a:a + k * w].rearrange("p (k n) -> p k n", k=k) for x in (self.high, self.low)]

    def ahead(self, splits=True):
        moved = True
        while moved:
            moved = False
            j = self.next_load
            if j < len(self.plan) and (j < self.n_raw or j - self.n_raw in self.raw_free):
                s = j % self.n_raw
                self.sp.need(self.raw_free.get(j - self.n_raw))
                for dst, src in self.plan[j]["pieces"](self.raw_slot(j)):
                    self.sp.engine.dma_start(dst, src).then_inc(self.sems[s], 16)
                    self.landed[s] += 16
                self.arrived[j] = (self.sems[s], self.landed[s])
                self.next_load += 1
                moved = True
            n = self.next_split
            if splits and n < len(self.parts) and self.parts[n][0] < self.next_load and (
                    n < self.n_half or n - self.n_half in self.half_free):
                j, part = self.parts[n]
                raw = part(self.raw_slot(j))
                high, low = self.half_slots(n)
                free = self.half_free.get(n - self.n_half)
                self.act.need(self.arrived[j], free)
                m = self.act.did(self.act.engine.copy(high, raw))
                self.dve.need(m, self.arrived[j], free)
                m = self.dve.did(self.dve.engine.tensor_tensor(low, raw, high.bitcast(F32), ALU.subtract))
                self.raw_free[j] = self.split_mark[n] = m
                if n + 1 < len(self.parts) and self.parts[n + 1][0] == j:
                    del self.raw_free[j]
                self.next_split += 1
                moved = True

    def take(self, key):
        j = self.next_take
        p = self.plan[j]
        assert p["key"] == key, (p["key"], key)
        self.next_take += 1
        self.ahead()
        if not p["parts"]:
            return self.raw_slot(j), self.arrived[j]
        n = self.first_part[j]
        return [(self.half_slots(n + i), self.split_mark[n + i]) for i in range(len(p["parts"]))]

    def done(self, mark, part=0):
        j = self.next_take - 1
        if self.plan[j]["parts"]:
            self.half_free[self.first_part[j] + part] = mark
        else:
            self.raw_free[j] = mark
        self.ahead()


def panel(key, w, k0, kc, n0, nn, by_columns=False):
    def view(slot):
        return slot.rearrange("p (k n) -> p k n", k=kc)

    def pieces(slot):
        return [(view(slot), w[k0 * P:(k0 + kc) * P, n0:n0 + nn].rearrange("(k p) n -> p k n", p=P))]
    if by_columns:
        parts = [lambda slot, i=i: view(slot)[:, :, i * nn // 2:(i + 1) * nn // 2] for i in range(2)]
    else:
        parts = [lambda slot, i=i: view(slot)[:, i * kc // 2:(i + 1) * kc // 2, :] for i in range(2)]
    return dict(key=(key, k0, n0), pieces=pieces, size=kc * nn, parts=parts)


def by_features(key, w, n0, n1):
    return [panel(key, w, 0, DC, n, 256, True) for n in range(n0, n1, 256)]


def by_tokens(key, w, n0, n1):
    return [panel(key, w, k, 4, n, min(512, n1 - n)) for n in range(n0, n1, 512) for k in (0, 4)]


def deep(key, w, chunks):
    return [panel(key, w, k, 2, 0, D) for k in chunks]


def weight_plan(T):
    w = T["w_in_ab"][0]

    def gate_pieces(slot):
        v = slot.rearrange("p (k n) -> p k n", k=DC)
        return [(v[:, :, i * 8:i * 8 + 8], w[:, c:c + 8].rearrange("(k p) n -> p k n", p=P))
                for i, c in enumerate((COL_BETA, COL_IF))]
    plan = [dict(key="gates", pieces=gate_pieces, size=DC * 16, parts=[lambda slot: slot.rearrange("p (k n) -> p k n", k=DC)])]
    for key, n0 in FEATURES_AB:
        plan += by_features(key, w, n0, n0 + 256)
    for c in (COL_Z, COL_VB, COL_O):
        plan += by_tokens("zvo", w, c, c + 512)
    plan += deep("out_ab", T["w_out_ab"][0], OUT_AB)
    for layer in range(2):
        if layer:
            plan += sum([by_tokens("qkv_c", T["w_qkv_c"][0], n, n + 512) for n in (1024, 0, 512)], [])
            plan += deep("o_c", T["w_o_c"][0], range(0, DC, 2))
        plan += by_features("up", T["w_up"][layer], 0, DFF1) + deep("down", T["w_down"][layer], range(0, DFF1 // P, 2))
        plan += deep("ple", T["w_ple"][layer], [0]) + deep("ple_gate", T["w_ple_gate"][layer], range(0, DC, 2))
    for l in range(2):
        uq, ukv = T["mla_w_uq_2"][l], T["mla_w_ukv_2"][l]

        def mla_pieces(slot, uq=uq, ukv=ukv):
            return [(slot[:, 0:384], uq[0:P, :]), (slot[0:64, 384:768], uq[P:192, :]), (slot[:, 768:1280], ukv)]
        plan += by_tokens("mem_kv", T["mem_w_kv_2"][l], 0, 512) + by_tokens("in_2", T["w_in_2"][l], 0, 2048)
        plan.append(dict(key="mla", pieces=mla_pieces, size=1280, parts=[]))
        plan += by_tokens("in_2", T["w_in_2"][l], 2048, D_IN2)
        plan += deep("o_2", T["w_o_2"][l], OUT_2)
        for n in range(0, DFF2, 256):
            plan += by_features("ff_gate", T["ffn_w_gate_2"][l], n, n + 256) + by_features("ff_up", T["ffn_w_up_2"][l], n, n + 256)
        plan += deep("down_2", T["ffn_w_down_2"][l], range(0, DFF2 // P, 2))
    return plan


class Out:

    def __init__(self, key, buffers, slots, bias=None):
        self.key, self.buffers, self.slots, self.bias = key, buffers, slots, bias


def spread(ap, axis, n):
    shape = list(ap.shape)
    shape.insert(axis, n)
    return ap.unsqueeze(axis).to_broadcast(shape)


def skewed(stages, n):
    for step in range(n + max(lag for lag, _ in stages)):
        for lag, stage in stages:
            if 0 <= step - lag < n:
                stage(step - lag)




def program(nc, T, out):
    ctx = ExitStack()
    with ctx:
        def sbuf(name, shape, dt=F32):
            return ctx.enter_context(nc.sbuf_tensor(name, shape, dt))

        def sem(name):
            return ctx.enter_context(nc.semaphore(name))

        pe = Line(nc.tensor, sem("pe_done"))
        dve = Line(nc.vector, sem("dve_done"))
        act = Line(nc.scalar, sem("act_done"))
        pool = Line(nc.gpsimd, sem("pool_done"))
        sp = Line(nc.sync, sem("sp_done"))
        V, A, G, E = nc.vector, nc.scalar, nc.gpsimd, nc.tensor

        consts = sbuf("consts", [P, N_KEPT])
        cols = sbuf("cols", [P, N_COLS])
        rows = sbuf("rows", [P, ROW_MAX])
        h = sbuf("h", [P, NT, D])
        trig = sbuf("trig", [P, 2, NT, 60])
        junk = sbuf("junk", [P, D], mybir.dt.bfloat16)
        WIDTH = 8 * 256
        N_RAW, N_HALF = 3, 2
        raw = sbuf("weights_raw", [P, N_RAW * WIDTH])
        high, low = [sbuf("weights_" + n, [P, N_HALF * WIDTH], F32R) for n in ("high", "low")]
        psum = [ctx.enter_context(nc.psum_tensor(f"bank{b}", [P, 512], F32)) for b in range(8)]
        banks = Banks(psum)
        weights = Weights(sp, act, dve, weight_plan(T), raw, high, low, WIDTH, [sem(f"raw{s}_landed") for s in range(N_RAW)])
        s_in, s_later, s_rows, s_mem, s_p, s_out = [sem(n + "_landed") for n in ("inputs", "later_inputs", "rows", "memory", "p", "output")]

        def const(name):
            a, w = CONST[name]
            return consts[:, a:a + w] if a < N_KEPT else consts_ab[:, a - N_KEPT:a - N_KEPT + w]

        ident = const("ident")
        ones = const("causal3")[:, P:2 * P]

        scopes, n_cut = {"left": [], "right": []}, [0]

        def shaped(v, *shape):
            names = "abcd"[:len(shape)]
            return v if len(shape) == 1 else v.rearrange("p (%s) -> p %s" % (" ".join(names), " ".join(names)),
                                                         **{k: n for k, n in zip(names, shape)})

        def cut(*shape, dt=F32, side="left"):
            n_cut[0] += 1
            n = int(np.prod(shape))
            return shaped(scopes[side][-1].enter_context(nc.sbuf_tensor(f"buffer{n_cut[0]}", [P, n], dt, side=side))[:, :], *shape)

        def right(*shape, dt=F32):
            return cut(*shape, dt=dt, side="right")

        def cut_pair(*shape):
            return cut(*shape, dt=F32R), cut(*shape, dt=F32R)

        def scope(side="left"):
            scopes[side].append(ExitStack())

        def close(side="left"):
            scopes[side].pop().close()

        def copy_on(line, dst, src, *after):
            line.need(*after)
            if line is act:
                return act.did(A.copy(dst, src))
            return line.did(line.engine.tensor_copy(dst, src))

        def inv_root(ms, root, inv, after):
            act.need(after)
            m = act.did(A.activation(root, ms, ACT.Sqrt))
            dve.need(m)
            return dve.did(V.reciprocal(inv, root))

        def transposes(blocks, after):
            b = banks.take(pe)
            pe.need(after)
            for k, src in enumerate(blocks):
                w = src.shape[-1]
                mm = E.transpose(psum[b][0:w, k * P:(k + 1) * P], src, ident)
            return b, pe.did(mm)

        evac_turn = [0]

        def evacuate(b, dst, src, *after):
            evac_turn[0] += 1
            m = copy_on(act if evac_turn[0] % 2 else dve, dst, src, *after)
            banks.free(b, m)
            return m

        def feature_major(src, n_chunks, dst, after, gain=None, free=None):
            marks = []
            high, low = dst
            for k in range(0, n_chunks, 2):
                b, done = transposes([src[:, t, (k + i) * P:(k + i + 1) * P] for i in range(2) for t in range(NT)], after)
                bank = psum[b][:, :].rearrange("p (k n) -> p k n", k=2)
                act.need(done, free)
                if gain is None:
                    m = act.did(A.copy(high[:, k:k + 2, :], bank))
                    dve.need(m)
                    m = dve.did(V.tensor_tensor(low[:, k:k + 2, :], bank, high[:, k:k + 2, :].bitcast(F32), ALU.subtract))
                else:
                    for i in range(2):
                        m = act.did(A.activation(high[:, k + i, :], bank[:, i, :], ACT.Copy, scale=gain[:, k + i:k + i + 1]))
                    dve.need(m)
                    for i in range(2):
                        m = dve.did(V.scalar_tensor_tensor(low[:, k + i, :], bank[:, i, :], gain[:, k + i:k + i + 1],
                                                           high[:, k + i, :].bitcast(F32), ALU.mult, ALU.subtract))
                banks.free(b, m)
                marks.append(m)
            return marks

        def heads_transposed(src, n, d, dst, after):
            marks = []
            for k in range(0, n, 2):
                m_ = min(2, n - k)
                b, m = transposes([src(k + i, t) for i in range(m_) for t in range(NT)], after)
                bank = psum[b][0:d, 0:m_ * SEQ].rearrange("p (k n) -> p k n", k=m_)
                marks.append(evacuate(b, dst[0:d, k:k + m_, :], bank, m))
            return marks

        junk_written = [None]

        def square_sum(src, total, *after):
            act.need(*after, junk_written[0])
            m = act.did(A.activation(junk[:, 0:src.shape[-1]], src, ACT.Square, accum_out=total))
            junk_written[0] = m
            return m

        def rms(src, after, r=None):
            r = cut(NT) if r is None else r
            for t in range(NT):
                m = square_sum(src[:, t, :], r[:, t:t + 1], after[t])
            dve.need(m)
            m = dve.did(V.tensor_scalar(r, r, 1.0 / D, EPS, ALU.mult, ALU.add))
            return r, inv_root(r, r, r, m)

        def along_tokens(r, after):
            R = cut(2, SEQ)
            diag = cut(NT, P)
            dve.need(after)
            for t in range(NT):
                m = dve.did(V.tensor_scalar(diag[:, t, :], ident, r[:, t:t + 1], None, ALU.mult))
            b = banks.take(pe)
            pe.need(m)
            for t in range(NT):
                mm = E.matmul(psum[b][:, t * P:(t + 1) * P], ones, diag[:, t, :], start=True, stop=True)
            done = pe.did(mm)
            act.need(done)
            for k in range(2):
                m = act.did(A.copy(R[:, k, :], psum[b][:, 0:SEQ]))
            banks.free(b, m)
            return R, m

        def along_tokens_later(r, after):
            made = []

            def get():
                if not made:
                    made.append(along_tokens(r, after))
                return made[0]
            return get

        def product(out, x, w, first, last):
            (xh, xl), (wh, wl) = x, w
            E.matmul(out, xh, wh, start=first, stop=False)
            E.matmul(out, xh, wl, start=False, stop=False)
            return E.matmul(out, xl, wh, start=False, stop=last)

        def half(pair, index):
            return tuple(v[index] for v in pair)

        def token_linear(xT, key, n0, nn, evac, after, between=None):
            held = [banks.take(pe) for _ in range(NT)]
            for k0 in (0, 4):
                for i, (w, m) in enumerate(weights.take((key, k0, n0))):
                    pe.need(m, after[(k0 + 2 * i) // 2])
                    done = []
                    for t in range(NT):
                        for k in range(2):
                            c = k0 + 2 * i + k
                            mm = product(psum[held[t]][:, 0:nn], half(xT, np.s_[:, c, t * P:(t + 1) * P]),
                                         half(w, np.s_[:, k, :]), c == 0, c == DC - 1)
                        done.append(pe.did(mm))
                    weights.done(done[-1], i)
                    if k0 + 2 * i == DC - 2:
                        for t in range(NT):
                            evac(t, held[t], done[t])
                    if between:
                        between()

        def deep_panel(held, x, c0, key, k0, after, first, last):
            parts = weights.take((key, k0, 0))
            done = []
            for t, i in [(t, i) for t in range(NT) for i in range(2)] if last else [(t, i) for i in range(2) for t in range(NT)]:
                w, m = parts[i]
                pe.need(m, after)
                for side in range(2):
                    mm = product(psum[held[2 * t + side]][:, :], half(x, np.s_[:, c0 + i, t * P:(t + 1) * P]),
                                 half(w, np.s_[:, 0, side * 512:(side + 1) * 512]), first and i == 0, last and i == 1)
                    if last and i == 1:
                        done.append(pe.did(mm))
                if t == NT - 1:
                    weights.done(done[-1] if last and i else pe.did(mm), i)
            return done

        def deep_linear(xT, kc, key, after):
            held = [banks.take(pe) for _ in range(4)]
            for k0 in range(0, kc, 2):
                done = deep_panel(held, xT, k0, key, k0, after[k0 // 2], k0 == 0, k0 + 2 == kc)
            return held, done

        def feature_linear(xT, key, n0, evac, after):
            parts = weights.take((key, 0, n0))
            b = banks.take(pe)
            for i, (w, m) in enumerate(parts):
                pe.need(m)
                for k in range(DC):
                    pe.need(after[k // 2])
                    mm = product(psum[b][:, i * SEQ:(i + 1) * SEQ], half(w, np.s_[:, k, :]),
                                 half(xT, np.s_[:, k, :]), k == 0, k == DC - 1)
                done = pe.did(mm)
                weights.done(done, i)
            evac(n0 // P, b, done)

        def add_normed(held, done, mix, gain, gain_after):
            ss = cut(NT, 4)
            out_ = []
            for t in range(NT):
                ready = []
                for side in range(2):
                    b = held[2 * t + side]
                    part = slice(side * 512, (side + 1) * 512)
                    m = square_sum(psum[b][:, :], ss[:, t, side:side + 1], done[2 * t + side])
                    ready.append(m)
                    dve.need(m, gain_after)
                    m = dve.did(V.tensor_tensor(mix[:, t, part], psum[b][:, :], gain[:, part], ALU.mult))
                    banks.free(b, m)
                dve.need(ready)
                s2 = ss[:, t, 2:3]
                m = dve.did(V.tensor_tensor(s2, ss[:, t, 0:1], ss[:, t, 1:2], ALU.add))
                dve.need(m)
                m = dve.did(V.tensor_scalar(s2, s2, 1.0 / D, EPS, ALU.mult, ALU.add))
                m = inv_root(s2, s2, s2, m)
                dve.need(m)
                out_.append(dve.did(V.scalar_tensor_tensor(h[:, t, :], mix[:, t, :], s2, h[:, t, :], ALU.mult, ALU.add)))
            return out_

        def add_plain(held, done):
            out_ = []
            for i, b in enumerate(held):
                v = h[:, i // 2, (i % 2) * 512:(i % 2 + 1) * 512]
                dve.need(done[i])
                m = dve.did(V.tensor_tensor(v, v, psum[b][:, :], ALU.add))
                banks.free(b, m)
                out_.append(m)
            return [out_[1], out_[3]]

        pos_f = sbuf("pos_f", [P, 4])
        pos_i = sbuf("pos_i", [P, 4], I32)
        scope()
        consts_ab = cut(N_CONST - N_KEPT)
        sp.engine.dma_start(h[:, :, :], T["x"][0].rearrange("(t p) d -> p t d", p=P)).then_inc(s_in, 16)
        sp.engine.dma_start(consts[:, :], T["consts"][:, 0:N_KEPT]).then_inc(s_in, 16)
        sp.engine.dma_start(cols[:, :], T["cols"]).then_inc(s_in, 16)
        loaded = (s_in, 48)
        weights.ahead(splits=False)
        sp.engine.dma_start(pos_i[:, :], T["positions"]).then_inc(s_later, 16)
        sp.engine.dma_start(consts_ab, T["consts"][:, N_KEPT:]).then_inc(s_later, 16)
        later_loaded = (s_later, 32)

        rows_count = [0]

        def load_rows(layer):
            pool.need(loaded, dve.last(), act.last())
            n = ROW_LEN[layer]
            G.dma_start(rows[:, 0:n], T["rows"][layer:layer + 1, 0:n].partition_broadcast(P).rearrange("q a n -> q (a n)")
                                ).then_inc(s_rows, 16)
            rows_count[0] += 16
            return (s_rows, rows_count[0])

        def row(layer, name):
            a, n = ROWS[layer][name]
            return rows[:, a:a + n]

        trig_ready = []

        def turn_tables():
            scope("right")
            ang = right(NT, 60)
            turns = right(NT, 60)
            dve.need(later_loaded)
            m = dve.did(V.tensor_copy(pos_f[:, :], pos_i[:, :]))
            dve.need(m)
            for t in range(NT):
                m = dve.did(V.tensor_scalar(ang[:, t, 0:ROT_C], const("freq")[:, 0:ROT_C], pos_f[:, t:t + 1], None, ALU.mult))
                m = dve.did(V.tensor_scalar(ang[:, t, ROT_C:60], const("freq")[:, ROT_C:60], pos_f[:, 2 + t:3 + t], None, ALU.mult))
            PI_A = 6.28125
            PI_B = float(np.float32(np.floor((TWO_PI - PI_A) * 2 ** 21) / 2 ** 21))
            PI_C = float(TWO_PI - PI_A - PI_B)
            MAGIC = float(3 * 2 ** 22)
            for which, shift in ((0, 0.25), (1, 0.0)):
                dst = trig[:, which, :, :]
                dve.need(m)
                m = dve.did(V.tensor_scalar(turns[:, :, :], ang[:, :, :], 1.0 / TWO_PI, shift, ALU.mult, ALU.add))
                dve.need(m)
                m = dve.did(V.tensor_scalar(turns[:, :, :], turns[:, :, :], MAGIC, None, ALU.add))
                dve.need(m)
                m = dve.did(V.tensor_scalar(turns[:, :, :], turns[:, :, :], MAGIC, None, ALU.subtract))
                src = ang
                for part in (PI_A, PI_B, PI_C):
                    dve.need(m)
                    m = dve.did(V.scalar_tensor_tensor(dst, turns[:, :, :], -part, src if src is dst else src[:, :, :], ALU.mult, ALU.add))
                    src = dst
                if shift:
                    dve.need(m)
                    m = dve.did(V.tensor_scalar(dst, dst, float(np.pi / 2), None, ALU.add))
                dve.need(m)
                m = dve.did(V.tensor_scalar(dst, dst, float(np.float32(3.1415925)), -float(np.float32(3.1415925)), ALU.min, ALU.max))
                act.need(m)
                trig_done = act.did(A.activation(dst, dst, ACT.Sin))
            close("right")
            return trig_done

        def rope(x, dst, n, r, f0, t, tmp1, tmp2, after):
            c = spread(spread(trig[:, 0, t, f0:f0 + r], 1, 2), 1, n)
            s = spread(trig[:, 1, t, f0:f0 + r], 1, n)
            x4 = x.rearrange("p n (two r) -> p n two r", two=2)
            d4 = dst.rearrange("p n (two r) -> p n two r", two=2)
            a = tmp1[:, 0:n * 2 * r].rearrange("p (n two r) -> p n two r", two=2, r=r)
            b = tmp2[:, 0:n * 2 * r].rearrange("p (n two r) -> p n two r", two=2, r=r)
            dve.need(after, trig_ready, dve.last())
            dve.did(V.tensor_tensor(b[:, :, 0, :], x4[:, :, 1, :], s, ALU.mult))
            dve.did(V.tensor_tensor(b[:, :, 1, :], x4[:, :, 0, :], s, ALU.mult))
            m = dve.did(V.tensor_tensor(a, x4, c, ALU.mult))
            dve.need(m)
            dve.did(V.tensor_tensor(d4[:, :, 0, :], a[:, :, 0, :], b[:, :, 0, :], ALU.subtract))
            return dve.did(V.tensor_tensor(d4[:, :, 1, :], a[:, :, 1, :], b[:, :, 1, :], ALU.add))

        def feed_forward_1(layer, h_ready, rows_ready):
            hT = cut_pair(DC, SEQ)
            aT = cut_pair(DFF1 // P, SEQ)
            r = cut(2, 512)
            sq = cut(2, 512)
            g0 = COLS["pre1"] + (layer * 2 + 1) * DC
            xm = feature_major(h, DC, hT, h_ready, cols[:, g0:g0 + DC])
            inv, m = rms(h, h_ready)
            factor = along_tokens_later(inv, m)
            if layer == 0:
                trig_ready.append(turn_tables())
            r_free, sq_free = [None] * 2, [None] * 2
            ready = []

            def evac(c, b, done):
                i = len(ready) % 2
                dst = [v[:, c:c + 2, :].rearrange("p k n -> p (k n)") for v in aT]
                R, R_ready = factor()
                dve.need(done, r_free[i], R_ready)
                m = dve.did(V.scalar_tensor_tensor(r[:, i, :], psum[b][:, :], 0.0, R.rearrange("p k n -> p (k n)"), ALU.max, ALU.mult))
                banks.free(b, m)
                act.need(m)
                hi = act.did(A.activation(dst[0], r[:, i, :], ACT.Square))
                pool.need(m, sq_free[i])
                m = pool.did(G.tensor_tensor(sq[:, i, :], r[:, i, :], r[:, i, :], ALU.mult))
                r_free[i] = [m, hi]
                dve.need(m, hi)
                sq_free[i] = dve.did(V.tensor_tensor(dst[1], sq[:, i, :], dst[0].bitcast(F32), ALU.subtract))
                ready.append(sq_free[i])
            for n0 in range(0, DFF1, 256):
                feature_linear(hT, "up", n0, evac, xm)
            held, done = deep_linear(aT, DFF1 // P, "down", ready)
            return add_normed(held, done, cut(NT, D), row(layer, "post_ff"), rows_ready)

        def gated_add(layer, h_ready, M):
            hT = cut_pair(DC, SEQ)
            gate = cut(4, 512)
            emb = cut(4, 512)
            pt = cut(NT, 256)
            pool.need(pe.last(), dve.last(), act.last())
            pT = cut_pair(2, SEQ)
            G.dma_start(pt, T["p"][layer, 0].rearrange("(t p) d -> p t d", p=P)).then_inc(s_p, 16)
            p_ready = (s_p, 16 * (layer + 1))
            m = feature_major(h, DC, hT, h_ready)
            pm = feature_major(pt, 2, pT, [p_ready])
            held, done = deep_linear(pT, 2, "ple", pm)
            em = [evacuate(b, emb[:, i, :], psum[b][:, :], done[i]) for i, b in enumerate(held)]
            if M:
                memory_turned(0, M)
            held, done = deep_linear(hT, DC, "ple_gate", m)
            out_ = []
            for i, b in enumerate(held):
                t, side = i // 2, i % 2
                act.need(done[i])
                g = act.did(A.activation(gate[:, i, :], psum[b][:, :], ACT.Sigmoid))
                banks.free(b, g)
                dve.need(g, em[i])
                m = dve.did(V.tensor_tensor(gate[:, i, :], gate[:, i, :], emb[:, i, :], ALU.mult))
                dve.need(m)
                v = h[:, t, side * 512:(side + 1) * 512]
                out_.append(dve.did(V.tensor_tensor(v, v, gate[:, i, :], ALU.add)))
            return [out_[1], out_[3]]

        def mixer_ab(h_ready, rows_ready):
            top = cut_pair(DC, SEQ)
            xm = feature_major(h, DC, top, h_ready, cols[:, COLS["pre1"]:COLS["pre1"] + DC])
            inv, inv_ready = rms(h, h_ready)
            factor = along_tokens_later(inv, inv_ready)
            gates, gT = cut(NT, 16), cut(SEQ)
            (wg, wm), = weights.take("gates")
            b = banks.take(pe)
            for k in range(DC):
                pe.need(wm, xm[k // 2])
                mm = product(psum[b][0:16, 0:SEQ], half(wg, np.s_[:, k, :]), half(top, np.s_[:, k, :]), k == 0, k == DC - 1)
            done = pe.did(mm)
            weights.done(done)
            act.need(done)
            gT_ready = act.did(A.copy(gT[0:16, :], psum[b][0:16, 0:SEQ]))
            banks.free(b, gT_ready)
            v8, l8, g8, beta, gc, ab, mcol = cut(NT, 8), cut(NT, 8), cut(NT, 8), cut(NT, 4), cut(NT, 8), cut(NT, 8), cut(NT, 8)
            ea, abT, mxT = cut(8), cut(SEQ), cut(SEQ)
            tri = const("causal3")
            at = {}

            def gate_chain():
                b = banks.take(pe)
                pe.need(gT_ready)
                for t in range(NT):
                    mm = E.transpose(psum[b][:, t * 16:t * 16 + 16], gT[0:16, t * P:(t + 1) * P], ident[0:16, 0:16])
                done = pe.did(mm)
                dve.need(done, rows_ready, inv_ready, later_loaded)
                for t in range(NT):
                    gates_ready = dve.did(V.scalar_tensor_tensor(gates[:, t, :], psum[b][:, t * 16:t * 16 + 16], inv[:, t:t + 1],
                                                                 row(0, "gate_bias"), ALU.mult, ALU.add))
                banks.free(b, gates_ready)
                gview = gates.rearrange("p t (a b) -> p t a b", a=4)
                dve.need(gates_ready)
                m = dve.did(V.tensor_tensor(v8.rearrange("p t (a b) -> p t a b", a=2), gview[:, :, 1::2, :],
                                            spread(const("sign8").rearrange("p (a b) -> p a b", a=2), 1, NT), ALU.mult))
                dve.need(m)
                m = dve.did(V.scalar_tensor_tensor(l8, v8, -1.0, v8, ALU.mult, ALU.max))
                act.need(m)
                m = act.did(A.activation(l8, l8, ACT.Exp, scale=-1.0))
                m2 = act.did(A.activation(ea[:, 0:4], row(0, "a_log"), ACT.Exp))
                act.need(m)
                m = act.did(A.activation(l8, l8, ACT.Ln, bias=1.0))
                m3 = act.did(A.activation(beta, gates[:, :, 0:4], ACT.Sigmoid))
                dve.did(V.memset(ea[:, 4:8], 1.0))
                dve.need(m, m2, dve.last())
                m = dve.did(V.scalar_tensor_tensor(g8, v8, 0.0, l8, ALU.max, ALU.add))
                dve.need(m)
                g_ready = dve.did(V.scalar_tensor_tensor(g8, g8, -1.0, spread(ea, 1, NT), ALU.mult, ALU.mult))
                yield
                yield
                b = banks.take(pe)
                pe.need(g_ready)
                for t in range(NT):
                    for s_ in range(t + 1):
                        mm = E.matmul(psum[b][:, t * 8:t * 8 + 8], tri[:, (t + s_) * P:(t + s_ + 1) * P], g8[:, s_, :],
                                      start=(s_ == 0), stop=(s_ == t))
                done = pe.did(mm)
                dve.need(done)
                gc_ready = dve.did(V.tensor_copy(gc, psum[b][:, 0:16].rearrange("p (t n) -> p t n", t=NT)))
                banks.free(b, gc_ready)
                yield
                yield
                dve.need(gc_ready, m3)
                dve.did(V.tensor_copy(ab[:, :, 0:4], beta))
                m = dve.did(V.tensor_tensor(ab[:, :, 4:8], gates[:, :, 8:12], gc[:, :, 4:8], ALU.subtract))
                b, done = transposes([ab[:, t, :] for t in range(NT)], [m])
                act.need(done)
                m = act.did(A.copy(abT[0:8, :], psum[b][0:8, 0:SEQ]))
                banks.free(b, m)
                dve.need(m)
                mx_ready = dve.did(V.tensor_tensor_scan(mxT[0:8, :], abT[0:8, :], abT[0:8, :], 0.0, ALU.max, ALU.max))
                yield
                yield
                b = banks.take(pe)
                pe.need(mx_ready)
                for t in range(NT):
                    mm = E.transpose(psum[b][:, t * 8:t * 8 + 8], mxT[0:8, t * P:(t + 1) * P], ident[0:8, 0:8])
                done = pe.did(mm)
                dve.need(done)
                mcol_ready = dve.did(V.tensor_copy(mcol, psum[b][:, 0:16].rearrange("p (t n) -> p t n", t=NT)))
                banks.free(b, mcol_ready)
                at.update(beta=m3, mx=mx_ready, mcol=mcol_ready)

            qkv = cut(12, SEQ)
            qkb = cut(8, SEQ)
            both_gates = cut(2 * NT * 512)
            zs, og = [shaped(both_gates[:, k * 1024:(k + 1) * 1024], NT, 512) for k in range(2)]
            vb = cut(NT, 512)
            scope("right")
            pad = right(2, 2, SEQ + 3)
            cv = right(2, 2, SEQ)
            zeroed = pool.did(G.memset(pad[:, :, :, 0:3], 0.0))
            pad_free, cv_free = [zeroed, zeroed], [None, None]
            qkv_ready = []
            wc = COLS["conv_a"]
            turn = [0]

            def evac(c, b, done):
                i = turn[0] % 2
                turn[0] += 1
                R, R_ready = factor()
                dve.need(done, pad_free[i], R_ready)
                m = dve.did(V.tensor_tensor(pad[:, i, :, 3:], psum[b][:, :].rearrange("p (k n) -> p k n", k=2), R, ALU.mult))
                banks.free(b, m)
                ends = []
                for j in range(2):
                    ch = c + j
                    dve.need(m, cv_free[i])
                    e = dve.did(V.tensor_scalar(cv[:, i, j, :], pad[:, i, j, 0:SEQ], cols[:, wc + ch * 4:wc + ch * 4 + 1],
                                                None, ALU.mult))
                    ends.append(e)
                for k in range(1, 4):
                    for j in range(2):
                        ch = c + j
                        dve.need(ends[j])
                        ends[j] = dve.did(V.scalar_tensor_tensor(cv[:, i, j, :], pad[:, i, j, k:k + SEQ],
                                                                 cols[:, wc + ch * 4 + k:wc + ch * 4 + k + 1],
                                                                 cv[:, i, j, :], ALU.mult, ALU.add))
                pad_free[i] = ends[1]
                act.need(ends)
                cv_free[i] = act.did(A.activation(qkv[:, c:c + 2, :], cv[:, i, :, :], ACT.Silu))
                qkv_ready.append(cv_free[i])

            kbT = cut(4, SEQ)
            scratch = cut(4 * 512)
            sq = shaped(scratch, 4, 512)
            l2, l2T = cut(NT, 8), cut(SEQ)
            select = const("select").rearrange("p (h n) -> p h n", h=8)
            flat = qkv.rearrange("p k n -> p (k n)")
            l2_ready = []
            vbeta = cut(NT, 512)
            v_ready = []

            def norms_and_values():
                squared = []
                for c in range(0, 8, 2):
                    src = flat[:, c * SEQ:(c + 2) * SEQ]
                    pool.need(qkv_ready[c // 2])
                    squared.append(pool.did(G.tensor_tensor(sq[:, c // 2, :], src, src, ALU.mult)))
                yield
                b = banks.take(pe)
                for c in range(8):
                    pe.need(squared[c // 2])
                    for t in range(NT):
                        a = (c % 2) * SEQ + t * P
                        mm = E.matmul(psum[b][:, t * 8 + c:t * 8 + c + 1], sq[:, c // 2, a:a + P], ones[:, 0:1], start=True, stop=True)
                done = pe.did(mm)
                dve.need(done)
                m = dve.did(V.tensor_scalar(l2, psum[b][:, 0:16].rearrange("p (t n) -> p t n", t=NT), EPS, None, ALU.add))
                banks.free(b, m)
                m = inv_root(l2, l2, l2, m)
                yield
                b, done = transposes([l2[:, t, :] for t in range(NT)], [m])
                act.need(done)
                turned = act.did(A.copy(l2T[0:8, :], psum[b][0:8, 0:SEQ]))
                banks.free(b, turned)
                yield
                for c in range(0, 8, 2):
                    b = banks.take(pe)
                    pe.need(turned)
                    for i in range(2):
                        mm = E.matmul(psum[b][:, i * SEQ:(i + 1) * SEQ], select[0:8, c + i, :], l2T[0:8, :], start=True, stop=True)
                    done = pe.did(mm)
                    src = flat[:, c * SEQ:(c + 2) * SEQ]
                    dve.need(done)
                    m = dve.did(V.scalar_tensor_tensor(src, src, float(P) ** -0.5 if c < 4 else 1.0, psum[b][:, :], ALU.mult, ALU.mult))
                    banks.free(b, m)
                    l2_ready.append(m)
                yield
                for t in range(NT):
                    b, done = transposes([qkv[:, 8 + c, t * P:(t + 1) * P] for c in range(4)], qkv_ready)
                    dve.need(done, at["beta"])
                    m = dve.did(V.tensor_tensor(vbeta[:, t, :].rearrange("p (h d) -> p h d", h=4),
                                                psum[b][:, :].rearrange("p (h d) -> p h d", h=4),
                                                spread(beta[:, t, :], 2, P), ALU.mult))
                    banks.free(b, m)
                    v_ready.append(m)
            norms = norms_and_values()
            qkb_ready = []

            def evac_qk(c, b, done):
                c -= COL_QB // P
                R, R_ready = factor()
                dve.need(done, R_ready)
                m = dve.did(V.scalar_tensor_tensor(qkb[:, c:c + 2, :], psum[b][:, :].rearrange("p (k n) -> p k n", k=2),
                                                   float(P) ** -0.5 if c < 4 else 1.0, R, ALU.mult, ALU.mult))
                banks.free(b, m)
                qkb_ready.append(m)
            chain = gate_chain()
            for key, n0 in FEATURES_AB:
                feature_linear(top, key, n0, evac if key == "qkv_a" else evac_qk, xm)
                next(chain, None)
                if len(qkv_ready) >= 4:
                    next(norms, None)
            for _ in chain:
                pass
            close("right")
            gb = cut(NT, P)
            LT = cut(4, 384)
            AT = cut(4, 384)
            PT = cut(4, 384)
            dec = cut(2, 384)
            dec_free = [None, None]
            gb_free = None
            LT_ready, AT_ready, PT_ready = [], [], []

            def key_query(dst_bank, kT, qT, after):
                pe.need(after)
                E.matmul(psum[dst_bank][:, 0:SEQ], kT[:, 0:P], qT[:, 0:SEQ], start=True, stop=True)
                return pe.did(E.matmul(psum[dst_bank][:, SEQ:384], kT[:, P:SEQ], qT[:, P:SEQ], start=True, stop=True))

            level = const("level").rearrange("p (l n) -> p l n", l=7)
            N_, M_ = [[cut(4, P) for _ in range(NT)] for _ in range(2)]
            C_ = [shaped(sq[:, j, :], 4, P) for j in range(NT)]
            Q_ = [shaped(sq[:, NT + j, :], 4, P) for j in range(NT)]
            n_ready, m_ready, q_free, c_free, q_ready = [[None] * 2 for _ in range(5)]
            idb = spread(ident, 1, 4)

            def diag(j):
                return LT[:, :, 0:P] if j == 0 else LT[:, :, SEQ:384]

            def decays():
                nonlocal gb_free
                for hd in range(4):
                    b = banks.take(pe)
                    pe.need(at["mx"])
                    done = pe.did(E.matmul(psum[b][:, 0:SEQ], select[0:8, hd, :], abT[0:8, :], start=True, stop=True))
                    dve.need(done, l2_ready)
                    kb_ready = dve.did(V.tensor_tensor(kbT[:, hd, :], qkv[:, 4 + hd, :], psum[b][:, 0:SEQ], ALU.mult))
                    banks.free(b, kb_ready)
                    dve.need(gb_free)
                    m = dve.did(V.tensor_copy(gb, spread(g8[:, :, hd], 2, P)))
                    b = banks.take(pe)
                    pe.need(m)
                    E.matmul(psum[b][:, 0:SEQ], gb[:, 0, :], tri[:, 0:SEQ], start=True, stop=False)
                    gb_free = done = pe.did(E.matmul(psum[b][:, P:SEQ], gb[:, 1, :], tri[:, SEQ:384], start=False, stop=True))
                    i = hd % 2
                    dve.need(done, dec_free[i])
                    dve.did(V.tensor_scalar(dec[:, i, 0:SEQ], psum[b][:, 0:SEQ], gc[:, 0, hd:hd + 1], 0.0, ALU.subtract, ALU.min))
                    m = dve.did(V.tensor_scalar(dec[:, i, SEQ:384], psum[b][:, P:SEQ], gc[:, 1, hd:hd + 1], 0.0, ALU.subtract, ALU.min))
                    banks.free(b, m)
                    act.need(m)
                    m = dec_ready = act.did(A.activation(dec[:, i, :], dec[:, i, :], ACT.Exp))
                    pool.need(m)
                    e2 = pool.did(G.tensor_tensor(AT[:, hd, :], dec[:, i, :], const("causal3"), ALU.mult))
                    yield
                    b = banks.take(pe)
                    done = key_query(b, qkv[:, 4 + hd, :], kbT[:, hd, :], [kb_ready])
                    dve.need(done, dec_ready)
                    m = dve.did(V.tensor_tensor(LT[:, hd, :], dec[:, i, :], psum[b][:, 0:384], ALU.mult))
                    dec_free[i] = [e2, m]
                    banks.free(b, m)
                    LT_ready.append(m)
                    b = banks.take(pe)
                    done = key_query(b, qkv[:, 4 + hd, :], qkv[:, hd, :], [l2_ready])
                    dve.need(done, e2)
                    m = dve.did(V.tensor_tensor(AT[:, hd, :], AT[:, hd, :], psum[b][:, 0:384], ALU.mult))
                    banks.free(b, m)
                    AT_ready.append(m)
    
            def inverted():
                for j in range(NT):
                    pool.need(LT_ready)
                    m = pool.did(G.tensor_tensor(C_[j], diag(j), spread(level[:, 0, :], 1, 4), ALU.mult))
                    dve.need(m)
                    c_free[j] = n_ready[j] = dve.did(V.tensor_tensor(N_[j], idb, C_[j], ALU.subtract))
                    b, done = transposes([N_[j][:, hd, :] for hd in range(4)], [n_ready[j]])
                    act.need(done)
                    m_ready[j] = act.did(A.copy(M_[j], psum[b][:, :].rearrange("p (h n) -> p h n", h=4)))
                    banks.free(b, m_ready[j])
                yield
                for lv in range(1, 7):
                    for j in range(NT):
                        pool.need(c_free[j])
                        cm = pool.did(G.tensor_tensor(C_[j], diag(j), spread(level[:, lv, :], 1, 4), ALU.mult))
                        b = banks.take(pe)
                        pe.need(cm, m_ready[j], n_ready[j])
                        for hd in range(4):
                            mm = E.matmul(psum[b][:, hd * P:(hd + 1) * P], C_[j][:, hd, :], M_[j][:, hd, :], start=True, stop=True)
                        c_free[j] = done = pe.did(mm)
                        act.need(done, q_free[j])
                        q_ready[j] = act.did(A.copy(Q_[j], psum[b][:, :].rearrange("p (h n) -> p h n", h=4)))
                        banks.free(b, q_ready[j])
                    yield
                    for j in range(NT):
                        for product_of in ("N", "M") if lv < 6 else ("N",):
                            b = banks.take(pe)
                            pe.need(q_ready[j])
                            for hd in range(4):
                                x, y = (Q_, N_) if product_of == "N" else (N_, Q_)
                                mm = E.matmul(psum[b][:, hd * P:(hd + 1) * P], x[j][:, hd, :], y[j][:, hd, :], start=True, stop=True)
                            done = pe.did(mm)
                            if product_of == "N":
                                bn = b
                            else:
                                dve.need(done)
                                m_ready[j] = dve.did(V.tensor_tensor(M_[j], M_[j], psum[b][:, :].rearrange("p (h n) -> p h n", h=4), ALU.subtract))
                                banks.free(b, m_ready[j])
                        q_free[j] = done
                        dve.need(done)
                        n_ready[j] = dve.did(V.tensor_tensor(N_[j], N_[j], psum[bn][:, :].rearrange("p (h n) -> p h n", h=4), ALU.subtract))
                        banks.free(bn, n_ready[j])
                    yield

            def side():
                yield from norms
                yield from decays()
                yield from inverted()
            side = side()

            lin_ready = []
            for n0, dst, fn in ((COL_Z, zs, ACT.Silu), (COL_VB, vb, ACT.Copy), (COL_O, og, ACT.Sigmoid)):
                def evac(t, b, done, dst=dst, fn=fn):
                    act.need(done, inv_ready)
                    m = act.did(A.activation(dst[:, t, :], psum[b][:, :], fn, scale=inv[:, t:t + 1]))
                    banks.free(b, m)
                    lin_ready.append(m)
                token_linear(top, "zvo", n0, 512, evac, xm, lambda: next(side, None))

            for hd in range(4):
                i = hd % 2
                b = banks.take(pe)
                pe.need(at["mx"])
                done = pe.did(E.matmul(psum[b][:, 0:SEQ], select[0:8, 4 + hd, :], mxT[0:8, :], start=True, stop=True))
                dve.need(done, dec_free[i])
                dve.did(V.tensor_scalar(dec[:, i, 0:SEQ], psum[b][:, 0:SEQ], ab[:, 0, 4 + hd:5 + hd], 0.0, ALU.subtract, ALU.max))
                m = dve.did(V.tensor_scalar(dec[:, i, SEQ:384], psum[b][:, P:SEQ], ab[:, 1, 4 + hd:5 + hd], 0.0, ALU.subtract, ALU.max))
                banks.free(b, m)
                act.need(m)
                m = act.did(A.activation(dec[:, i, :], dec[:, i, :], ACT.Exp, scale=-1.0))
                pool.need(m)
                e = dec_free[i] = pool.did(G.tensor_tensor(PT[:, hd, :], dec[:, i, :], const("causal3"), ALU.mult))
                next(side, None)
                b = banks.take(pe)
                done = key_query(b, qkb[:, 4 + hd, :], qkb[:, hd, :], qkb_ready)
                dve.need(done, e)
                m = dve.did(V.tensor_tensor(PT[:, hd, :], PT[:, hd, :], psum[b][:, 0:384], ALU.mult))
                banks.free(b, m)
                PT_ready.append(m)
                next(side, None)

            def weighted(W3, val, t, after):
                b = banks.take(pe)
                pe.need(after)
                for hd in range(4):
                    for s_ in range(t + 1):
                        k = t + s_
                        mm = E.matmul(psum[b][:, hd * P:(hd + 1) * P], W3[:, hd, k * P:(k + 1) * P],
                                      val[:, s_, hd * P:(hd + 1) * P], start=(s_ == 0), stop=(s_ == t))
                return b, pe.did(mm)

            db = banks.take(pe)
            pe.need(PT_ready)
            for t in range(NT):
                for hd in range(4):
                    for s_ in range(t + 1):
                        k = t + s_
                        mm = E.matmul(psum[db][:, t * 4 + hd:t * 4 + hd + 1], PT[:, hd, k * P:(k + 1) * P], ones[:, 0:1],
                                      start=(s_ == 0), stop=(s_ == t))
            done = pe.did(mm)
            den, em = cut(NT, 4), cut(NT, 4)
            act.need(done)
            den_abs = act.did(A.activation(den, psum[db][:, 0:8].rearrange("p (t n) -> p t n", t=NT), ACT.Abs))
            banks.free(db, den_abs)
            dve.need(at["mcol"])
            m = dve.did(V.tensor_tensor(em, gc[:, :, 4:8], mcol[:, :, 4:8], ALU.add))
            act.need(m)
            m = act.did(A.activation(em, em, ACT.Exp, scale=-1.0))
            dve.need(m, den_abs)
            m = dve.did(V.tensor_tensor(den, den, em, ALU.max))
            dve.need(m)
            den_ready = dve.did(V.reciprocal(den, den))
            mixed_a, squares_a = [shaped(scratch[:, k * 1024:(k + 1) * 1024], NT, 512) for k in range(2)]
            mixed_b, squares_b = [shaped(flat[:, k * 1024:(k + 1) * 1024], NT, 512) for k in range(2)]
            b_ready = []
            for t in range(NT):
                b, done = weighted(PT, vb, t, [PT_ready, lin_ready])
                dve.need(done, den_ready)
                m = dve.did(V.tensor_tensor(mixed_b[:, t, :].rearrange("p (h d) -> p h d", h=4),
                                            psum[b][:, :].rearrange("p (h d) -> p h d", h=4),
                                            spread(den[:, t, :], 2, P), ALU.mult))
                banks.free(b, m)
                b_ready.append(m)
                next(side, None)
            for _ in side:
                pass

            def finished(x, squares, ss, gate, gain, after):
                pool.need(after)
                m = pool.did(G.tensor_tensor(squares, x, x, ALU.mult))
                pool.need(lin_ready, rows_ready)
                gated = pool.did(G.tensor_tensor(gate, gate, spread(gain, 1, NT), ALU.mult))
                dve.need(m)
                m = dve.did(V.tensor_reduce(ss, squares.rearrange("p t (h d) -> p (t h) d", h=4), AXX, ALU.add))
                dve.need(m)
                m = dve.did(V.tensor_scalar(ss, ss, 1.0 / P, EPS, ALU.mult, ALU.add))
                m = inv_root(ss, ss, ss, m)
                heads = x.rearrange("p t (h d) -> p (t h) d", h=4)
                dve.need(m, after)
                m = dve.did(V.tensor_tensor(heads, heads, spread(ss, 2, P), ALU.mult))
                dve.need(m, gated)
                return dve.did(V.tensor_tensor(x, x, gate, ALU.mult))

            U = shaped(kbT.rearrange("p h n -> p (h n)"), NT, 512)
            Z = cut(512)
            b = banks.take(pe)
            pe.need(n_ready, v_ready)
            for hd in range(4):
                mm = E.matmul(psum[b][:, hd * P:(hd + 1) * P], N_[0][:, hd, :], vbeta[:, 0, hd * P:(hd + 1) * P], start=True, stop=True)
            done = pe.did(mm)
            u1 = copy_on(act, U[:, 0, :], psum[b][:, :], done)
            banks.free(b, u1)
            b = banks.take(pe)
            pe.need(u1)
            for hd in range(4):
                mm = E.matmul(psum[b][:, hd * P:(hd + 1) * P], LT[:, hd, P:SEQ], U[:, 0, hd * P:(hd + 1) * P], start=True, stop=True)
            done = pe.did(mm)
            dve.need(done)
            m = dve.did(V.tensor_tensor(Z, vbeta[:, 1, :], psum[b][:, :], ALU.subtract))
            banks.free(b, m)
            b = banks.take(pe)
            pe.need(m)
            for hd in range(4):
                mm = E.matmul(psum[b][:, hd * P:(hd + 1) * P], N_[1][:, hd, :], Z[:, hd * P:(hd + 1) * P], start=True, stop=True)
            done = pe.did(mm)
            u2 = copy_on(act, U[:, 1, :], psum[b][:, :], done)
            banks.free(b, u2)

            ss_a, ss_b = cut(NT * 4), cut(NT * 4)
            b_done = finished(mixed_b, squares_b, ss_b, og, row(0, "norm_b"), b_ready)
            a_ready = []
            for t in range(NT):
                b, done = weighted(AT, U, t, [u1, u2, AT_ready])
                a_ready.append(evacuate(b, mixed_a[:, t, :], psum[b][:, :], done))
            turned = {4: feature_major(mixed_b, 4, [v[:, 4:8, :] for v in top], [b_done])}
            a_done = finished(mixed_a, squares_a, ss_a, zs, row(0, "norm_a"), a_ready)
            held = [banks.take(pe) for _ in range(4)]
            for k0 in OUT_AB:
                if k0 == 0:
                    turned[0] = feature_major(mixed_a, 4, [v[:, 0:4, :] for v in top], [a_done])
                done = deep_panel(held, top, k0, "out_ab", k0, turned[k0 // 4 * 4][k0 % 4 // 2], k0 == OUT_AB[0], k0 == OUT_AB[-1])
            return held, done, shaped(both_gates, NT, D)

        def attention(groups, S, PTb, mx, den, out):
            state, qk_slot = [None] * len(groups), {}
            freeS, freeP, freeSt, freeQK, ready = [None, None], [None], [None, None], [None, None], {}

            def prepare(n):
                if groups[n]["prepare"] is None:
                    qk_slot[n], ready[n] = qk_slot[n - 1], ready[n - 1]
                else:
                    qk_slot[n] = n % 2
                    ready[n] = groups[n]["prepare"](n % 2, freeQK[n % 2])

            def tiles(g):
                return ((0, 0, P), (1, P, SEQ)) if g["causal"] else ((0, 0, SEQ), (1, SEQ, SEQ))

            def scores(n):
                g = groups[n]
                i, qk = n % 2, qk_slot[n]
                scored = [[], []]
                for t, c0, nk in tiles(g):
                    for heads in ((0, 2, 1, 3),) if nk == P else ((0, 2), (1, 3)):
                        per = len(heads)
                        b = banks.take(pe)
                        pe.need(ready[n])
                        for j, hh in enumerate(heads):
                            if j == 2 and g.get("rows_apart", True):
                                pe.need(pe.did(mm))
                            at = hh if per == 4 else j
                            mm = E.matmul(psum[b][:, at * nk:(at + 1) * nk], g["q"](qk, hh)[:, t * P:(t + 1) * P],
                                          g["k"](qk, hh)[:, 0:nk], start=True, stop=True)
                        done = freeQK[qk] = pe.did(mm)
                        bank = psum[b][:, :].rearrange("p (h n) -> p h n", h=per)
                        dve.need(done, freeS[i], freeSt[i])
                        own = slice(None) if per == 4 else slice(heads[0], None, 2)
                        s_ = S[:, i, own, c0:c0 + nk]
                        if g.get("bias") is not None:
                            dve.need(g["bias_ready"])
                            m = dve.did(V.scalar_tensor_tensor(s_, bank, g["scale"], g["bias"][:, own, c0:c0 + nk],
                                                               ALU.mult, ALU.subtract))
                        elif g.get("mask") is None:
                            m = dve.did(V.tensor_scalar(s_, bank, g["scale"], None, ALU.mult))
                        else:
                            m = dve.did(V.scalar_tensor_tensor(s_, bank, g["scale"], spread(g["mask"][:, c0:c0 + nk], 1, per),
                                                               ALU.mult, ALU.add))
                        banks.free(b, m)
                        scored[t].append(m)
                for t, c0, nk in tiles(g):
                    dve.need(scored[t])
                    m = dve.did(V.tensor_reduce(mx[:, i, t, :], S[:, i, :, c0:c0 + nk], AXX, ALU.max, negate=True))
                    if g.get("sink") is not None:
                        dve.need(m)
                        m = dve.did(V.tensor_tensor(mx[:, i, t, :], mx[:, i, t, :], g["minus_sink"], ALU.min))
                    act.need(m)
                    for hh in range(4):
                        e = act.did(A.activation(S[:, i, hh, c0:c0 + nk], S[:, i, hh, c0:c0 + nk], ACT.Exp,
                                                 bias=mx[:, i, t, hh:hh + 1], accum_out=den[:, i, t, hh:hh + 1]))
                if g.get("sink") is not None:
                    sk = den[:, i, 2:4, :]
                    dve.need(m)
                    m2 = dve.did(V.tensor_tensor(sk, mx[:, i, :, :], spread(g["sink"], 1, NT), ALU.add))
                    act.need(m2)
                    m2 = act.did(A.activation(sk, sk, ACT.Exp))
                    dve.need(m2, e)
                    m2 = dve.did(V.tensor_tensor(den[:, i, 0:2, :], den[:, i, 0:2, :], sk, ALU.add))
                    state[n] = [[m2, e]]
                else:
                    state[n] = [[e]]

            def turned(n):
                g = groups[n]
                i = n % 2
                marks = []
                n_blk = 3 if g["causal"] else 4
                for k in range(n_blk):
                    b, m = transposes([S[:, i, hh, k * P:(k + 1) * P] for hh in range(4)], [state[n][0]])
                    act.need(freeP[0])
                    dve.need(freeP[0])
                    marks.append(evacuate(b, PTb[:, k, :, :], psum[b][:, :].rearrange("p (h n) -> p h n", h=4), m))
                freeS[i] = m
                state[n].append(marks)

            def values(n):
                g = groups[n]
                i = n % 2
                b = banks.take(pe)
                pe.need(state[n][1], g["v_ready"])
                for t in range(NT):
                    blocks = ((0, 0),) if g["causal"] and t == 0 else ((1, 0), (2, 1)) if g["causal"] else ((2 * t, 0), (2 * t + 1, 1))
                    for hh in range(4):
                        for x, (k, s_) in enumerate(blocks):
                            mm = E.matmul(psum[b][:, (t * 4 + hh) * 64:(t * 4 + hh + 1) * 64], PTb[:, k, hh, :], g["v"](hh, s_),
                                          start=(x == 0), stop=(x == len(blocks) - 1))
                done = pe.did(mm)
                freeP[0] = done
                dve.need(state[n][0])
                state[n][0] = dve.did(V.reciprocal(den[:, i, 0:2, :], den[:, i, 0:2, :]))
                bank = psum[b][:, :].rearrange("p (t h d) -> p t h d", t=NT, h=4)
                dve.need(done, state[n][0])
                m = g["finish"](bank, den[:, i, 0:2, :])
                freeSt[i] = m
                banks.free(b, m)

            out_free, out_ready, held, done = {}, {}, [], []

            def out_turned(n):
                g = groups[n]
                if "out" in g:
                    i = g["out"][1] % out.slots
                    out_ready[n], = feature_major(g["out"][0], 2, [v[:, 2 * i:2 * i + 2, :] for v in out.buffers], [freeSt[n % 2]],
                                                  free=out_free.get(i))

            def out_products(n):
                g = groups[n]
                if "out" in g:
                    if not held:
                        held.extend(banks.take(pe) for _ in range(4))
                        if out.bias is not None:
                            for i, b in enumerate(held):
                                E.matmul(psum[b][:, :], ones[0:1, :], out.bias[0:1, i % 2 * 512:(i % 2 + 1) * 512], start=True, stop=False)
                    _, j, k0 = g["out"]
                    i = j % out.slots
                    done.extend(deep_panel(held, out.buffers, 2 * i, out.key, k0, out_ready[n], j == 0 and out.bias is None, n == len(groups) - 1))
                    out_free[i] = pe.last()

            def next_ready(n):
                if n + 1 < len(groups) and "work" in groups[n + 1]:
                    groups[n + 1]["work"]()
            skewed([(4, out_turned), (3, values), (2, turned), (1, scores), (4, out_products), (0, prepare), (0, next_ready)],
                   len(groups))
            return held, done

        def scaled_into(dst):
            def finish(bank, rden):
                for t in range(NT):
                    m = dve.did(V.tensor_tensor(dst[:, t, :].rearrange("p (h d) -> p h d", h=4), bank[:, t, :, :],
                                                spread(rden[:, t, :], 2, 64), ALU.mult))
                return m
            return finish

        def mixer_c(h_ready, rows_ready):
            mixed, hT = cut(NT, D), cut_pair(DC, SEQ)
            xm = feature_major(h, DC, hT, h_ready, cols[:, COLS["pre1"] + 2 * DC:COLS["pre1"] + 3 * DC])
            inv, inv_ready = rms(h, h_ready)
            proj = cut(NT, 1536)
            tmp1, tmp2 = cut(512), cut(512)

            def projected(n0):
                marks = []

                def evac(t, b, done):
                    dve.need(done, rows_ready, inv_ready)
                    m = dve.did(V.scalar_tensor_tensor(proj[:, t, n0:n0 + 512], psum[b][:, :], inv[:, t:t + 1],
                                                       row(1, "b_qkv")[:, n0:n0 + 512], ALU.mult, ALU.add))
                    banks.free(b, m)
                    marks.append(m)
                token_linear(hT, "qkv_c", n0, 512, evac, xm)
                return marks

            def turned_heads(c0, n, after):
                for t in range(NT):
                    x = proj[:, t, c0:c0 + n * CHD].rearrange("p (n d) -> p n d", d=CHD)
                    m = rope(x, x, n, ROT_C, 0, t, tmp1, tmp2, after)
                return m

            v_marks = projected(1024)
            q_marks = projected(0)
            k_turned = turned_heads(1024, 4, v_marks)
            turned = {0: [k_turned, turned_heads(0, 8, q_marks)]}
            q_marks = projected(512)

            def last_queries():
                turned[1] = [k_turned, turned_heads(512, 8, q_marks)]
            S = cut(2, 4, 512)
            PTb = cut(4, 4, P)
            QK = cut(2, 3, SEQ)
            k2 = cut(2, NT, P)
            mx, den = cut(2, NT, 4), cut(2, 4, 4)
            dve.need(rows_ready)
            minus_sink = cut(CH)
            m = dve.did(V.tensor_scalar(minus_sink, row(1, "sinks"), -1.0, None, ALU.mult))
            dve.need(m)
            groups = []
            for kv in range(CKV):
                def prep(i, free, kv=kv):
                    act.need(free)
                    dve.need(free)
                    k = proj[:, :, 1024 + kv * 64:1024 + (kv + 1) * 64]
                    for t in range(NT):
                        pool.need(turned[kv // 2], free)
                        k2_ready = pool.did(G.tensor_copy(k2[:, i, t, :].rearrange("p (a d) -> p a d", a=2), spread(k[:, t, :], 1, 2)))
                    return heads_transposed(
                        lambda c, t: proj[:, t, kv * 256 + c * P:kv * 256 + (c + 1) * P] if c < 2 else k2[:, i, t, :],
                        3, P, QK[:, i, :, :], [turned[kv // 2], k2_ready])
                groups.append(dict(
                    prepare=prep, causal=True, scale=CHD ** -0.5, mask=const("window_neg"),
                    q=lambda i, hh: QK[hh % 2 * 64:(hh % 2 + 1) * 64, i, hh // 2, :],
                    k=lambda i, hh: QK[hh % 2 * 64:(hh % 2 + 1) * 64, i, 2, :],
                    v=lambda hh, s_, kv=kv: proj[:, s_, 1280 + kv * 64:1280 + (kv + 1) * 64], v_ready=v_marks,
                    sink=row(1, "sinks")[:, kv * 4:kv * 4 + 4],
                    minus_sink=minus_sink[:, kv * 4:kv * 4 + 4], finish=scaled_into(mixed[:, :, kv * 256:(kv + 1) * 256]),
                    out=(mixed[:, :, kv * 256:(kv + 1) * 256], kv, 2 * kv)))
            groups[1]["work"] = last_queries
            held, done = attention(groups, S, PTb, mx, den, Out("o_c", hT, 4, row(1, "b_o")))
            return held, done, mixed

        def memory_loaded(l):
            kvm = right(NT, 512)
            scope("right")
            mem, memT = right(NT, D), (right(DC, SEQ, dt=F32R), right(DC, SEQ, dt=F32R))
            pool.need(pe.last(), dve.last(), act.last())
            G.dma_start(mem, T["mem_2"][0].rearrange("(t p) d -> p t d", p=P)).then_inc(s_mem, 16)
            return dict(kvm=kvm, mem=mem, memT=memT, loaded=(s_mem, 16 * (l + 1)))

        def memory_turned(l, M):
            g0 = COLS["mem2"] + l * DC
            M["turned"] = feature_major(M["mem"], DC, M["memT"], [M["loaded"]], cols[:, g0:g0 + DC])
            M["inv"], M["inv_ready"] = rms(M["mem"], [M["loaded"]] * NT, r=right(NT))

        def memory_projected(M):
            M["ready"] = []

            def evac(t, b, done):
                act.need(done, M["inv_ready"])
                m = act.did(A.activation(M["kvm"][:, t, :], psum[b][:, :], ACT.Copy, scale=M["inv"][:, t:t + 1]))
                banks.free(b, m)
                M["ready"].append(m)
            token_linear(M["memT"], "mem_kv", 0, 512, evac, M["turned"])
            close("right")

        def mixer_2(l, h_ready, rows_ready, M):
            layer = 2 + l
            R = lambda name: row(layer, name)
            memory_projected(M)
            kvm, mk = M["kvm"], M["ready"]
            mixed = cut(NT, MIX2)
            scope()
            hp = cut(NT, D_IN2)
            PTb = cut(4, 4, P)
            squares = cut(2, 1024)
            st = cut(NT, 48)
            st2 = cut(NT, 16)
            cT = cut(3, SEQ)
            qa, kva, ka = cut(NT, 384), cut(NT, 512), cut(NT, 384)
            turn_a, turn_b = cut(P), cut(P)
            squares_free, square_turn = [None] * 2, [0]

            def sum_squares(x, n, d, dst, after):
                i = square_turn[0] = 1 - square_turn[0]
                a = shaped(squares[:, i, 0:NT * n * d], NT, n * d)
                pool.need(after, squares_free[i])
                m = pool.did(G.tensor_tensor(a, x, x, ALU.mult))
                dve.need(m)
                squares_free[i] = dve.did(V.tensor_reduce(dst, a.rearrange("p t (n d) -> p t n d", d=d), AXX, ALU.add))
                return squares_free[i]

            def roots(x, inv, after):
                dve.need(after)
                if isinstance(inv, float):
                    m = dve.did(V.tensor_scalar(x, x, inv, EPS, ALU.mult, ALU.add))
                else:
                    m = dve.did(V.tensor_tensor(x, x, inv, ALU.mult))
                    dve.need(m)
                    m = dve.did(V.tensor_scalar(x, x, EPS, None, ALU.add))
                return inv_root(x, x, x, m)

            def normed(x, n, d, ss, gain, after):
                x4 = x.rearrange("p t (n d) -> p t n d", n=n)
                dve.need(after)
                m = dve.did(V.tensor_tensor(x4, x4, spread(ss, 3, d), ALU.mult))
                dve.need(m, rows_ready)
                return dve.did(V.tensor_tensor(x, x, spread(gain, 1, NT), ALU.mult))

            def squared(slot, *kinds):
                at = slot
                for c0, n, d, name in kinds:
                    m = sum_squares(hp[:, :, c0:c0 + n * d], n, d, st[:, :, at:at + n], pj_of(c0 + n * d))
                    at += n
                return slot, at, kinds, m

            def scaled(slot, end, kinds, m):
                m = roots(st[:, :, slot:end], spread(const("inv_d")[:, slot:end], 1, NT), m)
                marks = []
                for c0, n, d, name in kinds:
                    marks.append(normed(hp[:, :, c0:c0 + n * d], n, d, st[:, :, slot:slot + n], R(name), m))
                    slot += n
                return marks

            scope("right")
            hT = right(DC, SEQ, dt=F32R), right(DC, SEQ, dt=F32R)
            g0 = COLS["attn2"] + l * DC
            xm = feature_major(h, DC, hT, h_ready, cols[:, g0:g0 + DC])
            inv, inv_ready = rms(h, h_ready)
            pj = []

            def pj_of(end):
                need = NT * -(-end // 512)
                assert len(pj) >= need
                return pj[:need]

            def projected(n0):
                nn = min(512, D_IN2 - n0)

                def evac(t, b, done):
                    act.need(done, inv_ready)
                    m = act.did(A.activation(hp[:, t, n0:n0 + nn], psum[b][:, 0:nn], ACT.Copy, scale=inv[:, t:t + 1]))
                    banks.free(b, m)
                    pj.append(m)
                token_linear(hT, "in_2", n0, nn, evac, xm)

            projected(0)
            m = sum_squares(kvm[:, :, 0:256], 4, 64, st2[:, :, 12:16], mk)
            m = roots(st2[:, :, 12:16], 1.0 / 64, m)
            memk_ready = normed(kvm[:, :, 0:256], 4, 64, st2[:, :, 12:16], R("memk"), m)
            projected(512)
            low_rank = scaled(*squared(0, (C_CQ, 1, 192, "cq"), (C_CKV, 1, 128, "ckv"), (C_KR, 1, 32, "kr")))
            projected(1024)
            cT_ready = []
            for k, (c0, w) in enumerate(((0, P), (P, 64), (C_CKV, P))):
                b, mt = transposes([hp[:, t, c0:c0 + w] for t in range(NT)], [low_rank])
                cT_ready.append(evacuate(b, cT[0:w, k, :], psum[b][0:w, 0:SEQ], mt))
            fox_ready = scaled(*squared(3, (C_FOX, 8, 64, "fox")))
            projected(1536)
            w3, wm = weights.take("mla")
            am = []
            for t in range(NT):
                b = banks.take(pe)
                pe.need(wm, cT_ready)
                E.matmul(psum[b][:, 0:384], cT[:, 0, t * P:(t + 1) * P], w3[:, 0:384], start=True, stop=False)
                done = pe.did(E.matmul(psum[b][:, 0:384], cT[0:64, 1, t * P:(t + 1) * P], w3[0:64, 384:768], start=False, stop=True))
                am.append(evacuate(b, qa[:, t, :], psum[b][:, 0:384], done))
                b = banks.take(pe)
                done = pe.did(E.matmul(psum[b][:, :], cT[:, 2, t * P:(t + 1) * P], w3[:, 768:1280], start=True, stop=True))
                am.append(evacuate(b, kva[:, t, :], psum[b][:, :], done))
            weights.done(done)

            fx = cut(NT, 4)
            lf = cut(NT, 4)
            dve.need(pj_of(C_FF + 4), rows_ready)
            m = dve.did(V.tensor_tensor(fx, hp[:, :, C_FF:C_FF + 4], spread(R("fox_b"), 1, NT), ALU.add))
            dve.need(m)
            m = dve.did(V.scalar_tensor_tensor(lf, fx, -1.0, fx, ALU.mult, ALU.max))
            act.need(m)
            m = act.did(A.activation(lf, lf, ACT.Exp, scale=-1.0))
            act.need(m)
            m = act.did(A.activation(lf, lf, ACT.Ln, bias=1.0))
            dve.need(m)
            lf_ready = dve.did(V.scalar_tensor_tensor(lf, fx, 0.0, lf, ALU.min, ALU.subtract))
            gb = cut(4, NT, P)
            dve.need(lf_ready)
            gb_ready = dve.did(V.tensor_copy(gb, spread(lf.rearrange("p t h -> p h t"), 3, P)))
            lam_init = 0.8 - 0.6 * float(np.exp(-0.3 * l))
            lm = cut(68)
            lv = R("lambda").rearrange("p (a d) -> p a d", a=4)
            lm3 = lm[:, 0:64].rearrange("p (a d) -> p a d", a=2)
            m = dve.did(V.tensor_tensor(lm3, lv[:, 0::2, :], lv[:, 1::2, :], ALU.mult))
            dve.need(m)
            m = dve.did(V.tensor_reduce(lm[:, 64:66], lm3, AXX, ALU.add))
            act.need(m)
            m = act.did(A.activation(lm[:, 64:66], lm[:, 64:66], ACT.Exp))
            dve.need(m)
            m = dve.did(V.tensor_tensor(lm[:, 66:67], lm[:, 64:65], lm[:, 65:66], ALU.subtract))
            dve.need(m)
            lam_ready = dve.did(V.tensor_scalar(lm[:, 66:67], lm[:, 66:67], lam_init, -1.0, ALU.add, ALU.mult))
            projected(2048)

            tri = const("causal3")
            b = banks.take(pe)
            pe.need(lf_ready)
            for t in range(NT):
                for s_ in range(t + 1):
                    mm = E.matmul(psum[b][:, t * 4:t * 4 + 4], tri[:, (t + s_) * P:(t + s_ + 1) * P], lf[:, s_, :],
                                  start=(s_ == 0), stop=(s_ == t))
            done = pe.did(mm)
            fc = cut(NT, 4)
            dve.need(done)
            fc_ready = dve.did(V.tensor_copy(fc, psum[b][:, 0:8].rearrange("p (t n) -> p t n", t=NT)))
            banks.free(b, fc_ready)
            X = cut(4, 384)
            for hh in range(4):
                b = banks.take(pe)
                pe.need(gb_ready)
                E.matmul(psum[b][:, 0:SEQ], gb[:, hh, 0, :], tri[:, 0:SEQ], start=True, stop=False)
                gb_read = done = pe.did(E.matmul(psum[b][:, P:SEQ], gb[:, hh, 1, :], tri[:, SEQ:384], start=False, stop=True))
                dve.need(done, fc_ready)
                cn = const("causal_neg")
                dve.did(V.scalar_tensor_tensor(X[:, hh, 0:P], psum[b][:, 0:P], fc[:, 0, hh:hh + 1], cn[:, 0:P], ALU.subtract, ALU.subtract))
                X_ready = dve.did(V.scalar_tensor_tensor(X[:, hh, P:384], psum[b][:, 0:SEQ], fc[:, 1, hh:hh + 1], cn[:, P:384],
                                                         ALU.subtract, ALU.subtract))
                banks.free(b, X_ready)

            qa4 = qa.rearrange("p t (n d) -> p t n d", n=4)
            kv4a = kva.rearrange("p t (n d) -> p t n d", n=4)
            ka4 = ka.rearrange("p t (n d) -> p t n d", n=4)

            later = {}

            def mla_normed():
                for x, w, sums in ((qa, 384, ((0, 0, 32), (4, 32, 96))), (kva, 512, ((8, 0, 64),))):
                    i = square_turn[0] = 1 - square_turn[0]
                    a = shaped(squares[:, i, 0:NT * w], NT, w)
                    pool.need(am, squares_free[i])
                    m = pool.did(G.tensor_tensor(a, x, x, ALU.mult))
                    dve.need(m)
                    for at, d0, d1 in sums:
                        m = squares_free[i] = dve.did(V.tensor_reduce(
                            st2[:, :, at:at + 4], a.rearrange("p t (n d) -> p t n d", n=4)[:, :, :, d0:d1], AXX, ALU.add))
                dve.need(m)
                dve.did(V.tensor_scalar(st2[:, :, 0:4], st2[:, :, 0:4], 1.0 / 32, EPS, ALU.mult, ALU.add))
                m = dve.did(V.tensor_scalar(st2[:, :, 4:12], st2[:, :, 4:12], 1.0 / 64, EPS, ALU.mult, ALU.add))
                m = inv_root(st2[:, :, 0:12], st2[:, :, 0:12], st2[:, :, 0:12], m)
                gq = R("mla_q").rearrange("p (n d) -> p n d", n=4)
                gk = R("mla_k").rearrange("p (n d) -> p n d", n=4)
                dve.need(m)
                q1 = dve.did(V.tensor_tensor(qa4[:, :, :, 0:32], qa4[:, :, :, 0:32], spread(st2[:, :, 0:4], 3, 32), ALU.mult))
                q2 = dve.did(V.tensor_tensor(qa4[:, :, :, 32:96], qa4[:, :, :, 32:96], spread(st2[:, :, 4:8], 3, 64), ALU.mult))
                k1 = dve.did(V.tensor_tensor(ka4[:, :, :, 32:96], kv4a[:, :, :, 0:64], spread(st2[:, :, 8:12], 3, 64), ALU.mult))
                ready = []
                for t in range(NT):
                    pool.need(q1, q2)
                    q3 = pool.did(G.tensor_tensor(qa4[:, t], qa4[:, t], gq, ALU.mult))
                    pool.need(k1)
                    ready.append(pool.did(G.tensor_tensor(ka4[:, t, :, 32:96], ka4[:, t, :, 32:96], gk, ALU.mult)))
                    kr = hp[:, t, C_KR:C_KR + 32].rearrange("p (n d) -> p n d", n=1)
                    e = rope(kr, kr, 1, ROT_A, ROT_C, t, turn_a, turn_b, low_rank)
                    dve.need(e)
                    dve.did(V.tensor_copy(ka4[:, t, :, 0:32], spread(hp[:, t, C_KR:C_KR + 32], 1, 4)))
                    ready.append(rope(qa4[:, t, :, 0:32], qa4[:, t, :, 0:32], 4, ROT_A, ROT_C, t, turn_a, turn_b, q3))
                later["mla"] = ready

            def turned_heads(c0, n, d, r, f0, after):
                for t in range(NT):
                    x = hp[:, t, c0:c0 + n * d].rearrange("p (n d) -> p n d", n=n)[:, :, 0:2 * r]
                    m = rope(x, x, n, r, f0, t, turn_a, turn_b, after)
                return m

            mla_normed()
            projected(2560)
            moba = squared(11, (C_MOBA, 8, 64, "moba"))
            close("right")
            S = cut(2, 4, 512)
            scope("right")

            def moba_turned():
                later["moba"] = turned_heads(C_MOBA, 8, 64, ROT_M, ROT_C + ROT_A, scaled(*moba))
                later["squares"] = squared(19, (C_DIFF, 16, 32, "diff")), squared(35, (C_MEM, 4, 64, "memq"))

            def diff_turned():
                later["diff"] = turned_heads(C_DIFF, 16, 32, ROT_D, ROT_C + ROT_A + ROT_M, scaled(*later["squares"][0]))

            def memory_scaled():
                later["mem"] = [memk_ready, scaled(*later["squares"][1])]

            QK = right(2, 8, SEQ)
            mx, den = cut(2, NT, 4), cut(2, 4, 4)
            both_d = gb.rearrange("p h t n -> p (h t n)")
            d1, d2 = [shaped(both_d[:, k * 512:(k + 1) * 512], NT, 256) for k in range(2)]

            def group(src, after, n, w, at, scale, v, v_ready, finish, out=None, **more):
                def prep(i, free):
                    act.need(free)
                    dve.need(free)
                    return heads_transposed(src, n, w, QK[:, i, :, :], [later[after] if isinstance(after, str) else after])

                def operand(i, hh, key):
                    c, p0, d = at(hh)
                    return QK[p0:p0 + d, i, c + key * n // 2, :]
                if out is not None:
                    k0 = OUT_2[out]
                    more["out"] = mixed[:, :, k0 * P:(k0 + 2) * P], out, k0
                return dict(prepare=prep if src else None, scale=scale, v=v, v_ready=v_ready, finish=finish,
                            q=lambda i, hh: operand(i, hh, 0), k=lambda i, hh: operand(i, hh, 1), **more)

            def in_pairs(hh):
                return hh // 2, hh % 2 * 64, 64

            def in_fours(pair):
                return lambda hh: ((2 * hh + pair) // 4, (2 * hh + pair) % 4 * 32, 32)

            def hp_v(c0):
                return lambda hh, s_: hp[:, s_, c0 + hh * 64:c0 + (hh + 1) * 64]

            def finish_diff(bank, rden):
                dve.need(gb_read)
                m = scaled_into(d2)(bank, rden)
                dve.need(m, lam_ready)
                m = dve.did(V.scalar_tensor_tensor(d1, d2, lm[:, 66:67], d1, ALU.mult, ALU.add))
                dve.need(m)
                m = dve.did(V.tensor_tensor(d2, d1, d1, ALU.mult))
                dve.need(m)
                m = dve.did(V.tensor_reduce(st2[:, :, 0:4], d2.rearrange("p t (n d) -> p t n d", n=4), AXX, ALU.add))
                m = roots(st2[:, :, 0:4], 1.0 / 64, m)
                dve.need(m)
                for t in range(NT):
                    m = dve.did(V.tensor_tensor(d1[:, t, :].rearrange("p (n d) -> p n d", n=4), d1[:, t, :].rearrange("p (n d) -> p n d", n=4),
                                                spread(st2[:, t, 0:4], 2, 64), ALU.mult))
                dve.need(m)
                return dve.did(V.scalar_tensor_tensor(mixed[:, :, 768:1024], d1, 1.0 - lam_init, spread(R("sub"), 1, NT),
                                                      ALU.mult, ALU.mult))

            cneg = const("causal_neg")
            groups = [
                group(lambda c, t: hp[:, t, C_FOX + c * P:C_FOX + (c + 1) * P], fox_ready, 4, P, in_pairs, 64 ** -0.5, hp_v(C_FOX + 512), pj,
                      scaled_into(mixed[:, :, 256:512]), out=0, causal=True, bias=X, bias_ready=X_ready),
                group(lambda x, t: (qa4 if x < 4 else ka4)[:, t, x % 4, :], "mla", 8, 96,
                      lambda hh: (hh, 0, 96), 96 ** -0.5,
                      lambda hh, s_: kva[:, s_, hh * P + 64:(hh + 1) * P], am, scaled_into(mixed[:, :, 0:256]), out=1, causal=True, mask=cneg),
                group(lambda c, t: hp[:, t, C_MOBA + c * P:C_MOBA + (c + 1) * P], "moba", 4, P, in_pairs, 64 ** -0.5, hp_v(C_MOBA + 512), pj,
                      scaled_into(mixed[:, :, 512:768]), out=2, work=moba_turned, causal=True, mask=cneg),
            ]
            for pair in range(2):
                groups.append(group(None if pair else lambda c, t: hp[:, t, C_DIFF + c * P:C_DIFF + (c + 1) * P],
                                    "diff", 4, P, in_fours(pair), 32 ** -0.5, hp_v(C_DIFF + 512), pj, finish_diff if pair else scaled_into(d1), out=3 if pair else None,
                                    **({} if pair else dict(work=diff_turned)),
                                    causal=True, mask=cneg))
            groups.append(group(lambda c, t: hp[:, t, C_MEM + c * P:C_MEM + (c + 1) * P] if c < 2 else
                                kvm[:, t, (c - 2) * P:(c - 1) * P], "mem", 4, P, in_pairs, 64 ** -0.5,
                                lambda hh, s_: kvm[:, s_, 256 + hh * 64:256 + (hh + 1) * 64], mk,
                                scaled_into(mixed[:, :, 1024:1280]), out=4, work=memory_scaled, causal=False))
            held, done = attention(groups, S, PTb, mx, den, Out("o_2", (right(2, SEQ, dt=F32R), right(2, SEQ, dt=F32R)), 1))
            close()
            close("right")
            close("right")
            return add_plain(held, done)

        def feed_forward_2(l, h_ready, M):
            hT = cut_pair(DC, SEQ)
            aT = cut_pair(DFF2 // P, SEQ)
            pad = cut(2, 2, SEQ + 2)
            cv = cut(3, 2, SEQ)
            g0 = COLS["ffn2"] + l * DC
            xm = feature_major(h, DC, hT, h_ready, cols[:, g0:g0 + DC])
            inv, m = rms(h, h_ready)
            factor = along_tokens_later(inv, m)
            pool.need(xm)
            zeroed = pool.did(G.memset(pad[:, :, :, 0:2], 0.0))
            pad_free, cv_free = [zeroed] * 2, [None] * 3
            cw, cb = COLS["fconv_w"] + l * 66, COLS["fconv_b"] + l * 22
            ready, gated = [], {}

            def evac_gate(c, b, done):
                i, q = (c // 2) % 3, (c // 2) % 2
                R, R_ready = factor()
                dve.need(done, pad_free[q], R_ready)
                m = dve.did(V.tensor_tensor(pad[:, q, :, 2:], psum[b][:, :].rearrange("p (k n) -> p k n", k=2), R, ALU.mult))
                banks.free(b, m)
                ends = [None, None]
                for k in range(3):
                    for j in range(2):
                        tap = cols[:, cw + k * 22 + c + j:cw + k * 22 + c + j + 1]
                        dve.need(m, cv_free[i], ends[j])
                        src = pad[:, q, j, k:k + SEQ]
                        if k == 0:
                            ends[j] = dve.did(V.tensor_scalar(cv[:, i, j, :], src, tap, cols[:, cb + c + j:cb + c + j + 1],
                                                              ALU.mult, ALU.add))
                        else:
                            ends[j] = dve.did(V.scalar_tensor_tensor(cv[:, i, j, :], src, tap, cv[:, i, j, :], ALU.mult, ALU.add))
                pad_free[q] = ends[1]
                act.need(ends)
                m = act.did(A.activation(cv[:, i, :, :], cv[:, i, :, :], ACT.Silu))
                pool.need(m, R_ready)
                gated[c] = i, pool.did(G.tensor_tensor(cv[:, i, :, :], cv[:, i, :, :], R, ALU.mult))

            def evac_up(c, b, done):
                i, m = gated[c]
                dve.need(done, m)
                m = dve.did(V.tensor_tensor(cv[:, i, :, :], cv[:, i, :, :], psum[b][:, :].rearrange("p (k n) -> p k n", k=2), ALU.mult))
                banks.free(b, m)
                act.need(m)
                hi = act.did(A.copy(aT[0][:, c:c + 2, :], cv[:, i, :, :]))
                dve.need(m, hi)
                cv_free[i] = dve.did(V.tensor_tensor(aT[1][:, c:c + 2, :], cv[:, i, :, :], aT[0][:, c:c + 2, :].bitcast(F32), ALU.subtract))
                ready.append(cv_free[i])
            for n0 in range(0, DFF2, 256):
                feature_linear(hT, "ff_gate", n0, evac_gate, xm)
                feature_linear(hT, "ff_up", n0, evac_up, xm)
            if M:
                memory_turned(1, M)
            held, done = deep_linear(aT, DFF2 // P, "down_2", ready)
            return add_plain(held, done)

        hm, M = [loaded] * NT, None
        for layer in range(2):
            rows_ready = load_rows(layer)
            if layer:
                scope()
            held, done, mix = (mixer_ab if layer == 0 else mixer_c)(hm, rows_ready)
            hm = add_normed(held, done, mix, row(layer, "post"), rows_ready)
            close()
            scope()
            hm = feed_forward_1(layer, hm, rows_ready)
            close()
            scope()
            if layer == 1:
                scope("right")
                M = memory_loaded(0)
            hm = gated_add(layer, hm, M)
            close()
        for l in range(2):
            rows_ready = load_rows(2 + l)
            scope()
            hm = mixer_2(l, hm, rows_ready, M)
            close()
            scope()
            M = None
            if l == 0:
                scope("right")
                M = memory_loaded(1)
            hm = feed_forward_2(l, hm, M)
            close()
        sp.need(dve.last())
        sp.engine.dma_start(out[0].rearrange("(t p) d -> p t d", p=P), h[:, :, :]).then_inc(s_out, 16)
        sp.engine.wait_ge(s_out, 16)


WEIGHTS = ["x", "p", "w_in_ab", "w_out_ab", "w_qkv_c", "w_o_c", "w_up", "w_down", "w_ple", "w_ple_gate", "mem_2",
           "w_in_2", "mla_w_uq_2", "mla_w_ukv_2", "mem_w_kv_2", "w_o_2", "ffn_w_gate_2", "ffn_w_up_2", "ffn_w_down_2"]


def columns(v):
    return np.ascontiguousarray(v.reshape(-1, P).T)


def kernel(**inputs):
    import concourse.bacc as bacc
    from concourse.bass_utils import run_bass_kernel_spmd

    inputs = {k: np.asarray(v) for k, v in inputs.items()}
    f = np.float32
    cols = [columns(inputs["norm_gains"][layer, which]) for layer in range(2) for which in (0, 2)]
    cols += [columns(inputs[name][l]) for name in ("attn_norm_2", "ffn_norm_2", "mem_norm_2") for l in range(2)]
    cols.append(inputs["conv_a"][0].reshape(4, 12, P).transpose(2, 1, 0).reshape(P, 48))
    cols += [inputs["ffn_conv_w_2"][l].reshape(3, 22, P).transpose(2, 0, 1).reshape(P, 66) for l in range(2)]
    cols += [columns(inputs["ffn_conv_b_2"][l]) for l in range(2)]
    zeros4 = np.zeros(4, f)
    rows = np.zeros((4, ROW_MAX), f)

    def put(layer, name, *values):
        a, n = ROWS[layer][name]
        rows[layer, a:a + n] = np.concatenate([v.reshape(-1) for v in values])

    for layer in range(2):
        put(layer, "post", inputs["norm_gains"][layer, 1])
        put(layer, "post_ff", inputs["norm_gains"][layer, 3])
    put(0, "norm_a", *[inputs["norm_a"][0]] * 4)
    put(0, "norm_b", inputs["norm_b"][0])
    put(0, "gate_bias", zeros4, inputs["dt_bias"][0], inputs["i_bias_b"][0], inputs["f_bias_b"][0])
    put(0, "a_log", inputs["a_log"][0])
    put(1, "b_qkv", inputs["b_qkv_c"][0])
    put(1, "b_o", inputs["b_o_c"][0])
    put(1, "sinks", inputs["sinks_c"][0])
    for l in range(2):
        i = {k: inputs[k + "_2"][l] for k in ("mla_cq_norm", "mla_ckv_norm", "mla_q_norm", "mla_k_norm", "fox_q_norm",
                                              "fox_k_norm", "moba_q_norm", "moba_k_norm", "diff_q_norm", "diff_k_norm",
                                              "diff_sub_norm", "mem_q_norm", "mem_k_norm", "fox_b_f", "diff_lambda")}
        put(2 + l, "cq", i["mla_cq_norm"])
        put(2 + l, "ckv", i["mla_ckv_norm"])
        put(2 + l, "kr", i["mla_k_norm"][:32])
        put(2 + l, "fox", *[i["fox_q_norm"]] * 4, *[i["fox_k_norm"]] * 4)
        put(2 + l, "moba", *[i["moba_q_norm"]] * 4, *[i["moba_k_norm"]] * 4)
        put(2 + l, "diff", *[i["diff_q_norm"]] * 8, *[i["diff_k_norm"]] * 8)
        put(2 + l, "memq", *[i["mem_q_norm"]] * 4)
        put(2 + l, "memk", *[i["mem_k_norm"]] * 4)
        put(2 + l, "mla_q", *[i["mla_q_norm"]] * 4)
        put(2 + l, "mla_k", *[i["mla_k_norm"][32:]] * 4)
        put(2 + l, "sub", *[i["diff_sub_norm"]] * 4)
        put(2 + l, "fox_b", i["fox_b_f"])
        put(2 + l, "lambda", i["diff_lambda"])
    arrays = {name: np.ascontiguousarray(inputs[name]) for name in WEIGHTS}
    arrays["cols"] = np.ascontiguousarray(np.concatenate(cols, 1))
    arrays["rows"] = rows
    arrays["consts"] = constants()
    arrays["positions"] = np.ascontiguousarray(np.concatenate(
        [inputs[n].reshape(NT, P).T for n in ("positions", "positions_2")], 1))

    nc = bacc.Bacc("TRN2", target_bir_lowering=False, num_devices=1)
    arrays = {f"in_{k}": v for k, v in arrays.items()}
    T = {k[3:]: nc.dram_tensor(k, v.shape, bass.mybir.dt.from_np(v.dtype), kind="ExternalInput").ap() for k, v in arrays.items()}
    out = nc.dram_tensor("out_0_dram", (1, SEQ, D), F32, kind="ExternalOutput").ap()
    program(nc, T, out)
    result = run_bass_kernel_spmd(nc, [arrays], core_ids=[0])
    return result.results[0]["out_0_dram"]
```
